# Optimizing a Trainium2 kernel written in Bass

```python
import math
import jax, jax.numpy as jnp
from jax import lax
import numpy as np

D_MODEL = 1024
BATCH = 1
SEQ = 256
DEPTH = 1

CHUNK = 64
Q_BLOCK = 2 * CHUNK
SB_HEADS = 8
SB_HEAD_DIM = 64
SB_WIDTH = SB_HEADS * SB_HEAD_DIM
SSM_GROUP = 16
SSM_WIDTH = 512
SSM_GROUPS = SSM_WIDTH // SSM_GROUP
SSM_STATE = 64
PLE_DIM = 256
N_EXPERTS = 32
TOP_K = 4
D_FF = D_MODEL
SWIGLU_LIMIT = 7.0
SWIGLU_ALPHA = 1.702
MOE_BLOCK = 256
EPS = 1e-6
IN_COLS = 3 * SB_WIDTH + SSM_WIDTH + 2 * D_MODEL

kernel_name = "hybrid_stickbreak_s5_moe_ple"

def rmsnorm(x, g):
    xf = x.astype(jnp.float32)
    y = xf * lax.rsqrt(jnp.mean(xf * xf, axis=-1, keepdims=True) + EPS)
    return (y * g.astype(jnp.float32)).astype(x.dtype)

def stick_breaking_attention(q, k, v):
    s_len, dh = q.shape[2], q.shape[3]
    scale = dh ** -0.5
    outs = []
    for start in range(0, s_len, Q_BLOCK):
        end = start + Q_BLOCK
        qb = q[:, :, start:end].astype(jnp.float32)
        kb = k[:, :, :end].astype(jnp.float32)
        vb = v[:, :, :end].astype(jnp.float32)
        z = jnp.einsum('bhtd,bhsd->bhts', qb, kb) * scale
        t_idx = start + jnp.arange(Q_BLOCK)
        s_idx = jnp.arange(end)
        mask = s_idx[None, :] < t_idx[:, None]
        log_keep = jnp.where(mask, jax.nn.log_sigmoid(-z), 0.0)
        later = lax.cumsum(log_keep, axis=3, reverse=True) - log_keep
        w = jnp.where(mask, jnp.exp(jax.nn.log_sigmoid(z) + later), 0.0)
        outs.append(jnp.einsum('bhts,bhsd->bhtd', w, vb))
    return jnp.concatenate(outs, axis=2).astype(q.dtype)

def s5_ssm(u, a_re, a_im, log_dt, b_re, b_im, c_re, c_im, d_skip):
    f32 = jnp.float32
    bsz, s_len, _ = u.shape
    uf = u.astype(f32)
    ug = uf.reshape(bsz, s_len, SSM_GROUPS, SSM_GROUP)
    lr = a_re.astype(f32)
    li = a_im.astype(f32)
    dt = jnp.exp(log_dt.astype(f32))[:, None]
    mag = jnp.exp(lr * dt)
    abar_r = mag * jnp.cos(li * dt)
    abar_i = mag * jnp.sin(li * dt)
    den = lr * lr + li * li
    nr = abar_r - 1.0
    ni = abar_i
    fr = (nr * lr + ni * li) / den
    fi = (ni * lr - nr * li) / den
    br = b_re.astype(f32)
    bi = b_im.astype(f32)
    bbar_r = fr[..., None] * br - fi[..., None] * bi
    bbar_i = fr[..., None] * bi + fi[..., None] * br
    xr = jnp.einsum('bsgc,gpc->sbgp', ug, bbar_r)
    xi = jnp.einsum('bsgc,gpc->sbgp', ug, bbar_i)
    ar = jnp.broadcast_to(abar_r[None, None], (s_len, 1, SSM_GROUPS, SSM_STATE))
    ai = jnp.broadcast_to(abar_i[None, None], (s_len, 1, SSM_GROUPS, SSM_STATE))

    def combine(e1, e2):
        a1r, a1i, b1r, b1i = e1
        a2r, a2i, b2r, b2i = e2
        return (a2r * a1r - a2i * a1i,
                a2r * a1i + a2i * a1r,
                a2r * b1r - a2i * b1i + b2r,
                a2r * b1i + a2i * b1r + b2i)

    _, _, hr, hi = lax.associative_scan(combine, (ar, ai, xr, xi), axis=0)
    y = (jnp.einsum('sbgp,gcp->bsgc', hr, c_re.astype(f32))
         - jnp.einsum('sbgp,gcp->bsgc', hi, c_im.astype(f32)))
    y = y.reshape(bsz, s_len, SSM_WIDTH) + d_skip.astype(f32) * uf
    return y.astype(u.dtype)

def moe_swiglu(h, w_router, b_router, w_up, b_up, w_down, b_down):
    f32 = jnp.float32
    bsz, s_len, d = h.shape
    n = bsz * s_len
    nk = n * TOP_K
    hf = h.reshape(n, d)
    logits = hf.astype(f32) @ w_router.astype(f32) + b_router.astype(f32)
    top_val, top_idx = lax.top_k(logits, TOP_K)
    gate = jax.nn.softmax(top_val, axis=-1)
    expert = top_idx.reshape(-1)
    weight = gate.reshape(-1)
    token = jnp.arange(nk, dtype=jnp.int32) // TOP_K
    order = jnp.argsort(expert, stable=True)
    e_sorted = expert[order]
    counts = jnp.bincount(expert, length=N_EXPERTS)
    padded = (counts + MOE_BLOCK - 1) // MOE_BLOCK * MOE_BLOCK
    start = jnp.cumsum(counts) - counts
    pad_end = jnp.cumsum(padded)
    pad_start = pad_end - padded
    dst = pad_start[e_sorted] + jnp.arange(nk) - start[e_sorted]
    n_blocks = -(-nk // MOE_BLOCK) + N_EXPERTS
    rows = n_blocks * MOE_BLOCK
    row_token = jnp.zeros((rows,), jnp.int32).at[dst].set(token[order])
    row_weight = jnp.zeros((rows,), f32).at[dst].set(weight[order])
    block_expert = jnp.minimum(
        jnp.searchsorted(pad_end, jnp.arange(n_blocks) * MOE_BLOCK, side='right'),
        N_EXPERTS - 1)
    xs = hf[row_token].reshape(n_blocks, MOE_BLOCK, d)

    def expert_block(args):
        xb, e = args
        gu = xb.astype(f32) @ w_up[e].astype(f32) + b_up[e].astype(f32)
        g = jnp.minimum(gu[:, :D_FF], SWIGLU_LIMIT)
        up = jnp.clip(gu[:, D_FF:], -SWIGLU_LIMIT, SWIGLU_LIMIT)
        act = (up + 1.0) * g * jax.nn.sigmoid(SWIGLU_ALPHA * g)
        return act @ w_down[e].astype(f32) + b_down[e].astype(f32)

    ys = lax.map(expert_block, (xs, block_expert)).reshape(rows, d)
    out = jax.ops.segment_sum(ys * row_weight[:, None], row_token, num_segments=n)
    return out.reshape(bsz, s_len, d).astype(h.dtype)

def setup_inputs(seed: int = 0) -> dict:
    key = jax.random.key(seed)
    ks = iter(jax.random.split(key, 40))
    f32 = jnp.float32
    L = DEPTH

    def nrm(shape, scale):
        return jax.random.normal(next(ks), shape, f32) * scale

    def gain(shape):
        return 1.0 + 0.05 * jax.random.normal(next(ks), shape, f32)

    n_idx = jnp.arange(SSM_STATE, dtype=f32)
    return {
        "x": nrm((BATCH, SEQ, D_MODEL), 1.0),
        "p": nrm((DEPTH, BATCH, SEQ, PLE_DIM), 1.0),
        "g_mix": gain((L, D_MODEL)),
        "w_in": nrm((L, D_MODEL, IN_COLS), D_MODEL ** -0.5),
        "g_q": gain((L, SB_HEAD_DIM)),
        "g_k": gain((L, SB_HEAD_DIM)),
        "w_attn_branch": nrm((L, SB_WIDTH, D_MODEL), SB_WIDTH ** -0.5),
        "a_re": -0.5 + nrm((L, SSM_GROUPS, SSM_STATE), 0.01),
        "a_im": math.pi * n_idx + nrm((L, SSM_GROUPS, SSM_STATE), 0.01),
        "log_dt": jax.random.uniform(next(ks), (L, SSM_GROUPS), f32,
                                     math.log(1e-3), math.log(1e-1)),
        "b_re": nrm((L, SSM_GROUPS, SSM_STATE, SSM_GROUP), (2 * SSM_GROUP) ** -0.5),
        "b_im": nrm((L, SSM_GROUPS, SSM_STATE, SSM_GROUP), (2 * SSM_GROUP) ** -0.5),
        "c_re": nrm((L, SSM_GROUPS, SSM_GROUP, SSM_STATE), (2 * SSM_STATE) ** -0.5),
        "c_im": nrm((L, SSM_GROUPS, SSM_GROUP, SSM_STATE), (2 * SSM_STATE) ** -0.5),
        "d_skip": gain((L, SSM_WIDTH)),
        "w_glu": nrm((L, SSM_WIDTH, 2 * D_MODEL), SSM_WIDTH ** -0.5),
        "b_glu": nrm((L, 2 * D_MODEL), 0.01),
        "w_out": nrm((L, D_MODEL, D_MODEL), D_MODEL ** -0.5),
        "g_ffn": gain((L, D_MODEL)),
        "w_router": nrm((L, D_MODEL, N_EXPERTS), D_MODEL ** -0.5),
        "b_router": nrm((L, N_EXPERTS), 0.01),
        "w_up": nrm((L, N_EXPERTS, D_MODEL, 2 * D_FF), D_MODEL ** -0.5),
        "b_up": nrm((L, N_EXPERTS, 2 * D_FF), 0.01),
        "w_down": nrm((L, N_EXPERTS, D_FF, D_MODEL), D_FF ** -0.5),
        "b_down": nrm((L, N_EXPERTS, D_MODEL), 0.01),
        "g_ple_gate": gain((L, D_MODEL)),
        "w_ple_gate": nrm((L, D_MODEL, D_MODEL), D_MODEL ** -0.5),
        "w_ple_proj": nrm((L, PLE_DIM, D_MODEL), PLE_DIM ** -0.5),
        "g_ple_post": gain((L, D_MODEL)),
    }

def reference(x, p, g_mix, w_in, g_q, g_k, w_attn_branch, a_re, a_im, log_dt,
              b_re, b_im, c_re, c_im, d_skip, w_glu, b_glu, w_out, g_ffn,
              w_router, b_router, w_up, b_up, w_down, b_down,
              g_ple_gate, w_ple_gate, w_ple_proj, g_ple_post):
    bsz, s_len, d = x.shape
    splits = [SB_WIDTH, 2 * SB_WIDTH, 3 * SB_WIDTH,
              3 * SB_WIDTH + SSM_WIDTH, 3 * SB_WIDTH + SSM_WIDTH + D_MODEL]

    def heads(t):
        return t.reshape(bsz, s_len, SB_HEADS, SB_HEAD_DIM).transpose(0, 2, 1, 3)

    for i in range(DEPTH):
        h = rmsnorm(x, g_mix[i])
        proj = h @ w_in[i]
        q, k, v, u, gate_a, gate_s = jnp.split(proj, splits, axis=-1)
        qh = rmsnorm(heads(q), g_q[i])
        kh = rmsnorm(heads(k), g_k[i])
        o = stick_breaking_attention(qh, kh, heads(v))
        o = o.transpose(0, 2, 1, 3).reshape(bsz, s_len, SB_WIDTH)
        attn_branch = o @ w_attn_branch[i]

        y = s5_ssm(u, a_re[i], a_im[i], log_dt[i], b_re[i], b_im[i],
                   c_re[i], c_im[i], d_skip[i])
        zg = jax.nn.gelu(y) @ w_glu[i] + b_glu[i]
        ssm_branch = zg[..., :D_MODEL] * jax.nn.sigmoid(zg[..., D_MODEL:])

        mixed = jax.nn.sigmoid(gate_a) * attn_branch + jax.nn.sigmoid(gate_s) * ssm_branch
        x = x + mixed @ w_out[i]

        x = x + moe_swiglu(rmsnorm(x, g_ffn[i]), w_router[i], b_router[i],
                           w_up[i], b_up[i], w_down[i], b_down[i])

        ple_gate = jax.nn.sigmoid(rmsnorm(x, g_ple_gate[i]) @ w_ple_gate[i])
        ple = rmsnorm(p[i] @ w_ple_proj[i], g_ple_post[i])
        x = x + ple_gate * ple
    return x


_drawn_inputs = setup_inputs


def setup_inputs(seed=0):
    import zlib

    import numpy as np

    out = dict(_drawn_inputs(seed))
    spreads = {}
    factors = {'g_q': 2.717,
     'g_k': 3.195,
     'a_re': 8.0,
     'b_re': 3.043,
     'b_im': 3.704,
     'b_glu': 5.382,
     'b_up': 8.0,
     'b_down': 8.0,
     'g_ple_gate': 6.874}
    for name, (base, spread) in spreads.items():
        noise = np.random.default_rng([zlib.crc32(name.encode()), seed]).standard_normal(out[name].shape)
        drawn = base * np.exp(spread * noise) if base else spread * noise
        out[name] = __import__('jax').numpy.asarray(drawn.astype(out[name].dtype))
    for name, factor in factors.items():
        out[name] = (out[name] * factor).astype(out[name].dtype)
    return out
```

```python
from contextlib import ExitStack

import concourse.bass as bass
from concourse import mybir

P = 128
HALF = P // 2
BANK = 512
NBANKS = 8
F32 = mybir.dt.float32
BF16 = mybir.dt.bfloat16
I32 = mybir.dt.int32
ALU = mybir.AluOpType
ACT = mybir.ActivationFunctionType
AX = mybir.AxisListType.X

EPS = 1e-6
LIMIT = 7.0
ALPHA = 1.702
HIDDEN = -1e30
NEVER = -3e38
TAKEN = 3e38
TWO_PI = 6.283185307179586
TWO_PI_HI, TWO_PI_MID = 6.28125, 0.0019340515136718750
TWO_PI_LO = TWO_PI - TWO_PI_HI - TWO_PI_MID
ROUNDER = 12582912.0
PI_F32 = 3.1415925
SQUARINGS = 8
TAYLOR = 7
CAP = 64


class Steps:

    def __init__(self, eng, sem):
        self.eng, self.sem, self.n, self.shift = eng, sem, 0, 0

    def did(self, ins):
        self.n += 1
        return ins.then_inc(self.sem, 1)

    def settle(self):
        self.eng.wait_ge(self.sem, self.n + self.shift)

    def link(self, ins):
        self.did(ins)
        self.settle()
        return ins


def order_of_banks():
    jobs = ["par"] + [f"ht{i}" for i in range(4)] + ["u0", "u1", "q0", "q1", "k0", "k1", "v0", "v1"]
    jobs += ["bt0", "bt1", "ct0", "ct1", "qt0", "qt1", "kt0", "kt1"]
    for s in range(4 + 2):
        if s < 4:
            jobs += [f"z{2 * s}", f"z{2 * s + 1}"]
        if s >= 2:
            jobs += [f"o{s - 2}"]
    jobs += [f"x{i}" for i in range(4)]
    for b in range(4):
        jobs += [f"g{2 * b}", f"g{2 * b + 1}"]
        jobs += [f"x{4 * b + 4 + i}" for i in range(4)] if b < 3 else [f"a{i}" for i in range(4)]
        jobs += [f"y{b}"]
    jobs += [f"glu{i}" for i in range(8)] + [f"out{i}" for i in range(4)]
    jobs += [f"xt{i}" for i in range(4)] + ["lg", "rk", "gt"] + [f"bd{i}" for i in range(4)]
    return {name: (i % NBANKS, i // NBANKS) for i, name in enumerate(jobs)}


def hybrid_layer(nc, x, p, g_mix, w_in, g_q, g_k, w_attn, a_re, a_im, log_dt, b_re, b_im, c_re, c_im, d_skip,
                 w_glu, b_glu, w_out, g_ffn, w_router, b_router, w_up, b_up, w_down, b_down,
                 g_ple_gate, w_ple_gate, w_ple_proj, g_ple_post, out):
    _, SEQ, D = x.shape
    PLE = p.shape[3]
    G, N = a_re.shape[1:]
    GC = b_re.shape[3]
    W = G * GC
    E = w_router.shape[2]
    F = w_down.shape[2]
    DH = g_q.shape[1]
    H = w_attn.shape[1] // DH
    TB = SEQ // P
    DT = D // P
    WT = W // P
    PAIRS = H // 2
    TILES = G * N // P
    assert (TB, DT, WT, PAIRS, TILES, E, F, PLE) == (2, 8, 4, 4, 16, 32, D, 2 * P)
    BANKS = order_of_banks()

    with ExitStack() as ctx:
        def sem(name):
            return ctx.enter_context(nc.semaphore(name))

        def sb(name, cols, dt=F32):
            return ctx.enter_context(nc.sbuf_tensor(name, [P, cols], dt))

        PLACES, PLACE = 6, 4096
        ring = sb("ring", PLACES * PLACE)
        arena = sb("arena", 27136)
        ident = sb("ident", P)
        neg_tri = sb("neg_tri", P)
        neg_ones = sb("neg_ones", P)
        small = sb("small", 680)
        ident_b = sb("ident_b", P, BF16)
        hide_b = sb("hide_b", P, BF16)
        flag = sb("flag", 1, I32)
        bank = [ctx.enter_context(nc.psum_tensor(f"bank{i}", [P, BANK], F32)) for i in range(NBANKS)]

        def area(at, *dims):
            n = 1
            for d in dims:
                n *= d
            ap = arena[:, at:at + n]
            if len(dims) == 2:
                return ap.rearrange("p (a b) -> p a b", a=dims[0])
            if len(dims) == 3:
                return ap.rearrange("p (a b c) -> p a b c", a=dims[0], b=dims[1])
            return ap

        def spread(ap, n):
            return ap.unsqueeze(2).broadcast_to([ap.shape[0], ap.shape[1], n])

        A_X, A_HT, A_Q, A_K, A_QT, A_KT, A_V, A_UT, A_OT, A_GY, A_TC, A_GATE, A_BT, A_CT = (
            0, 2048, 4096, 5120, 6144, 7168, 8192, 9216, 10240, 11264, 12288, 20480, 24576, 25600)
        X = area(A_X, TB, D)
        HT = area(A_HT, DT, SEQ)
        Q = area(A_Q, TB, 512)
        K = area(A_K, TB, 512)
        QT = area(A_QT, PAIRS, SEQ)
        KT = area(A_KT, PAIRS, SEQ)
        V = area(A_V, TB, 512)
        UT = area(A_UT, WT, SEQ)
        OT = area(A_OT, PAIRS, SEQ)
        GY = area(A_GY, WT, SEQ)
        COS = area(A_TC, TILES, SEQ)
        SIN = area(A_TC + 4096, TILES, SEQ)
        GATE = area(A_GATE, 2 * DT, SEQ)
        BT = area(A_BT, 2, WT, P)
        CT = area(A_CT, 3, WT, P)
        SQ = area(A_GY, 512)
        SOFT = area(A_Q, 4, 384)
        PROB = area(A_GY, 2, 384)
        ROT = area(A_X, 2, 2, 512)
        BACK = area(A_Q, 4, 2, 512)
        TMP = area(A_TC, 2, 4096)
        B_RAW = area(A_GATE, 2, TILES, 2 * GC)
        B_BAR = area(A_GATE + 1024, 2, TILES, 2 * GC)
        C_RAW = area(A_GATE + 2048, 2, WT, N)
        C_MASK = area(A_GATE + 2560, 2, WT, P)
        S5 = area(A_GATE + 3584, 32, TILES)
        PR = area(A_OT, P)
        LDT = area(A_OT + 128, 2)
        SZ = area(A_X, 4, SEQ)
        X2 = area(A_HT, TB, D)
        XN = area(A_Q, TB, D)
        H2T = area(A_QT, DT, SEQ)
        XB = arena[:, A_GATE:A_GATE + 3072].bitcast(BF16).rearrange("p (s t d) -> p s t d", s=3, t=TB)
        REST = area(A_V, TB, D)
        WPG = area(A_TC, DT, D)
        WPP = area(A_X, PLE // P, D)
        XS = area(A_QT, DT, CAP)
        ACTT = area(A_QT + 512, WT, P)
        Y = area(A_QT + 1024, 512)
        WSEL = area(A_QT + 1536, TB, P)
        WSELT = area(A_QT + 1792, TB, P)
        BUP = area(A_V, 2 * F)
        ACTS = area(A_V + 2048, 3, 512)
        PIN = area(A_V + 3584, TB, PLE)
        PLEV = area(A_Q, TB, D)
        GPOST = area(A_BT, D)
        PT_IN = area(A_BT + 1024, PLE // P, SEQ)
        BDOWN = area(A_BT + 1536, D)
        XT3 = area(A_QT, DT, SEQ)
        GSIG = area(A_V, TB, D)
        R0 = A_GATE + 3072
        SLOT = arena[:, R0:R0 + SEQ]
        SLOT_I = area(A_V + 2560, SEQ).bitcast(I32)
        LOGIT = area(R0 + 256, TB, E + 8)
        LEFT = area(R0 + 336, TB, E + 8)
        CHOSEN = area(R0 + 416, TB, E)
        GATES = area(R0 + 480, TB, E)
        RANK = area(R0 + 544, TB, E + 1)
        WR = area(R0 + 612, DT, E)
        GT = area(A_V + 2048, TB, P)
        XN3 = area(A_GATE, TB, D)
        SELB = arena[:, R0 + 868:R0 + 868 + CAP].bitcast(BF16).rearrange("p (t c) -> p t c", t=TB)
        PICK = arena[:, R0 + 932:R0 + 932 + CAP]
        NPAR = 94
        PAR = small[:, 0:NPAR]
        P_ARE, P_AIM, P_LDT, P_GMIX, P_GFFN, P_GPLE, P_DSKIP, P_BGLU, P_GQ, P_GK = 0, 16, 32, 48, 56, 64, 72, 76, 92, 93
        RHO = small[:, 96:112]
        SSQ = small[:, 112:120]
        RSTD = small[:, 120:128]
        HSQ = small[:, 128:160]
        PARITY = small[:, 160:162]
        TOP8 = small[:, 162:178]
        NTOP = small[:, 178:180]
        SUM = small[:, 180:184]
        CNT = small[:, 184:186]
        BROUT = small[:, 186:218]
        AKC = small[:, 218:234]
        AKS = small[:, 234:250]
        AKT = small[:, 250:282]
        ODD = small[:, 282:283]
        PSQ = small[:, 284:286]
        PRT = small[:, 286:288]
        TRI = small[:, 320:448]
        ONES = small[:, 448:576]

        full = [sem(f"full{i}") for i in range(NBANKS)]
        free = [sem(f"free{i}") for i in range(NBANKS)]
        arrived = [sem(f"arrived{i}") for i in range(PLACES)]
        names = ("x_in params_in dt_in bc_in ident_set odd_set b_zero x_sq x_ms x_root x_normal dt_rows angle_set "
                 "sine_set bbar_set tables_set head_sq head_ms head_ms_all head_root heads_set abs_set soft_set "
                 "sp_set cum_full rot_set back_set gelu_set sz_set mixed_set x_again x2_sq x2_ms x2_root "
                 "x2_normal router_in slots_set logit_top exp_set chosen_set flag_set gates_ready down_bias_in "
                 "split_set up_bias_in ple_in pt_full pt_set pp_full pp_set pp_sq pp_ms pp_root x3_set x3_sq "
                 "x3_ms x3_root x3_normal xt3_full xt3_set pg_full pg_sig fin_set stored dve_step act_step "
                 "pool_step").split()
        S = {n: sem(n) for n in names}
        moe_names = ("sel_set wsel_set pick_set wt_full wt_set gx_full xs_set up_g up_u g_set sig_set act_set at_full "
                     "at_set y_full y_set sc_full sc_add dve_step").split()
        M = {n: sem("e_" + n) for n in moe_names}

        W_ORDER = [("in", i) for i in (3, 0, 1, 2, 4, 5, 6, 7)] + [("attn", 0)] + [("glu", 0), ("glu", 1)] + [("out", 0), ("out", 1)]
        TURN = {k: (i % PLACES, i // PLACES) for i, k in enumerate(W_ORDER)}
        FIRST = len(W_ORDER)
        PER_EXPERT = 6
        EXP_PLACE = [(FIRST + c) % PLACES for c in range(PER_EXPERT)]
        EXP_USES = [(FIRST + c) // PLACES for c in range(PER_EXPERT)]
        LAST_READ = {("in", 3): "u1", ("in", 0): "q1", ("in", 1): "k1", ("in", 2): "v1", ("attn", 0): "a3",
                     ("glu", 0): "glu7", ("glu", 1): "glu7", ("out", 0): "out1", ("out", 1): "out3"}
        LAST_READ.update({("in", 4 + i): f"g{2 * i + 1}" for i in range(4)})
        READ = {c: sem(f"read{c}") for c in (0, 1, 2, 4)}

        def place(i):
            return ring[:, i * PLACE:(i + 1) * PLACE]

        def weight(key, a):
            return place(TURN[key][0]).rearrange("p (a n) -> p a n", a=a)

        def up_source(e, c):
            return w_up[0, e, 2 * P * c:2 * P * (c + 1), :].rearrange("(k p) n -> p k n", p=P)

        def down_source(e, c):
            return w_down[0, e, 4 * P * c:4 * P * (c + 1), :].rearrange("(k p) n -> p k n", p=P)

        def expert_source(e, c):
            if isinstance(e, int):
                return up_source(e, c) if c < 4 else down_source(e, c - 4)
            if c < 4:
                return w_up[0, bass.ds(e, 1), 2 * P * c:2 * P * (c + 1), :].rearrange("o (k p) n -> p (o k) n", p=P)
            c -= 4
            return w_down[0, bass.ds(e, 1), 4 * P * c:4 * P * (c + 1), :].rearrange("o (k p) n -> p (o k) n", p=P)

        PASSES = TB * P // CAP - 1

        def wait_full(eng, job):
            eng.wait_ge(full[BANKS[job][0]], BANKS[job][1] + 1)

        def release(ins, job):
            return ins.then_inc(free[BANKS[job][0]], 1)

        def released(eng, job):
            eng.wait_ge(free[BANKS[job][0]], BANKS[job][1] + 1)

        def ps(job):
            return bank[BANKS[job][0]]

        def pairs(ap, a=2):
            return ap.rearrange("p (a n) -> p a n", a=a)

        GX, UG, UU, WTB, ATB, YB = 0, 1, 2, 3, 4, 5
        SCATTER = (6, 7, WTB, ATB)

        block = ctx.enter_context(nc.Block())

        @block.sync
        def _(sp):
            sp.dma_start(X[:, 0, :], x[0, 0:P, :]).then_inc(S["x_in"], 16)
            sp.dma_start(X[:, 1, :], x[0, P:SEQ, :]).then_inc(S["x_in"], 16)

            def source(key):
                name, i = key
                if name == "in":
                    return w_in[0, :, 512 * i:512 * (i + 1)].rearrange("(k p) n -> p k n", p=P)
                if name == "attn":
                    return w_attn[0].rearrange("(k p) n -> p k n", p=P)
                if name == "glu":
                    return w_glu[0, 2 * P * i:2 * P * (i + 1), :].rearrange("(k p) n -> p k n", p=P)
                return w_out[0, :, 512 * i:512 * (i + 1)].rearrange("(k p) n -> p k n", p=P)

            def load(at, src):
                sp.dma_start(place(at).rearrange("p (a n) -> p a n", a=src.shape[1]), src).then_inc(arrived[at], 16)

            held = {}
            for key in W_ORDER:
                at = TURN[key][0]
                if at in held:
                    wait_full(sp, held[at])
                load(at, source(key))
                held[at] = LAST_READ[key]
            for c in range(PER_EXPERT):
                wait_full(sp, held[EXP_PLACE[c]])
                load(EXP_PLACE[c], expert_source(0, c))

            def load_expert(n, e):
                for c in range(PER_EXPERT):
                    sp.wait_ge(READ[c] if c in READ else M["up_u" if c == 3 else "y_full"], n)
                    load(EXP_PLACE[c], expert_source(e, c))

            with sp.Fori(1, E) as e:
                load_expert(e, e)
            sp.wait_ge(S["flag_set"], 1)
            crowd = sp.value_load(flag[0:1, 0:1], min_val=0, max_val=SEQ)
            with sp.If(crowd > CAP):
                with sp.Fori(0, E) as e:
                    with sp.Fori(0, PASSES) as j:
                        n = E + e * PASSES + j
                        load_expert(n, e)
            for i in range(2 * TB):
                t, c = divmod(i, 2)
                sp.wait_ge(S["fin_set"], i + 1)
                sp.dma_start(out[0, t * P:(t + 1) * P, 512 * c:512 * (c + 1)],
                             X2[:, t, 512 * c:512 * (c + 1)]).then_inc(S["stored"], 16)
            sp.wait_ge(S["stored"], 32 * TB)

        @block.gpsimd
        def _(pool):
            st = Steps(pool, S["pool_step"])
            for m, v in ((ident[:, :], 0.0), (neg_ones[:, :], -1.0), (neg_tri[:, :], -1.0), (TRI, 1.0), (ONES, 1.0),
                         (hide_b[:, :], 0.0), (ident_b[:, :], 0.0)):
                st.did(pool.memset(m, v))
            st.settle()
            for m in (ident, ident_b):
                st.did(pool.affine_select(out=m[:, :], in_=m[:, :], compare_op=ALU.not_equal, fill=1.0, base=0,
                                          pattern=[[-1, P]], channel_multiplier=1))
            st.did(pool.affine_select(out=neg_tri[:, :], in_=neg_tri[:, :], compare_op=ALU.is_ge, fill=0.0, base=0,
                                      pattern=[[-1, P]], channel_multiplier=1))
            st.did(pool.affine_select(out=TRI, in_=TRI, compare_op=ALU.is_gt, fill=0.0, base=0,
                                      pattern=[[1, P]], channel_multiplier=-1))
            st.did(pool.affine_select(out=hide_b[:, :], in_=hide_b[:, :], compare_op=ALU.is_gt, fill=HIDDEN, base=0,
                                      pattern=[[1, P]], channel_multiplier=-1))
            st.settle()
            pool.sem_inc(S["ident_set"], 1)
            pool.iota(ODD.bitcast(I32), [[0, 1]], base=0, channel_multiplier=1).then_inc(S["odd_set"], 1)
            pool.memset(arena[:, A_GATE:A_GATE + 2 * TILES * 2 * GC], 0.0).then_inc(S["b_zero"], 1)

            released(pool, "o3")
            for i in range(TILES):
                b, j = divmod(i, 4)
                pool.wait_ge(S["rot_set"], i + 1)
                if b and j == 0:
                    wait_full(pool, f"y{b - 1}")
                for s, table in enumerate((COS, SIN)):
                    pool.tensor_tensor(pairs(BACK[:, j, s, :]), pairs(ROT[:, i % 2, 1, :]),
                                       table[:, i:i + 1, :].broadcast_to([P, 2, SEQ]), ALU.mult).then_inc(S["back_set"], 1)
            wait_full(pool, "g7")
            for t in range(TB):
                pool.dma_start(X2[:, t, :], x[0, t * P:(t + 1) * P, :]).then_inc(S["x_again"], 16)
            pool.wait_ge(S["mixed_set"], DT)
            pool.iota(SLOT_I, [[1, SEQ]], base=0, channel_multiplier=0).then_inc(S["slots_set"], 1)

        @block.scalar
        def _(act):
            st = Steps(act, S["act_step"])
            rows = [(P_ARE, a_re[0].rearrange("(t q) n -> t (q n)", q=2), TILES),
                    (P_AIM, a_im[0].rearrange("(t q) n -> t (q n)", q=2), TILES),
                    (P_GMIX, g_mix[0].rearrange("(k p) -> k p", p=P), DT),
                    (P_GFFN, g_ffn[0].rearrange("(k p) -> k p", p=P), DT),
                    (P_GPLE, g_ple_gate[0].rearrange("(k p) -> k p", p=P), DT),
                    (P_DSKIP, d_skip[0].rearrange("(k p) -> k p", p=P), WT),
                    (P_BGLU, b_glu[0].rearrange("(k p) -> k p", p=P), 2 * DT)]
            rows += [(at, g, 1) for at, g in ((P_GQ, g_q), (P_GK, g_k))]
            act.dma_start(LDT[32:48, :], log_dt[0].rearrange("(t q) -> t q", q=2)).then_inc(S["dt_in"], 16)
            for at, src, n in rows:
                if src.shape[-1] == P:
                    act.dma_start(PR[at:at + n, :], src).then_inc(S["params_in"], 16)
                else:
                    for h in range(2):
                        act.dma_start(PR[at:at + 1, h * DH:(h + 1) * DH], src).then_inc(S["params_in"], 16)
            act.wait_ge(S["b_zero"], 1)
            for r, src in enumerate((b_re, b_im)):
                for q in range(2):
                    act.dma_start(B_RAW[q * N:(q + 1) * N, r, :, q * GC:(q + 1) * GC],
                                  src[0].rearrange("(t q) n c -> q n t c", q=2)[q]).then_inc(S["bc_in"], 16)
            for r, src in enumerate((c_re, c_im)):
                act.dma_start(C_RAW[:, r, :, :], src[0].rearrange("(b g) c n -> (g c) b n", b=WT)).then_inc(S["bc_in"], 16)

            act.wait_ge(S["x_in"], 32)
            for t in range(TB):
                act.activation(TMP[:, t, 0:D], X[:, t, :], ACT.Square, accum_out=SSQ[:, t:t + 1]).then_inc(S["x_sq"], 1)
            act.wait_ge(S["x_ms"], 1)
            act.activation(RSTD[:, 0:TB], SSQ[:, 0:TB], ACT.Sqrt).then_inc(S["x_root"], 1)
            act.wait_ge(S["angle_set"], 1)
            act.activation(S5[:, 12, :], S5[:, 10, :], ACT.Sin).then_inc(S["sine_set"], 1)
            act.activation(S5[:, 13, :], S5[:, 10, :], ACT.Sin, scale=0.5).then_inc(S["sine_set"], 1)

            for i in range(2):
                wait_full(act, f"u{i}")
                release(act.activation(UT[:, 2 * i:2 * i + 2, :], pairs(ps(f"u{i}")[:, :]), ACT.Copy),
                        f"u{i}")
            for i, job in enumerate(("q0", "q1", "k0", "k1")):
                wait_full(act, job)
                if i:
                    act.wait_ge(S["head_ms"], i)
                act.activation(SQ, ps(job)[:, :], ACT.Square).then_inc(S["head_sq"], 1)
                release(act.activation((Q, K)[i // 2][:, i % 2, :], ps(job)[:, :], ACT.Copy), job)
            for t in range(TB):
                wait_full(act, f"v{t}")
                release(act.activation(V[:, t, :], ps(f"v{t}")[:, :], ACT.Copy), f"v{t}")
            for r in range(2):
                wait_full(act, f"bt{r}")
                release(act.activation(BT[:, r, :, :], pairs(ps(f"bt{r}")[:, :], WT), ACT.Copy),
                        f"bt{r}")
            wait_full(act, "ct0")
            act.activation(CT[:, 0, :, :], pairs(ps("ct0")[:, :], WT), ACT.Copy)
            release(act.activation(CT[:, 1, :, :], pairs(ps("ct0")[:, :], WT), ACT.Copy, scale=-1.0),
                    "ct0")
            wait_full(act, "ct1")
            release(act.activation(CT[:, 2, :, :], pairs(ps("ct1")[:, :], WT), ACT.Copy, scale=-1.0),
                    "ct1")
            act.wait_ge(S["head_ms_all"], 1)
            act.activation(HSQ, HSQ, ACT.Sqrt).then_inc(S["head_root"], 1)

            for s in range(PAIRS + 1):
                for h in (2 * s, 2 * s + 1) if s < PAIRS else ():
                    act.wait_ge(S["abs_set"], h + 1)
                    st.link(act.activation(SOFT[:, h % 4, :], SOFT[:, h % 4, :], ACT.Exp))
                    act.activation(SOFT[:, h % 4, :], SOFT[:, h % 4, :], ACT.Ln, bias=1.0).then_inc(S["soft_set"], 1)
                for h in (2 * s - 2, 2 * s - 1) if s >= 1 else ():
                    act.wait_ge(S["cum_full"], h + 1)
                    if h >= 2:
                        wait_full(act, f"o{h // 2 - 1}")
                    release(act.activation(PROB[:, h % 2, :], ps(f"z{h}")[:, 0:384], ACT.Exp),
                            f"z{h}")

            act.wait_ge(S["tables_set"], 1)
            for i in range(DT):
                wait_full(act, f"g{i}")
                release(act.activation(GATE[:, 2 * i:2 * i + 2, :], pairs(ps(f"g{i}")[:, :]), ACT.Sigmoid),
                        f"g{i}")
            for b in range(WT):
                released(act, f"y{b}")
                act.activation(GY[:, b, :], GY[:, b, :], ACT.Gelu_apprx_tanh).then_inc(S["gelu_set"], 1)
            for i in range(DT):
                wait_full(act, f"glu{i}")
                if i >= 4:
                    act.wait_ge(S["mixed_set"], i - 3)
                act.activation(SZ[:, i % 4, :], ps(f"glu{i}")[:, SEQ:2 * SEQ], ACT.Sigmoid,
                               bias=PAR[:, P_BGLU + DT + i:P_BGLU + DT + i + 1]).then_inc(S["sz_set"], 1)

            act.wait_ge(S["mixed_set"], DT)
            act.dma_start(WR, w_router[0].rearrange("(k p) n -> p k n", p=P)).then_inc(S["router_in"], 16)
            act.dma_start(BROUT[0:1, :], b_router).then_inc(S["router_in"], 16)
            act.dma_start(BDOWN[0:E, :], b_down[0]).then_inc(S["down_bias_in"], 16)
            for t in range(TB):
                released(act, f"out{2 + t}")
                act.activation(TMP[:, t, 0:D], X2[:, t, :], ACT.Square, accum_out=SSQ[:, 2 + t:3 + t]).then_inc(S["x2_sq"], 1)
            act.wait_ge(S["x2_ms"], 1)
            act.activation(RSTD[:, 2:4], SSQ[:, 2:4], ACT.Sqrt).then_inc(S["x2_root"], 1)
            act.wait_ge(S["x2_sq"], TB)
            act.dma_start(WPG, w_ple_gate[0].rearrange("(k p) n -> p k n", p=P)).then_inc(S["ple_in"], 16)
            act.dma_start(WPP, w_ple_proj[0].rearrange("(k p) n -> p k n", p=P)).then_inc(S["ple_in"], 16)
            act.dma_start(PIN, p[0, 0].rearrange("(t p) n -> p t n", p=P)).then_inc(S["ple_in"], 16)
            act.dma_start(GPOST, g_ple_post[0:1, :].broadcast_to([P, D])).then_inc(S["ple_in"], 16)
            act.wait_ge(S["logit_top"], 1)
            for t in range(TB):
                act.activation(GATES[:, t, :], LOGIT[:, t, 0:E], ACT.Exp, bias=NTOP[:, t:t + 1]).then_inc(S["exp_set"], 1)
            act.wait_ge(S["split_set"], 1)
            act.dma_start(BUP[0:E, :], b_up[0]).then_inc(S["up_bias_in"], 16)

            def expert(m, n):
                act.wait_ge(m["g_set"], n + 1)
                act.activation(ACTS[:, 2, :], ACTS[:, 0, :], ACT.Sigmoid, scale=ALPHA).then_inc(m["sig_set"], 1)
                act.wait_ge(m["at_full"], n + 1)
                act.activation(ACTT, pairs(bank[ATB][:, :], WT), ACT.Copy).then_inc(m["at_set"], 1)
                act.wait_ge(m["y_full"], n + 1)
                act.activation(Y, bank[YB][:, :], ACT.Copy).then_inc(m["y_set"], 1)

            with act.Fori(0, E - 1) as e:
                expert(M, e)
            act.wait_ge(S["pp_set"], 4)
            for t in range(TB):
                act.activation(WPP[:, t, :], PLEV[:, t, :], ACT.Square, accum_out=PSQ[:, t:t + 1]).then_inc(S["pp_sq"], 1)
            act.wait_ge(S["pp_ms"], 1)
            act.activation(PRT, PSQ, ACT.Sqrt).then_inc(S["pp_root"], 1)
            expert(M, E - 1)
            act.wait_ge(S["flag_set"], 1)
            crowd = act.value_load(flag[0:1, 0:1], min_val=0, max_val=SEQ)
            with act.If(crowd > CAP):
                with act.Fori(0, E) as e:
                    with act.Fori(0, PASSES) as j:
                        expert(M, E + e * PASSES + j)

            act.wait_ge(S["x3_set"], 1)
            for t in range(TB):
                act.activation(XN3[:, t, :], X2[:, t, :], ACT.Square, accum_out=SSQ[:, 4 + t:5 + t]).then_inc(S["x3_sq"], 1)
            act.wait_ge(S["x3_ms"], 1)
            act.activation(RSTD[:, 4:6], SSQ[:, 4:6], ACT.Sqrt).then_inc(S["x3_root"], 1)
            for i in range(4):
                t, c = divmod(i, 2)
                act.wait_ge(S["pg_full"], i + 1)
                act.activation(GSIG[:, t, 512 * c:512 * (c + 1)], bank[i][:, :], ACT.Sigmoid).then_inc(S["pg_sig"], 1)

        @block.vector
        def _(dve):
            st = Steps(dve, S["dve_step"])
            T = lambda i: S5[:, i, :]

            def ts(*a):
                return st.link(dve.tensor_scalar(*a))

            def tt(*a):
                return st.link(dve.tensor_tensor(*a))

            def stt(*a):
                return st.link(dve.scalar_tensor_tensor(*a))

            def mean_plus_eps(ap, n):
                return dve.tensor_scalar(ap, ap, 1.0 / n, EPS, ALU.mult, ALU.add)

            dve.wait_ge(S["dt_in"], 16)
            dve.tensor_copy(PR[32:48, :].rearrange("p (q n) -> p q n", q=2),
                            spread(LDT[32:48, :], N)).then_inc(S["dt_rows"], 1)
            dve.wait_ge(S["x_sq"], TB)
            mean_plus_eps(SSQ[:, 0:TB], D).then_inc(S["x_ms"], 1)
            dve.wait_ge(S["x_root"], 1)
            st.link(dve.reciprocal(RSTD[:, 0:TB], RSTD[:, 0:TB]))
            for t in range(TB):
                dve.tensor_scalar(X[:, t, :], X[:, t, :], RSTD[:, t:t + 1], None, ALU.mult).then_inc(S["x_normal"], 1)
            wait_full(dve, "par")
            release(dve.tensor_copy(PAR, ps("par")[:, 0:NPAR]), "par")
            released(dve, "par")
            for i in range(4):
                t, half = divmod(i, 2)
                wait_full(dve, f"ht{i}")
                release(dve.tensor_tensor(HT[:, 4 * half:4 * half + 4, t * P:(t + 1) * P], pairs(ps(f"ht{i}")[:, :], 4),
                                          spread(PAR[:, P_GMIX + 4 * half:P_GMIX + 4 * half + 4], P), ALU.mult),
                        f"ht{i}")

            def expm1(y, v, z):
                ts(z, v, 1.0 / 2 ** SQUARINGS, None, ALU.mult)
                ts(y, z, 1.0 / TAYLOR, 1.0, ALU.mult, ALU.add)
                for k in range(TAYLOR - 1, 1, -1):
                    stt(y, y, 1.0 / k, z, ALU.mult, ALU.mult)
                    ts(y, y, 1.0, None, ALU.add)
                tt(y, y, z, ALU.mult)
                for _ in range(SQUARINGS):
                    stt(y, y, 2.0, y, ALU.add, ALU.mult)

            LR, LI = PAR[:, P_ARE:P_ARE + TILES], PAR[:, P_AIM:P_AIM + TILES]
            expm1(T(0), PAR[:, P_LDT:P_LDT + TILES], T(1))
            ts(T(0), T(0), 1.0, None, ALU.add)
            tt(T(2), LR, T(0), ALU.mult)
            tt(T(3), LI, T(0), ALU.mult)
            expm1(T(4), T(2), T(1))
            ts(RHO, T(4), 1.0, None, ALU.add)
            ts(T(5), T(3), 1.0 / TWO_PI, None, ALU.mult)
            ts(T(5), T(5), ROUNDER, None, ALU.add)
            ts(T(5), T(5), -ROUNDER, None, ALU.add)
            stt(T(10), T(5), -TWO_PI_HI, T(3), ALU.mult, ALU.add)
            stt(T(10), T(5), -TWO_PI_MID, T(10), ALU.mult, ALU.add)
            stt(T(10), T(5), -TWO_PI_LO, T(10), ALU.mult, ALU.add)
            dve.tensor_scalar(T(10), T(10), PI_F32, -PI_F32, ALU.min, ALU.max).then_inc(S["angle_set"], 1)
            dve.wait_ge(S["sine_set"], 2)
            stt(T(14), T(13), -2.0, T(13), ALU.mult, ALU.mult)
            ts(AKC, T(14), 1.0, None, ALU.add)
            st.link(dve.tensor_copy(AKS, T(12)))
            tt(T(6), T(4), AKC, ALU.mult)
            tt(T(6), T(6), T(14), ALU.add)
            tt(T(7), RHO, T(12), ALU.mult)
            tt(T(8), LR, LR, ALU.mult)
            tt(T(9), LI, LI, ALU.mult)
            tt(T(8), T(8), T(9), ALU.add)
            st.link(dve.reciprocal(T(8), T(8)))
            tt(T(16), T(6), LR, ALU.mult)
            tt(T(17), T(7), LI, ALU.mult)
            tt(T(16), T(16), T(17), ALU.add)
            tt(T(16), T(16), T(8), ALU.mult)
            tt(T(18), T(7), LR, ALU.mult)
            tt(T(19), T(6), LI, ALU.mult)
            tt(T(18), T(18), T(19), ALU.subtract)
            tt(T(18), T(18), T(8), ALU.mult)
            dve.wait_ge(S["bc_in"], 16 * 6)
            fr, fi = spread(T(16), 2 * GC), spread(T(18), 2 * GC)
            scratch = area(A_X, TILES, 2 * GC)
            for r, (f0, f1, op) in enumerate(((fr, fi, ALU.subtract), (fi, fr, ALU.add))):
                released(dve, "ht3")
                st.did(dve.tensor_tensor(B_BAR[:, r, :, :], B_RAW[:, 0, :, :], f0, ALU.mult))
                tt(scratch, B_RAW[:, 1, :, :], f1, ALU.mult)
                tt(B_BAR[:, r, :, :], B_BAR[:, r, :, :], scratch, op)
            dve.wait_ge(S["odd_set"], 1)
            odd = ODD.bitcast(I32)
            ts(odd, odd, 4, 1, ALU.logical_shift_right, ALU.bitwise_and)
            st.link(dve.tensor_copy(PARITY[:, 1:2], odd))
            ts(PARITY[:, 0:1], PARITY[:, 1:2], -1.0, 1.0, ALU.mult, ALU.add)
            for r in range(2):
                for q in range(2):
                    st.did(dve.tensor_scalar(C_MASK[:, r, :, q * N:(q + 1) * N], C_RAW[:, r, :, :],
                                             PARITY[:, q:q + 1], None, ALU.mult))
            st.settle()
            dve.memset(COS[:, :, 0:1], 1.0).then_inc(S["bbar_set"], 1)
            st.link(dve.memset(SIN[:, :, 0:1], 0.0))

            k = 1
            while k < SEQ:
                c_k, s_k = spread(AKC, k), spread(AKS, k)
                tmp = area(A_X, TILES * k).rearrange("p (a b) -> p a b", a=TILES)
                c0, s0, c1, s1 = COS[:, :, 0:k], SIN[:, :, 0:k], COS[:, :, k:2 * k], SIN[:, :, k:2 * k]
                st.did(dve.tensor_tensor(tmp, s0, s_k, ALU.mult))
                tt(c1, c0, c_k, ALU.mult)
                st.did(dve.tensor_tensor(s1, s0, c_k, ALU.mult))
                tt(c1, c1, tmp, ALU.subtract)
                tt(tmp, c0, s_k, ALU.mult)
                tt(s1, s1, tmp, ALU.add)
                k *= 2
                if k < SEQ:
                    st.did(dve.tensor_tensor(T(20), AKC, AKC, ALU.mult))
                    st.did(dve.tensor_tensor(T(21), AKS, AKS, ALU.mult))
                    stt(T(22), AKC, 2.0, AKS, ALU.mult, ALU.mult)
                    st.did(dve.tensor_tensor(AKC, T(20), T(21), ALU.subtract))
                    st.link(dve.tensor_copy(AKS, T(22)))
            dve.memset(SUM[:, 0:1], 0.0).then_inc(S["tables_set"], 1)

            for i in range(4):
                dve.wait_ge(S["head_sq"], i + 1)
                dve.tensor_reduce(HSQ[:, H * i:H * (i + 1)], SQ.rearrange("p (h d) -> p h d", h=H), AX,
                                  ALU.add).then_inc(S["head_ms"], 1)
            dve.wait_ge(S["head_ms"], 4)
            mean_plus_eps(HSQ, DH).then_inc(S["head_ms_all"], 1)
            dve.wait_ge(S["head_root"], 1)
            st.link(dve.reciprocal(HSQ, HSQ))
            for i in range(4):
                v = (Q, K)[i // 2][:, i % 2, :].rearrange("p (h d) -> p h d", h=H)
                released(dve, f"{'qk'[i // 2]}{i % 2}")
                dve.tensor_tensor(v, v, spread(HSQ[:, H * i:H * (i + 1)], DH), ALU.mult).then_inc(S["heads_set"], 1)
            for i in range(4):
                job = f"{'qk'[i // 2]}t{i % 2}"
                wait_full(dve, job)
                dst, col, scale = ((QT, P_GQ, DH ** -0.5), (KT, P_GK, 1.0))[i // 2]
                t = i % 2
                release(dve.tensor_scalar(dst[:, :, t * P:(t + 1) * P], pairs(ps(job)[:, :], PAIRS), PAR[:, col:col + 1],
                                          scale, ALU.mult, ALU.mult), job)

            for s in range(PAIRS + 2):
                for h in (2 * s, 2 * s + 1) if s < PAIRS else ():
                    wait_full(dve, f"z{h}")
                    if h >= 4:
                        dve.wait_ge(S["cum_full"], h - 3)
                    ts(SOFT[:, h % 4, :], ps(f"z{h}")[:, 0:384], 0.0, -2.0, ALU.max, ALU.mult)
                    dve.tensor_tensor(SOFT[:, h % 4, :], SOFT[:, h % 4, :], ps(f"z{h}")[:, 0:384],
                                      ALU.add).then_inc(S["abs_set"], 1)
                for h in (2 * s - 2, 2 * s - 1) if 1 <= s <= PAIRS else ():
                    dve.wait_ge(S["soft_set"], h + 1)
                    dve.scalar_tensor_tensor(SOFT[:, h % 4, :], ps(f"z{h}")[:, 0:384], 0.0, SOFT[:, h % 4, :],
                                             ALU.max, ALU.add).then_inc(S["sp_set"], 1)
                if s >= 2:
                    job = f"o{s - 2}"
                    wait_full(dve, job)
                    release(dve.tensor_copy(OT[:, s - 2, :], ps(job)[:, 0:SEQ]), job)

            def y_out(b):
                wait_full(dve, f"y{b}")
                release(dve.scalar_tensor_tensor(GY[:, b, :], UT[:, b, :], PAR[:, P_DSKIP + b:P_DSKIP + b + 1],
                                                 ps(f"y{b}")[:, 0:SEQ], ALU.mult, ALU.add), f"y{b}")

            def mix_attention():
                for i in range(4):
                    wait_full(dve, f"a{i}")
                    released(dve, f"g{i}")
                    release(dve.tensor_tensor(GATE[:, 2 * i:2 * i + 2, :], GATE[:, 2 * i:2 * i + 2, :],
                                              pairs(ps(f"a{i}")[:, :]), ALU.mult), f"a{i}")

            for i in range(TILES):
                b, j = divmod(i, 4)
                job = f"x{i}"
                m1, m2 = ROT[:, i % 2, 0, :], ROT[:, i % 2, 1, :]
                wait_full(dve, job)
                if i >= 2:
                    dve.wait_ge(S["back_set"], 2 * (i - 1))
                st.did(dve.tensor_tensor(pairs(m1), pairs(ps(job)[:, :]), COS[:, i:i + 1, :].broadcast_to([P, 2, SEQ]), ALU.mult))
                release(dve.tensor_tensor(pairs(m2), pairs(ps(job)[:, :]), SIN[:, i:i + 1, :].broadcast_to([P, 2, SEQ]),
                                          ALU.mult), job)
                released(dve, job)
                st.did(dve.tensor_tensor(m1[:, 0:SEQ], m1[:, 0:SEQ], m2[:, SEQ:], ALU.add))
                tt(m1[:, SEQ:], m1[:, SEQ:], m2[:, 0:SEQ], ALU.subtract)
                decay = RHO[:, i:i + 1].broadcast_to([P, SEQ])
                dve.tensor_tensor_scan(m2[:, 0:SEQ], decay, m1[:, 0:SEQ], 0.0, ALU.mult, ALU.add)
                dve.tensor_tensor_scan(m2[:, SEQ:], decay, m1[:, SEQ:], 0.0, ALU.mult, ALU.add).then_inc(S["rot_set"], 1)
                if j == 3 and b:
                    y_out(b - 1)
            mix_attention()
            y_out(3)

            released(dve, "a3")
            released(dve, "g7")
            for i in range(DT):
                job = f"glu{i}"
                z = SZ[:, i % 4, :]
                dve.wait_ge(S["sz_set"], i + 1)
                release(dve.scalar_tensor_tensor(z, ps(job)[:, 0:SEQ], PAR[:, P_BGLU + i:P_BGLU + i + 1], z,
                                                 ALU.add, ALU.mult), job)
                released(dve, job)
                tt(z, z, GATE[:, DT + i, :], ALU.mult)
                dve.tensor_tensor(GATE[:, i, :], GATE[:, i, :], z, ALU.add).then_inc(S["mixed_set"], 1)
            dve.wait_ge(S["x_again"], 16 * TB)
            for i in range(4):
                c, t = divmod(i, 2)
                wait_full(dve, f"out{i}")
                part = X2[:, t, 512 * c:512 * (c + 1)]
                release(dve.tensor_tensor(part, part, ps(f"out{i}")[:, :], ALU.add), f"out{i}")

            dve.wait_ge(S["x2_sq"], TB)
            mean_plus_eps(SSQ[:, 2:4], D).then_inc(S["x2_ms"], 1)
            dve.wait_ge(S["x2_root"], 1)
            st.link(dve.reciprocal(RSTD[:, 2:4], RSTD[:, 2:4]))
            for t in range(TB):
                dve.tensor_scalar(XN[:, t, :], X2[:, t, :], RSTD[:, 2 + t:3 + t], None, ALU.mult).then_inc(S["x2_normal"], 1)
            for i in range(4):
                t, half = divmod(i, 2)
                wait_full(dve, f"xt{i}")
                release(dve.tensor_tensor(H2T[:, 4 * half:4 * half + 4, t * P:(t + 1) * P], pairs(ps(f"xt{i}")[:, :], 4),
                                          spread(PAR[:, P_GFFN + 4 * half:P_GFFN + 4 * half + 4], P), ALU.mult),
                        f"xt{i}")

            dve.wait_ge(S["mixed_set"], DT)
            st.did(dve.memset(LOGIT[:, :, E:], NEVER))
            st.did(dve.memset(TOP8, NEVER))
            st.did(dve.memset(RANK[:, :, E:E + 1], -1.0))
            st.settle()
            wait_full(dve, "lg")
            release(dve.tensor_copy(LOGIT[:, :, 0:E], ps("lg")[:, 0:TB * E].rearrange("p (t e) -> p t e", t=TB)), "lg")
            released(dve, "lg")
            for t in range(TB):
                st.did(dve.max(TOP8[:, 8 * t:8 * t + 8], LOGIT[:, t, 0:E]))
            st.settle()
            for t in range(TB):
                st.did(dve.tensor_scalar(NTOP[:, t:t + 1], TOP8[:, 8 * t:8 * t + 1], -1.0, None, ALU.mult))
            st.settle()
            dve.memset(TOP8.rearrange("p (t k) -> p t k", t=TB)[:, :, 4:8], NEVER).then_inc(S["logit_top"], 1)
            dve.wait_ge(S["logit_top"], 1)
            for t in range(TB):
                st.did(dve.match_replace(LEFT[:, t, :], TOP8[:, 8 * t:8 * t + 8], LOGIT[:, t, :], TAKEN))
            st.settle()
            dve.tensor_tensor(CHOSEN, LEFT[:, :, 0:E], LOGIT[:, :, 0:E], ALU.not_equal).then_inc(S["chosen_set"], 1)
            dve.wait_ge(S["exp_set"], TB)
            dve.wait_ge(S["chosen_set"], 1)
            tt(GATES, GATES, CHOSEN, ALU.mult)
            st.link(dve.tensor_reduce(SUM[:, 0:TB], GATES, AX, ALU.add))
            st.link(dve.reciprocal(SUM[:, 0:TB], SUM[:, 0:TB]))
            dve.tensor_tensor(GATES, GATES, spread(SUM[:, 0:TB], E), ALU.mult).then_inc(S["gates_ready"], 1)
            wait_full(dve, "rk")
            st.did(dve.scalar_tensor_tensor(RANK[:, :, 0:E], ps("rk")[:, 0:TB * E].rearrange("p (t e) -> p t e", t=TB), 1.0,
                                            CHOSEN, ALU.add, ALU.mult))
            release(dve.tensor_reduce(CNT[0:1, 0:1], ps("rk")[0:1, TB * E:TB * E + E], AX, ALU.max), "rk")
            released(dve, "rk")
            dve.tensor_copy(flag[0:1, 0:1], CNT[0:1, 0:1]).then_inc(S["flag_set"], 1)
            st.link(dve.tensor_scalar(RANK[:, :, 0:E], RANK[:, :, 0:E], -1.0, None, ALU.add))
            dve.wait_ge(S["slots_set"], 1)
            st.link(dve.tensor_copy(SLOT, SLOT_I))
            st.link(dve.tensor_copy(XB[:, 0, :, :], XN))
            tt(REST, XN, XB[:, 0, :, :], ALU.subtract)
            st.link(dve.tensor_copy(XB[:, 1, :, :], REST))
            tt(REST, REST, XB[:, 1, :, :], ALU.subtract)
            dve.tensor_copy(XB[:, 2, :, :], REST).then_inc(S["split_set"], 1)
            wait_full(dve, "gt")
            release(dve.tensor_copy(GT[0:E, :, :], ps("gt")[0:E, 0:SEQ].rearrange("p (t n) -> p t n", t=TB)), "gt")
            for i in range(4):
                t, c = divmod(i, 2)
                wait_full(dve, f"bd{i}")
                part = X2[:, t, 512 * c:512 * (c + 1)]
                release(dve.tensor_tensor(part, part, ps(f"bd{i}")[:, :], ALU.add), f"bd{i}")

            def at(e):
                return slice(e, e + 1) if isinstance(e, int) else bass.ds(e, 1)

            def select(m, e, slots):
                for t in range(TB):
                    last = dve.tensor_scalar(SELB[:, t, :], slots, RANK[:, t, at(e)], None, ALU.is_equal)
                last.then_inc(m["sel_set"], 1)

            def select_weighted(m, e, slots):
                for t in range(TB):
                    last = dve.tensor_scalar(pairs(WSEL[:, t, :]), slots.unsqueeze(1).broadcast_to([P, 2, CAP]),
                                             RANK[:, t, at(e)], GATES[:, t, at(e)], ALU.is_equal, ALU.mult)
                last.then_inc(m["wsel_set"], 1)

            def pick(m, e):
                dve.tensor_copy(PICK[0:E, :], ident[0:E, at(e)].broadcast_to([E, CAP])).then_inc(m["pick_set"], 1)

            def gathered(m, n):
                dve.wait_ge(m["gx_full"], n + 1)
                dve.tensor_tensor(XS, pairs(bank[GX][:, :], DT), spread(PAR[:, P_GFFN:P_GFFN + DT], CAP),
                                  ALU.mult).then_inc(m["xs_set"], 1)

            def activate(m, n):
                dve.wait_ge(m["up_g"], n + 1)
                dve.tensor_scalar(ACTS[:, 0, :], bank[UG][:, :], LIMIT, None, ALU.min).then_inc(m["g_set"], 1)
                dve.wait_ge(m["up_u"], n + 1)
                dve.tensor_scalar(ACTS[:, 1, :], bank[UU][:, :], LIMIT, -LIMIT, ALU.min, ALU.max).then_inc(m["dve_step"], 1)
                dve.wait_ge(m["dve_step"], n * 2 + 1)
                dve.scalar_tensor_tensor(ACTS[:, 1, :], ACTS[:, 1, :], 1.0, ACTS[:, 0, :], ALU.add,
                                         ALU.mult).then_inc(m["dve_step"], 1)
                dve.wait_ge(m["dve_step"], n * 2 + 2)
                dve.wait_ge(m["sig_set"], n + 1)
                dve.tensor_tensor(ACTS[:, 1, :], ACTS[:, 1, :], ACTS[:, 2, :], ALU.mult).then_inc(m["act_set"], 1)

            def weights_back(m, n):
                dve.wait_ge(m["wt_full"], n + 1)
                dve.tensor_copy(WSELT, bank[WTB][:, 0:SEQ].rearrange("p (t n) -> p t n", t=TB)).then_inc(m["wt_set"], 1)

            def add_up(m, n):
                for q in range(4):
                    t, c = divmod(q, 2)
                    dve.wait_ge(m["sc_full"], n * 4 + q + 1)
                    part = X2[:, t, 512 * c:512 * (c + 1)]
                    dve.tensor_tensor(part, part, bank[SCATTER[q]][:, :], ALU.add).then_inc(m["sc_add"], 1)

            def expert(m, n):
                select(m, n + 1, SLOT[:, 0:CAP])
                select_weighted(m, n, SLOT[:, 0:CAP])
                activate(m, n)
                gathered(m, n + 1)
                weights_back(m, n)
                pick(m, n + 1)
                add_up(m, n)

            select(M, 0, SLOT[:, 0:CAP])
            pick(M, 0)
            gathered(M, 0)
            with dve.Fori(0, E - 1) as e:
                expert(M, e)
            dve.wait_ge(S["pt_full"], 1)
            dve.tensor_copy(PT_IN, pairs(bank[YB][:, :], PLE // P)).then_inc(S["pt_set"], 1)
            for i in range(4):
                t, c = divmod(i, 2)
                dve.wait_ge(S["pp_full"], i + 1)
                dve.tensor_copy(PLEV[:, t, 512 * c:512 * (c + 1)], bank[SCATTER[i]][:, :]).then_inc(S["pp_set"], 1)
            dve.wait_ge(S["pp_sq"], TB)
            mean_plus_eps(PSQ, D).then_inc(S["pp_ms"], 1)
            dve.wait_ge(S["pp_root"], 1)
            st.link(dve.reciprocal(PRT, PRT))
            dve.wait_ge(S["ple_in"], 64)
            for t in range(TB):
                st.did(dve.scalar_tensor_tensor(PLEV[:, t, :], PLEV[:, t, :], PRT[:, t:t + 1], GPOST, ALU.mult, ALU.mult))
            st.settle()
            expert(M, E - 1)
            dve.wait_ge(S["flag_set"], 1)
            crowd = dve.value_load(flag[0:1, 0:1], min_val=0, max_val=SEQ)
            with dve.If(crowd > CAP):
                with dve.Fori(0, E) as e:
                    with dve.Fori(0, PASSES) as j:
                        n = E + e * PASSES + j
                        slots = SLOT[:, bass.ds(j * CAP + CAP, CAP)]
                        select(M, e, slots)
                        select_weighted(M, e, slots)
                        pick(M, e)
                        gathered(M, n + 1)
                        activate(M, n)
                        weights_back(M, n)
                        add_up(M, n)

            st.settle()
            dve.wait_ge(M["sc_add"], 4 * E)
            dve.memset(SUM[:, 0:1], 0.0).then_inc(S["x3_set"], 1)
            dve.wait_ge(S["x3_sq"], TB)
            mean_plus_eps(SSQ[:, 4:6], D).then_inc(S["x3_ms"], 1)
            dve.wait_ge(S["x3_root"], 1)
            st.link(dve.reciprocal(RSTD[:, 4:6], RSTD[:, 4:6]))
            for t in range(TB):
                dve.tensor_scalar(XN3[:, t, :], X2[:, t, :], RSTD[:, 4 + t:5 + t], None, ALU.mult).then_inc(S["x3_normal"], 1)
            for i in range(4):
                t, half = divmod(i, 2)
                dve.wait_ge(S["xt3_full"], i + 1)
                dve.tensor_tensor(XT3[:, 4 * half:4 * half + 4, t * P:(t + 1) * P], pairs(bank[4 + i][:, :], 4),
                                  spread(PAR[:, P_GPLE + 4 * half:P_GPLE + 4 * half + 4], P), ALU.mult).then_inc(S["xt3_set"], 1)
            for i in range(4):
                t, c = divmod(i, 2)
                cols = slice(512 * c, 512 * (c + 1))
                dve.wait_ge(S["pg_sig"], i + 1)
                tt(GSIG[:, t, cols], GSIG[:, t, cols], PLEV[:, t, cols], ALU.mult)
                dve.tensor_tensor(X2[:, t, cols], X2[:, t, cols], GSIG[:, t, cols], ALU.add).then_inc(S["fin_set"], 1)

        @block.tensor
        def _(pe):
            I = ident[:, :]

            def take(job):
                at, use = BANKS[job]
                if use:
                    pe.wait_ge(free[at], use)
                return bank[at]

            def done(ins, job):
                return ins.then_inc(full[BANKS[job][0]], 1)

            def arrive(key):
                at, use = TURN[key]
                pe.wait_ge(arrived[at], 16 * (use + 1))

            pe.wait_ge(S["ident_set"], 1)
            pe.wait_ge(S["params_in"], 16 * 11)
            pe.wait_ge(S["dt_rows"], 1)
            done(pe.transpose(take("par")[:, 0:NPAR], PR[0:NPAR, :], I[0:NPAR, 0:NPAR]), "par")
            for i in range(4):
                t, half = divmod(i, 2)
                b = take(f"ht{i}")
                pe.wait_ge(S["x_normal"], t + 1)
                for k in range(4):
                    last = pe.transpose(b[:, P * k:P * (k + 1)], X[:, t, P * (4 * half + k):P * (4 * half + k + 1)], I)
                done(last, f"ht{i}")

            def columns(job, key, a, parts, rhs, n=DT):
                b = take(job)
                for i, m in enumerate(parts):
                    for k in range(n):
                        last = pe.matmul(b[:, SEQ * i:SEQ * (i + 1)], weight(key, a)[:, k, P * m:P * (m + 1)], rhs[:, k, :],
                                         start=(k == 0), stop=(k == n - 1))
                return done(last, job)

            released(pe, "ht3")
            arrive(("in", 3))
            for i in range(2):
                last = columns(f"u{i}", ("in", 3), DT, (2 * i, 2 * i + 1), HT)
            for n, name in enumerate("qkv"):
                arrive(("in", n))
                for t in range(TB):
                    b = take(f"{name}{t}")
                    for k in range(DT):
                        last = pe.matmul(b[:, :], HT[:, k, t * P:(t + 1) * P], weight(("in", n), DT)[:, k, :],
                                         start=(k == 0), stop=(k == DT - 1))
                    done(last, f"{name}{t}")
            pe.wait_ge(S["bbar_set"], 1)
            for r in range(2):
                b = take(f"bt{r}")
                flat = B_BAR[:, r, :, :].rearrange("p t c -> p (t c)")
                for k in range(WT):
                    last = pe.transpose(b[:, P * k:P * (k + 1)], flat[:, P * k:P * (k + 1)], I)
                done(last, f"bt{r}")
            for r in range(2):
                b = take(f"ct{r}")
                for k in range(WT):
                    last = pe.transpose(b[:, P * k:P * (k + 1)], C_MASK[:, r, k, :], I)
                done(last, f"ct{r}")
            for i in range(4):
                job = f"{'qk'[i // 2]}t{i % 2}"
                b = take(job)
                pe.wait_ge(S["heads_set"], i + 1)
                for k in range(PAIRS):
                    last = pe.transpose(b[:, P * k:P * (k + 1)], (Q, K)[i // 2][:, i % 2, P * k:P * (k + 1)], I)
                done(last, job)

            released(pe, "kt1")
            for s in range(PAIRS + 2):
                if s < PAIRS:
                    zs = [take(f"z{2 * s + q}") for q in range(2)]
                    for k, (lo, n) in enumerate(((0, SEQ), (P, P))):
                        for q in range(2):
                            rows = slice(DH * q, DH * (q + 1))
                            pe.matmul(zs[q][:, SEQ * k:SEQ * k + n], KT[rows, s, P * k:P * (k + 1)], QT[rows, s, lo:lo + n],
                                      start=(k == 0), stop=False, skip_group_check=True)
                    for q in range(2):
                        for k in range(2):
                            last = pe.matmul(zs[q][:, SEQ * k:SEQ * k + P], ident_b[:, :], hide_b[:, :],
                                             start=False, stop=True, skip_group_check=True)
                        done(last, f"z{2 * s + q}")
                if 1 <= s <= PAIRS:
                    for h in (2 * s - 2, 2 * s - 1):
                        b, sp = ps(f"z{h}"), SOFT[:, h % 4, :]
                        pe.wait_ge(S["sp_set"], h + 1)
                        pe.matmul(b[:, 0:SEQ], neg_tri[:, :], sp[:, 0:SEQ], start=False, stop=True, skip_group_check=True)
                        pe.matmul(b[:, P:SEQ], neg_ones[:, :], sp[:, SEQ:], start=False, stop=True, skip_group_check=True)
                        pe.matmul(b[:, SEQ:SEQ + P], neg_tri[:, :], sp[:, SEQ:], start=False, stop=True,
                                  skip_group_check=True).then_inc(S["cum_full"], 1)
                if s >= 2:
                    b = take(f"o{s - 2}")
                    for k in range(2):
                        for q in range(2):
                            h = 2 * (s - 2) + q
                            released(pe, f"z{h}")
                            last = pe.matmul(b[DH * q:DH * (q + 1), P * k:SEQ], V[:, k, DH * h:DH * (h + 1)],
                                             PROB[:, q, SEQ * k:SEQ * (k + 1) - P * k],
                                             start=(k == 0), stop=(k == 1))
                    done(last, f"o{s - 2}")

            def s5_in(blk):
                bs = [take(f"x{4 * blk + j}") for j in range(4)]
                for r in range(2):
                    for j in range(4):
                        rows = slice(32 * j, 32 * j + 32)
                        last = pe.matmul(bs[j][:, SEQ * r:SEQ * (r + 1)], BT[rows, r, blk, :], UT[rows, blk, :],
                                         start=True, stop=True)
                        if r == 1:
                            done(last, f"x{4 * blk + j}")

            def s5_out(blk):
                b = take(f"y{blk}")
                pe.wait_ge(S["back_set"], 8 * (blk + 1))
                for k, (c, s, r) in enumerate(((0, 0, 0), (1, 1, 1), (2, 1, 0), (2, 0, 1))):
                    for j in range(4):
                        last = pe.matmul(b[32 * j:32 * j + 32, 0:SEQ], CT[:, c, blk, 32 * j:32 * j + 32],
                                         BACK[:, j, s, SEQ * r:SEQ * (r + 1)], start=(k == 0), stop=(k == 3))
                done(last, f"y{blk}")

            released(pe, "ct1")
            released(pe, "u1")
            pe.wait_ge(S["tables_set"], 1)
            s5_in(0)
            for blk in range(WT):
                key = ("in", 4 + blk)
                arrive(key)
                for i in range(2):
                    last = columns(f"g{2 * blk + i}", key, DT, (2 * i, 2 * i + 1), HT)
                if blk < WT - 1:
                    s5_in(blk + 1)
                else:
                    released(pe, "o3")
                    arrive(("attn", 0))
                    for i in range(4):
                        last = columns(f"a{i}", ("attn", 0), WT, (2 * i, 2 * i + 1), OT, WT)
                s5_out(blk)
            pe.wait_ge(S["gelu_set"], WT)
            arrive(("glu", 0))
            arrive(("glu", 1))
            for i in range(DT):
                b = take(f"glu{i}")
                for h in range(2):
                    m = i + DT * h
                    for k in range(WT):
                        last = pe.matmul(b[:, SEQ * h:SEQ * (h + 1)], weight(("glu", k // 2), 2)[:, k % 2, P * m:P * (m + 1)],
                                         GY[:, k, :], start=(k == 0), stop=(k == WT - 1))
                done(last, f"glu{i}")
            pe.wait_ge(S["mixed_set"], DT)
            for i in range(4):
                c, t = divmod(i, 2)
                b = take(f"out{i}")
                arrive(("out", c))
                for k in range(DT):
                    last = pe.matmul(b[:, :], GATE[:, k, t * P:(t + 1) * P], weight(("out", c), DT)[:, k, :],
                                     start=(k == 0), stop=(k == DT - 1))
                done(last, f"out{i}")
            for i in range(4):
                t, half = divmod(i, 2)
                b = take(f"xt{i}")
                pe.wait_ge(S["x2_normal"], t + 1)
                for k in range(4):
                    last = pe.transpose(b[:, P * k:P * (k + 1)], XN[:, t, P * (4 * half + k):P * (4 * half + k + 1)], I)
                done(last, f"xt{i}")
            b = take("lg")
            pe.wait_ge(S["router_in"], 32)
            for t in range(TB):
                released(pe, f"xt{2 * t + 1}")
                o = b[:, E * t:E * (t + 1)]
                pe.matmul(o, ONES[0:1, :], BROUT[0:1, :], start=True, stop=False)
                for k in range(DT):
                    last = pe.matmul(o, H2T[:, k, t * P:(t + 1) * P], WR[:, k, :], start=False, stop=(k == DT - 1))
            done(last, "lg")
            b = take("rk")
            pe.wait_ge(S["chosen_set"], 1)
            pe.matmul(b[:, 0:E], TRI, CHOSEN[:, 0, :], start=True, stop=True)
            pe.matmul(b[:, E:2 * E], ONES, CHOSEN[:, 0, :], start=True, stop=False)
            pe.matmul(b[:, E:2 * E], TRI, CHOSEN[:, 1, :], start=False, stop=True)
            for t in range(TB):
                last = pe.matmul(b[0:1, 2 * E:3 * E], ONES[:, 0:1], CHOSEN[:, t, :], start=(t == 0), stop=(t == 1))
            done(last, "rk")
            b = take("gt")
            pe.wait_ge(S["gates_ready"], 1)
            for t in range(TB):
                last = pe.transpose(b[0:E, P * t:P * (t + 1)], GATES[:, t, :], I)
            done(last, "gt")
            released(pe, "gt")
            pe.wait_ge(S["down_bias_in"], 16)
            for i in range(4):
                t, c = divmod(i, 2)
                done(pe.matmul(take(f"bd{i}")[:, :], GT[0:E, t, :], BDOWN[0:E, 512 * c:512 * (c + 1)],
                               start=True, stop=True), f"bd{i}")

            def gather(m, n):
                pe.wait_ge(m["sel_set"], n + 1)
                for d in range(DT):
                    for i in range(3 * TB):
                        part, t = divmod(i, TB)
                        last = pe.matmul(bank[GX][:, CAP * d:CAP * (d + 1)], XB[:, part, t, P * d:P * (d + 1)], SELB[:, t, :],
                                         start=(i == 0), stop=(i == 3 * TB - 1))
                last.then_inc(m["gx_full"], 1)

            def chunk(c):
                return place(EXP_PLACE[c]).rearrange("p (a n) -> p a n", a=2 if c < 4 else 4)

            def up(m, n, wait_chunk, leave_chunk):
                pe.wait_ge(m["xs_set"], n + 1)
                pe.wait_ge(m["pick_set"], n + 1)
                for w in range(2):
                    for h in range(2):
                        pe.matmul(bank[UG + w][HALF * h:HALF * (h + 1), :], PICK[0:E, :],
                                  BUP[0:E, 512 * (2 * w + h):512 * (2 * w + h + 1)], start=True, stop=False)
                for c in range(4):
                    wait_chunk(c)
                    for k in (2 * c, 2 * c + 1):
                        for w in range(2):
                            for h in range(2):
                                last = pe.matmul(bank[UG + w][HALF * h:HALF * (h + 1), :], XS[:, k, :],
                                                 chunk(c)[:, k % 2, 512 * (2 * w + h):512 * (2 * w + h + 1)],
                                                 start=False, stop=(k == DT - 1))
                            if k == DT - 1:
                                last.then_inc(m[("up_g", "up_u")[w]], 1)
                    leave_chunk(last, c)

            def down(m, n, wait_chunk, leave_chunk):
                pe.wait_ge(m["wsel_set"], n + 1)
                for t in range(TB):
                    last = pe.transpose(bank[WTB][:, P * t:P * (t + 1)], WSEL[:, t, :], I)
                last.then_inc(m["wt_full"], 1)
                pe.wait_ge(m["act_set"], n + 1)
                for j in range(4):
                    last = pe.transpose(bank[ATB][:, P * j:P * (j + 1)], ACTS[:, 1, P * j:P * (j + 1)], I)
                last.then_inc(m["at_full"], 1)
                pe.wait_ge(m["at_set"], n + 1)
                for h in range(2):
                    wait_chunk(4 + h)
                    for j in range(4):
                        for c in range(2):
                            last = pe.matmul(bank[YB][HALF * c:HALF * (c + 1), :], ACTT[:, j, HALF * h:HALF * (h + 1)],
                                             chunk(4 + h)[:, j, 512 * c:512 * (c + 1)],
                                             start=(h == 0 and j == 0), stop=(h == 1 and j == 3))
                    if h == 1:
                        last.then_inc(m["y_full"], 1)
                    leave_chunk(last, 4 + h)
                pe.wait_ge(m["wt_set"], n + 1)
                pe.wait_ge(m["y_set"], n + 1)
                for q in range(4):
                    t, c = divmod(q, 2)
                    rows = slice(HALF * c, HALF * (c + 1))
                    pe.matmul(bank[SCATTER[q]][:, :], WSELT[rows, t, :], Y[rows, :], start=True,
                              stop=True).then_inc(m["sc_full"], 1)

            def main_wait(n):
                return lambda c: pe.wait_ge(arrived[EXP_PLACE[c]], n * 16 + 16 * (EXP_USES[c] + 1))

            def main_leave(last, c):
                if c in READ:
                    last.then_inc(READ[c], 1)

            for i in range(NBANKS):
                pe.wait_ge(free[i], sum(1 for at, _ in BANKS.values() if at == i))
            pe.wait_ge(S["split_set"], 1)
            pe.wait_ge(S["up_bias_in"], 16)
            gather(M, 0)
            with pe.Fori(0, E - 1) as e:
                up(M, e, main_wait(e), main_leave)
                gather(M, e + 1)
                down(M, e, main_wait(e), main_leave)
            pe.wait_ge(S["ple_in"], 64)
            for k in range(PLE // P):
                for t in range(TB):
                    last = pe.transpose(bank[YB][:, SEQ * k + P * t:SEQ * k + P * (t + 1)], PIN[:, t, P * k:P * (k + 1)], I)
            last.then_inc(S["pt_full"], 1)
            pe.wait_ge(S["pt_set"], 1)
            pe.wait_ge(M["sc_add"], 4 * (E - 1))
            for i in range(4):
                t, c = divmod(i, 2)
                for k in range(PLE // P):
                    last = pe.matmul(bank[SCATTER[i]][:, :], PT_IN[:, k, P * t:P * (t + 1)], WPP[:, k, 512 * c:512 * (c + 1)],
                                     start=(k == 0), stop=(k == PLE // P - 1))
                last.then_inc(S["pp_full"], 1)
            up(M, E - 1, main_wait(E - 1), main_leave)
            gather(M, E)
            down(M, E - 1, main_wait(E - 1), main_leave)
            pe.wait_ge(S["flag_set"], 1)
            crowd = pe.value_load(flag[0:1, 0:1], min_val=0, max_val=SEQ)
            with pe.If(crowd > CAP):
                with pe.Fori(0, E) as e:
                    with pe.Fori(0, PASSES) as j:
                        n = E + e * PASSES + j
                        gather(M, n + 1)
                        up(M, n + 1, main_wait(n), main_leave)
                        down(M, n, main_wait(n), main_leave)
            for i in range(4):
                t, half = divmod(i, 2)
                pe.wait_ge(S["x3_normal"], t + 1)
                for k in range(4):
                    last = pe.transpose(bank[4 + i][:, P * k:P * (k + 1)], XN3[:, t, P * (4 * half + k):P * (4 * half + k + 1)], I)
                last.then_inc(S["xt3_full"], 1)
            for i in range(4):
                t, c = divmod(i, 2)
                pe.wait_ge(S["xt3_set"], 2 * t + 2)
                for k in range(DT):
                    last = pe.matmul(bank[i][:, :], XT3[:, k, P * t:P * (t + 1)], WPG[:, k, 512 * c:512 * (c + 1)],
                                     start=(k == 0), stop=(k == DT - 1))
                last.then_inc(S["pg_full"], 1)


_INS = ["x", "p", "g_mix", "w_in", "g_q", "g_k", "w_attn_branch", "a_re", "a_im", "log_dt", "b_re", "b_im", "c_re", "c_im",
        "d_skip", "w_glu", "b_glu", "w_out", "g_ffn", "w_router", "b_router", "w_up", "b_up", "w_down", "b_down",
        "g_ple_gate", "w_ple_gate", "w_ple_proj", "g_ple_post"]
_OUTS = [((1, 256, 1024), "float32")]


def kernel(**inputs):
    import numpy as _np
    import concourse.bacc as _bacc
    from concourse import mybir as _mybir
    from concourse.bass_utils import run_bass_kernel_spmd as _run

    nc = _bacc.Bacc("TRN2", target_bir_lowering=False, num_devices=1)
    arrays, args = {}, []
    for name in _INS:
        a = _np.ascontiguousarray(inputs[name])
        arrays[f"in_{name}_dram"] = a
        args.append(nc.dram_tensor(f"in_{name}_dram", a.shape, _mybir.dt.from_np(a.dtype), kind="ExternalInput").ap())
    for i, (shape, dtype) in enumerate(_OUTS):
        dt = _mybir.dt.from_np(_np.dtype(dtype))
        args.append(nc.dram_tensor(f"out_{i}_dram", shape, dt, kind="ExternalOutput").ap())
    hybrid_layer(nc, *args)
    r = _run(nc, [arrays], core_ids=[0])
    got = tuple(r.results[0][f"out_{i}_dram"] for i in range(len(_OUTS)))
    return got[0]
```

```python
from contextlib import ExitStack

import concourse.bass as bass
from concourse import mybir

P = 128
HALF = P // 2
BANK = 512
NBANKS = 8
F32 = mybir.dt.float32
BF16 = mybir.dt.bfloat16
I32 = mybir.dt.int32
ALU = mybir.AluOpType
ACT = mybir.ActivationFunctionType
AX = mybir.AxisListType.X

EPS = 1e-6
LIMIT = 7.0
ALPHA = 1.702
HIDDEN = -1e30
NEVER = -3e38
TAKEN = 3e38
TWO_PI = 6.283185307179586
TWO_PI_HI, TWO_PI_MID = 6.28125, 0.0019340515136718750
TWO_PI_LO = TWO_PI - TWO_PI_HI - TWO_PI_MID
ROUNDER = 12582912.0
PI_F32 = 3.1415925
SQUARINGS = 8
TAYLOR = 7
CAP = 64
BESIDE_ATTENTION = ("u0", "u1", "g0", "g1", "g2", "g3")
EARLY_GATES = 2


class Steps:

    def __init__(self, eng, sem):
        self.eng, self.sem, self.n, self.shift = eng, sem, 0, 0

    def did(self, ins):
        self.n += 1
        return ins.then_inc(self.sem, 1)

    def settle(self):
        self.eng.wait_ge(self.sem, self.n + self.shift)

    def link(self, ins):
        self.did(ins)
        self.settle()
        return ins


def order_of_banks():
    jobs = ["par"] + [f"ht{i}" for i in range(4)] + ["q0", "q1", "k0", "k1", "v0", "v1"]
    jobs += ["bt0", "bt1", "ct0", "ct1", "qt0", "qt1", "kt0", "kt1"]
    for s in range(4 + 2):
        if s < 4:
            jobs += [f"z{2 * s}", f"z{2 * s + 1}"]
        if s >= 2:
            jobs += [f"o{s - 2}"]
        if s == 5:
            jobs += [f"x{i}" for i in range(4)]
        jobs += [BESIDE_ATTENTION[s]]
    for b in range(4):
        if b < 3:
            jobs += [f"x{4 * b + 4 + i}" for i in range(4)]
        jobs += [f"g{b + 4}", f"y{b}"] if b < 3 else [f"g{b + 4}", "a0", "a1", f"y{b}", "a2", "a3"]
    jobs += [f"glu{i}" for i in range(8)]
    jobs += ["out0", "out1", "out2", "xt0", "xt1", "pt", "out3", "pp0", "pp1", "xt2", "xt3", "lg", "pp2", "rk", "pp3"]
    return {name: (i % NBANKS, i // NBANKS) for i, name in enumerate(jobs)}


def hybrid_layer(nc, x, p, g_mix, w_in, g_q, g_k, w_attn, a_re, a_im, log_dt, b_re, b_im, c_re, c_im, d_skip,
                 w_glu, b_glu, w_out, g_ffn, w_router, b_router, w_up, b_up, w_down, b_down,
                 g_ple_gate, w_ple_gate, w_ple_proj, g_ple_post, out):
    _, SEQ, D = x.shape
    PLE = p.shape[3]
    G, N = a_re.shape[1:]
    GC = b_re.shape[3]
    W = G * GC
    E = w_router.shape[2]
    F = w_down.shape[2]
    DH = g_q.shape[1]
    H = w_attn.shape[1] // DH
    TB = SEQ // P
    DT = D // P
    WT = W // P
    PAIRS = H // 2
    TILES = G * N // P
    assert (TB, DT, WT, PAIRS, TILES, E, F, PLE) == (2, 8, 4, 4, 16, 32, D, 2 * P)
    BANKS = order_of_banks()

    with ExitStack() as ctx:
        def sem(name):
            return ctx.enter_context(nc.semaphore(name))

        def sb(name, cols, dt=F32):
            return ctx.enter_context(nc.sbuf_tensor(name, [P, cols], dt))

        PLACES, PLACE = 6, 4096
        ring = sb("ring", PLACES * PLACE)
        arena = sb("arena", 27136)
        ident = sb("ident", P)
        neg_tri = sb("neg_tri", P)
        neg_ones = sb("neg_ones", P)
        small = sb("small", 680)
        ident_b = sb("ident_b", P, BF16)
        hide_b = sb("hide_b", P, BF16)
        flag = sb("flag", 1, I32)
        bank = [ctx.enter_context(nc.psum_tensor(f"bank{i}", [P, BANK], F32)) for i in range(NBANKS)]

        def area(at, *dims):
            n = 1
            for d in dims:
                n *= d
            ap = arena[:, at:at + n]
            if len(dims) == 2:
                return ap.rearrange("p (a b) -> p a b", a=dims[0])
            if len(dims) == 3:
                return ap.rearrange("p (a b c) -> p a b c", a=dims[0], b=dims[1])
            return ap

        def spread(ap, n):
            return ap.unsqueeze(2).broadcast_to([ap.shape[0], ap.shape[1], n])

        A_X, A_HT, A_Q, A_K, A_QT, A_KT, A_V, A_UT, A_OT, A_GY, A_TC, A_GATE, A_BT, A_CT = (
            0, 2048, 4096, 5120, 6144, 7168, 8192, 9216, 10240, 11264, 12288, 20480, 24576, 25600)
        X = area(A_X, TB, D)
        HT = area(A_HT, DT, SEQ)
        Q = area(A_Q, TB, 512)
        K = area(A_K, TB, 512)
        QT = area(A_QT, PAIRS, SEQ)
        KT = area(A_KT, PAIRS, SEQ)
        V = area(A_V, TB, 512)
        UT = area(A_UT, WT, SEQ)
        OT = area(A_OT, PAIRS, SEQ)
        GY = area(A_GY, WT, SEQ)
        COS = area(A_TC, TILES, SEQ)
        SIN = area(A_TC + 4096, TILES, SEQ)
        GATE = area(A_GATE, 2 * DT, SEQ)
        BT = area(A_BT, 2, WT, P)
        CT = area(A_CT, 3, WT, P)
        SQ = area(A_UT, 4, 512)
        SOFT = area(A_Q, 4, 384)
        PROB = area(A_GY, 2, 384)
        ROT = area(A_X, 2, 2, 512)
        BACK = area(A_Q, 4, 2, 512)
        X_SQ = area(A_TC, TB, D)
        B_RAW = area(A_GATE, 2, TILES, 2 * GC)
        B_BAR = area(A_GATE + 1024, 2, TILES, 2 * GC)
        C_RAW = area(A_GATE + 2048, 2, WT, N)
        C_MASK = area(A_GATE + 2560, 2, WT, P)
        S5 = area(A_GATE + 3584, 32, TILES)
        PR = area(A_OT, P)
        LDT = area(A_OT + 128, 2)
        SZ = area(A_X, 4, SEQ)
        X2 = area(A_HT, TB, D)
        XN = area(A_Q, TB, D)
        H2T = area(A_QT, DT, SEQ)
        XB = arena[:, A_GATE:A_GATE + 3072].bitcast(BF16).rearrange("p (s t d) -> p s t d", s=3, t=TB)
        WPG = area(A_TC, DT, D)
        WPP = area(A_X, PLE // P, D)
        XS = area(A_QT, DT, CAP)
        ACTT = area(A_QT + 512, WT, P)
        Y = area(A_QT + 1024, 512)
        WSEL = area(A_QT + 1536, TB, P)
        WSELT = area(A_QT + 1792, TB, P)
        BUP = area(A_V, 2 * F)
        ACTS = area(A_V + 2048, 3, 512)
        PIN = area(A_V + 3584, TB, PLE)
        PLEV = area(A_X, TB, D)
        GPOST = area(A_BT, D)
        PT_IN = area(A_BT + 1024, PLE // P, SEQ)
        BDOWN = area(A_BT + 1536, D)
        XT3 = area(A_Q, DT, SEQ)
        GSIG = area(A_V, TB, D)
        R0 = A_GATE + 3072
        SLOT = arena[:, R0:R0 + SEQ]
        SLOT_I = area(A_V + 2560, SEQ).bitcast(I32)
        LOGIT = area(R0 + 256, TB, E + 8)
        LEFT = area(R0 + 336, TB, E + 8)
        CHOSEN = area(R0 + 416, TB, E)
        GATES = area(R0 + 480, TB, E)
        RANK = area(R0 + 544, TB, E + 1)
        WR = area(R0 + 612, DT, E)
        GT = area(A_V + 2048, TB, P)
        X3_SQ = area(A_GATE, TB, D)
        SELB = arena[:, R0 + 868:R0 + 868 + CAP].bitcast(BF16).rearrange("p (t c) -> p t c", t=TB)
        PICK = arena[:, R0 + 932:R0 + 932 + CAP]
        NPAR = 94
        PAR = small[:, 0:NPAR]
        P_ARE, P_AIM, P_LDT, P_GMIX, P_GFFN, P_GPLE, P_DSKIP, P_BGLU, P_GQ, P_GK = 0, 16, 32, 48, 56, 64, 72, 76, 92, 93
        RHO = small[:, 96:112]
        SSQ = small[:, 112:120]
        RSTD = small[:, 120:128]
        HSQ = small[:, 128:160]
        PARITY = small[:, 160:162]
        TOP8 = small[:, 162:178]
        NTOP = small[:, 178:180]
        SUM = small[:, 180:184]
        CNT = small[:, 184:186]
        BROUT = small[:, 186:218]
        AKC = small[:, 218:234]
        AKS = small[:, 234:250]
        AKT = small[:, 576:576 + 3 * TILES]
        ODD = small[:, 282:283]
        ODD_SCRATCH = small[:, 283:284]
        PSQ = small[:, 288:292]
        PRT = small[:, 286:288]
        TRI = small[:, 320:448]
        ONES = small[:, 448:576]

        full = [sem(f"full{i}") for i in range(NBANKS)]
        free = [sem(f"free{i}") for i in range(NBANKS)]
        arrived = [sem(f"arrived{i}") for i in range(PLACES)]
        names = ("x_in params_in dt_in bc_in ident_set odd_set b_zero x_sq x_ms x_root x_normal dt_rows angle_set "
                 "sine_set turn_set bbar_set tables_set pool_tables_set head_sq head_ms head_ms_all head_root heads_set "
                 "abs_set soft_set sp_set cum_full early_gates_set rot_set back_set gelu_set sz_set mixed_set x_again "
                 "x2_sq x2_ms x2_root x2_normal router_in slots_set logit_top exp_set chosen_set flag_set gates_ready "
                 "down_bias_in cast_set rest_set_0 rest_set_1 up_bias_in gate_in post_in ple_in pp_sq pp_ms pp_root "
                 "gt_full gt_set bd_full bd_add over_done x3_set x3_sq x3_ms x3_root xt3_full xt3_set pg_full "
                 "pg_sig fin_set stored dve_step act_step pool_step").split()
        S = {n: sem(n) for n in names}
        moe_names = ("sel_set wsel_set pick_set wt_full wt_set gx_full xs_set up_g up_u g_set sig_set act_set at_full "
                     "at_set y_full y_set sc_full sc_add dve_step").split()
        M = {n: sem("e_" + n) for n in moe_names}

        W_ORDER = [("in", i) for i in range(8)] + [("attn", 0)] + [("glu", 0), ("glu", 1)] + [("out", 0), ("out", 1)]
        TURN = {k: (i % PLACES, i // PLACES) for i, k in enumerate(W_ORDER)}
        FIRST = len(W_ORDER)
        PER_EXPERT = 6
        EXP_PLACE = [(FIRST + c) % PLACES for c in range(PER_EXPERT)]
        EXP_USES = [(FIRST + c) // PLACES for c in range(PER_EXPERT)]
        LAST_READ = {("in", 3): "u1", ("in", 0): "q1", ("in", 1): "k1", ("in", 2): "v1", ("attn", 0): "a3",
                     ("glu", 0): "glu7", ("glu", 1): "glu7", ("out", 0): "out2", ("out", 1): "out3"}
        LAST_READ.update({("in", 4 + i): f"g{2 * i + 1}" for i in range(4)})
        READ = {c: sem(f"read{c}") for c in (0, 1, 2, 4)}

        def place(i):
            return ring[:, i * PLACE:(i + 1) * PLACE]

        def weight(key, a):
            return place(TURN[key][0]).rearrange("p (a n) -> p a n", a=a)

        def up_source(e, c):
            return w_up[0, e, 2 * P * c:2 * P * (c + 1), :].rearrange("(k p) n -> p k n", p=P)

        def down_source(e, c):
            return w_down[0, e, 4 * P * c:4 * P * (c + 1), :].rearrange("(k p) n -> p k n", p=P)

        def expert_source(e, c):
            if isinstance(e, int):
                return up_source(e, c) if c < 4 else down_source(e, c - 4)
            if c < 4:
                return w_up[0, bass.ds(e, 1), 2 * P * c:2 * P * (c + 1), :].rearrange("o (k p) n -> p (o k) n", p=P)
            c -= 4
            return w_down[0, bass.ds(e, 1), 4 * P * c:4 * P * (c + 1), :].rearrange("o (k p) n -> p (o k) n", p=P)

        PASSES = TB * P // CAP - 1

        def wait_full(eng, job):
            eng.wait_ge(full[BANKS[job][0]], BANKS[job][1] + 1)

        def release(ins, job):
            return ins.then_inc(free[BANKS[job][0]], 1)

        def released(eng, job):
            eng.wait_ge(free[BANKS[job][0]], BANKS[job][1] + 1)

        def ps(job):
            return bank[BANKS[job][0]]

        def pairs(ap, a=2):
            return ap.rearrange("p (a n) -> p a n", a=a)

        LEVELS, DVE_TILES = SEQ.bit_length() - 1, 4

        def turn_tables(eng, st, lo, n, tmp_at, levels=range(LEVELS)):
            def tt(*a):
                return st.link(eng.tensor_tensor(*a))

            tiles = slice(lo, lo + n)
            c_a, s_a = AKC[:, tiles], AKS[:, tiles]
            c_sq, s_sq, c_s = (AKT[:, TILES * i + lo:TILES * i + lo + n] for i in range(3))
            for level in levels:
                k = 1 << level
                if level == 0:
                    st.did(eng.memset(COS[:, tiles, 0:1], 1.0))
                    st.link(eng.memset(SIN[:, tiles, 0:1], 0.0))
                c_k, s_k = spread(c_a, k), spread(s_a, k)
                tmp = area(tmp_at, n * k).rearrange("p (a b) -> p a b", a=n)
                c0, s0, c1, s1 = COS[:, tiles, 0:k], SIN[:, tiles, 0:k], COS[:, tiles, k:2 * k], SIN[:, tiles, k:2 * k]
                st.did(eng.tensor_tensor(tmp, s0, s_k, ALU.mult))
                tt(c1, c0, c_k, ALU.mult)
                st.did(eng.tensor_tensor(s1, s0, c_k, ALU.mult))
                tt(c1, c1, tmp, ALU.subtract)
                tt(tmp, c0, s_k, ALU.mult)
                tt(s1, s1, tmp, ALU.add)
                if level < LEVELS - 1:
                    st.did(eng.tensor_tensor(c_sq, c_a, c_a, ALU.mult))
                    st.did(eng.tensor_tensor(s_sq, s_a, s_a, ALU.mult))
                    tt(c_s, c_a, s_a, ALU.mult)
                    st.did(eng.tensor_tensor(c_a, c_sq, s_sq, ALU.subtract))
                    tt(s_a, c_s, c_s, ALU.add)

        GX, UG, UU, WTB, ATB, YB = 0, 1, 2, 3, 4, 5
        SCATTER = (6, 7, WTB, ATB)
        XT3B, PG = (GX, UG, UU, YB), (6, 7, WTB, ATB)

        block = ctx.enter_context(nc.Block())

        @block.sync
        def _(sp):
            sp.dma_start(X[:, 0, :], x[0, 0:P, :]).then_inc(S["x_in"], 16)
            sp.dma_start(X[:, 1, :], x[0, P:SEQ, :]).then_inc(S["x_in"], 16)
            rows = [(P_ARE, a_re[0].rearrange("(t q) n -> t (q n)", q=2), TILES),
                    (P_AIM, a_im[0].rearrange("(t q) n -> t (q n)", q=2), TILES),
                    (P_GMIX, g_mix[0].rearrange("(k p) -> k p", p=P), DT),
                    (P_GFFN, g_ffn[0].rearrange("(k p) -> k p", p=P), DT),
                    (P_GPLE, g_ple_gate[0].rearrange("(k p) -> k p", p=P), DT),
                    (P_DSKIP, d_skip[0].rearrange("(k p) -> k p", p=P), WT),
                    (P_BGLU, b_glu[0].rearrange("(k p) -> k p", p=P), 2 * DT)]
            rows += [(at, g, 1) for at, g in ((P_GQ, g_q), (P_GK, g_k))]
            sp.dma_start(LDT[32:48, :], log_dt[0].rearrange("(t q) -> t q", q=2)).then_inc(S["dt_in"], 16)
            for at, src, n in rows:
                if src.shape[-1] == P:
                    sp.dma_start(PR[at:at + n, :], src).then_inc(S["params_in"], 16)
                else:
                    for h in range(2):
                        sp.dma_start(PR[at:at + 1, h * DH:(h + 1) * DH], src).then_inc(S["params_in"], 16)

            def source(key):
                name, i = key
                if name == "in":
                    return w_in[0, :, 512 * i:512 * (i + 1)].rearrange("(k p) n -> p k n", p=P)
                if name == "attn":
                    return w_attn[0].rearrange("(k p) n -> p k n", p=P)
                if name == "glu":
                    return w_glu[0, 2 * P * i:2 * P * (i + 1), :].rearrange("(k p) n -> p k n", p=P)
                return w_out[0, :, 512 * i:512 * (i + 1)].rearrange("(k p) n -> p k n", p=P)

            def load(at, src):
                sp.dma_start(place(at).rearrange("p (a n) -> p a n", a=src.shape[1]), src).then_inc(arrived[at], 16)

            held = {}
            for key in W_ORDER:
                at = TURN[key][0]
                if at in held:
                    wait_full(sp, held[at])
                load(at, source(key))
                held[at] = LAST_READ[key]
                if key == ("in", 1):
                    sp.wait_ge(S["b_zero"], 1)
                    for r, src in enumerate((b_re, b_im)):
                        for q in range(2):
                            sp.dma_start(B_RAW[q * N:(q + 1) * N, r, :, q * GC:(q + 1) * GC],
                                         src[0].rearrange("(t q) n c -> q n t c", q=2)[q]).then_inc(S["bc_in"], 16)
                    for r, src in enumerate((c_re, c_im)):
                        sp.dma_start(C_RAW[:, r, :, :],
                                     src[0].rearrange("(b g) c n -> (g c) b n", b=WT)).then_inc(S["bc_in"], 16)
            for c in range(PER_EXPERT):
                wait_full(sp, held[EXP_PLACE[c]])
                load(EXP_PLACE[c], expert_source(0, c))

            def load_expert(n, e):
                for c in range(PER_EXPERT):
                    sp.wait_ge(READ[c] if c in READ else M["up_u" if c == 3 else "y_full"], n)
                    load(EXP_PLACE[c], expert_source(e, c))

            with sp.Fori(1, E) as e:
                load_expert(e, e)
            sp.wait_ge(S["flag_set"], 1)
            crowd = sp.value_load(flag[0:1, 0:1], min_val=0, max_val=SEQ)
            with sp.If(crowd > CAP):
                with sp.Fori(0, E) as e:
                    with sp.Fori(0, PASSES) as j:
                        n = E + e * PASSES + j
                        load_expert(n, e)
            for i in range(2 * TB):
                t, c = divmod(i, 2)
                sp.wait_ge(S["fin_set"], i + 1)
                sp.dma_start(out[0, t * P:(t + 1) * P, 512 * c:512 * (c + 1)],
                             X2[:, t, 512 * c:512 * (c + 1)]).then_inc(S["stored"], 16)
            sp.wait_ge(S["stored"], 32 * TB)

        @block.gpsimd
        def _(pool):
            st = Steps(pool, S["pool_step"])
            for m, v in ((ident[:, :], 0.0), (neg_ones[:, :], -1.0), (neg_tri[:, :], -1.0), (TRI, 1.0), (ONES, 1.0),
                         (hide_b[:, :], 0.0), (ident_b[:, :], 0.0)):
                st.did(pool.memset(m, v))
            st.settle()
            for m in (ident, ident_b):
                st.did(pool.affine_select(out=m[:, :], in_=m[:, :], compare_op=ALU.not_equal, fill=1.0, base=0,
                                          pattern=[[-1, P]], channel_multiplier=1))
            st.did(pool.affine_select(out=neg_tri[:, :], in_=neg_tri[:, :], compare_op=ALU.is_ge, fill=0.0, base=0,
                                      pattern=[[-1, P]], channel_multiplier=1))
            st.did(pool.affine_select(out=TRI, in_=TRI, compare_op=ALU.is_gt, fill=0.0, base=0,
                                      pattern=[[1, P]], channel_multiplier=-1))
            st.did(pool.affine_select(out=hide_b[:, :], in_=hide_b[:, :], compare_op=ALU.is_gt, fill=HIDDEN, base=0,
                                      pattern=[[1, P]], channel_multiplier=-1))
            st.settle()
            pool.sem_inc(S["ident_set"], 1)
            pool.iota(ODD.bitcast(I32), [[0, 1]], base=0, channel_multiplier=1).then_inc(S["odd_set"], 1)
            pool.memset(arena[:, A_GATE:A_GATE + 2 * TILES * 2 * GC], 0.0).then_inc(S["b_zero"], 1)

            pool.wait_ge(S["turn_set"], 1)
            turn_tables(pool, st, DVE_TILES, TILES - DVE_TILES, A_X + DVE_TILES * HALF * 2)
            pool.memset(ODD_SCRATCH, 0.0).then_inc(S["pool_tables_set"], 1)

            released(pool, "o3")
            for i in range(TILES):
                b, j = divmod(i, 4)
                pool.wait_ge(S["rot_set"], i + 1)
                if b and j == 0:
                    wait_full(pool, f"y{b - 1}")
                for s, table in enumerate((COS, SIN)):
                    pool.tensor_tensor(pairs(BACK[:, j, s, :]), pairs(ROT[:, i % 2, 1, :]),
                                       table[:, i:i + 1, :].broadcast_to([P, 2, SEQ]), ALU.mult).then_inc(S["back_set"], 1)
            wait_full(pool, "g7")
            for t in range(TB):
                pool.dma_start(X2[:, t, :], x[0, t * P:(t + 1) * P, :]).then_inc(S["x_again"], 16)
            released(pool, "y3")
            pool.dma_start(BDOWN[0:E, :], b_down[0]).then_inc(S["down_bias_in"], 16)
            pool.dma_start(BUP[0:E, :], b_up[0]).then_inc(S["up_bias_in"], 16)
            pool.dma_start(GPOST, g_ple_post[0:1, :].broadcast_to([P, D])).then_inc(S["post_in"], 16)
            pool.dma_start(WPG, w_ple_gate[0].rearrange("(k p) n -> p k n", p=P)).then_inc(S["gate_in"], 16)
            pool.wait_ge(S["mixed_set"], DT)
            pool.iota(SLOT_I, [[1, SEQ]], base=0, channel_multiplier=0).then_inc(S["slots_set"], 1)
            for i in range(2):
                pool.wait_ge(S["cast_set"], 2 * i + 2)
                pool.tensor_tensor(XN[:, 0, :], XN[:, 0, :], XB[:, i, 0, :], ALU.subtract).then_inc(S["rest_set_0"], 1)

        @block.scalar
        def _(act):
            st = Steps(act, S["act_step"])
            act.wait_ge(S["x_in"], 32)
            for t in range(TB):
                act.activation(X_SQ[:, t, :], X[:, t, :], ACT.Square, accum_out=SSQ[:, t:t + 1]).then_inc(S["x_sq"], 1)
            act.wait_ge(S["x_ms"], 1)
            act.activation(RSTD[:, 0:TB], SSQ[:, 0:TB], ACT.Sqrt).then_inc(S["x_root"], 1)
            for i, job in enumerate(("q0", "q1", "k0", "k1")):
                wait_full(act, job)
                act.activation(SQ[:, i, :], ps(job)[:, :], ACT.Square).then_inc(S["head_sq"], 1)
                release(act.activation((Q, K)[i // 2][:, i % 2, :], ps(job)[:, :], ACT.Copy), job)
                if i == 1:
                    act.wait_ge(S["angle_set"], 1)
                    act.activation(S5[:, 12, :], S5[:, 10, :], ACT.Sin).then_inc(S["sine_set"], 1)
                    act.activation(S5[:, 13, :], S5[:, 10, :], ACT.Sin, scale=0.5).then_inc(S["sine_set"], 1)
            act.wait_ge(S["head_ms_all"], 1)
            act.activation(HSQ, HSQ, ACT.Sqrt).then_inc(S["head_root"], 1)
            for t in range(TB):
                wait_full(act, f"v{t}")
                release(act.activation(V[:, t, :], ps(f"v{t}")[:, :], ACT.Copy), f"v{t}")
            for r in range(2):
                wait_full(act, f"bt{r}")
                release(act.activation(BT[:, r, :, :], pairs(ps(f"bt{r}")[:, :], WT), ACT.Copy),
                        f"bt{r}")
            wait_full(act, "ct0")
            act.activation(CT[:, 0, :, :], pairs(ps("ct0")[:, :], WT), ACT.Copy)
            release(act.activation(CT[:, 1, :, :], pairs(ps("ct0")[:, :], WT), ACT.Copy, scale=-1.0),
                    "ct0")
            wait_full(act, "ct1")
            release(act.activation(CT[:, 2, :, :], pairs(ps("ct1")[:, :], WT), ACT.Copy, scale=-1.0),
                    "ct1")

            def gate(i):
                wait_full(act, f"g{i}")
                release(act.activation(GATE[:, 2 * i:2 * i + 2, :], pairs(ps(f"g{i}")[:, :]), ACT.Sigmoid), f"g{i}")

            for s in range(PAIRS + 2):
                for h in (2 * s, 2 * s + 1) if s < PAIRS else ():
                    act.wait_ge(S["abs_set"], h + 1)
                    st.link(act.activation(SOFT[:, h % 4, :], SOFT[:, h % 4, :], ACT.Exp))
                    act.activation(SOFT[:, h % 4, :], SOFT[:, h % 4, :], ACT.Ln, bias=1.0).then_inc(S["soft_set"], 1)
                for h in (2 * s - 2, 2 * s - 1) if 1 <= s <= PAIRS else ():
                    act.wait_ge(S["cum_full"], h + 1)
                    if h >= 2:
                        wait_full(act, f"o{h // 2 - 1}")
                    release(act.activation(PROB[:, h % 2, :], ps(f"z{h}")[:, 0:384], ACT.Exp),
                            f"z{h}")
                beside = BESIDE_ATTENTION[s]
                wait_full(act, beside)
                i = int(beside[1])
                if beside[0] == "u":
                    release(act.activation(UT[:, 2 * i:2 * i + 2, :], pairs(ps(beside)[:, :]), ACT.Copy), beside)
                elif i < EARLY_GATES:
                    release(act.activation(GATE[:, 2 * i:2 * i + 2, :], pairs(ps(beside)[:, :]), ACT.Copy), beside)
                else:
                    gate(i)
            for i in range(EARLY_GATES):
                released(act, f"g{i}")
            early = GATE[:, 0:2 * EARLY_GATES, :]
            act.activation(early, early, ACT.Sigmoid).then_inc(S["early_gates_set"], 1)
            for i in range(4, DT):
                if i == DT - 1:
                    act.wait_ge(S["tables_set"], 1)
                gate(i)
            for b in range(WT):
                released(act, f"y{b}")
                act.activation(GY[:, b, :], GY[:, b, :], ACT.Gelu_apprx_tanh).then_inc(S["gelu_set"], 1)
            for i in range(DT):
                wait_full(act, f"glu{i}")
                if i >= 4:
                    act.wait_ge(S["mixed_set"], i - 3)
                act.activation(SZ[:, i % 4, :], ps(f"glu{i}")[:, SEQ:2 * SEQ], ACT.Sigmoid,
                               bias=PAR[:, P_BGLU + DT + i:P_BGLU + DT + i + 1]).then_inc(S["sz_set"], 1)

            act.wait_ge(S["mixed_set"], DT)
            act.dma_start(WR, w_router[0].rearrange("(k p) n -> p k n", p=P)).then_inc(S["router_in"], 16)
            act.dma_start(BROUT[0:1, :], b_router).then_inc(S["router_in"], 16)
            act.dma_start(WPP, w_ple_proj[0].rearrange("(k p) n -> p k n", p=P)).then_inc(S["ple_in"], 16)
            act.dma_start(PIN, p[0, 0].rearrange("(t p) n -> p t n", p=P)).then_inc(S["ple_in"], 16)
            for t in range(TB):
                for c in range(2):
                    released(act, f"out{2 * t + c}")
                act.activation(XN[:, t, :], X2[:, t, :], ACT.Square, accum_out=SSQ[:, 2 + t:3 + t]).then_inc(S["x2_sq"], 1)
                act.wait_ge(S["x2_ms"], t + 1)
                act.activation(RSTD[:, 2 + t:3 + t], SSQ[:, 2 + t:3 + t], ACT.Sqrt).then_inc(S["x2_root"], 1)
                if t == 0:
                    wait_full(act, "pt")
                    release(act.activation(PT_IN, pairs(ps("pt")[:, :], PLE // P), ACT.Copy), "pt")

            def embeddings(c):
                for t in range(TB):
                    wait_full(act, f"pp{TB * c + t}")
                for t in range(TB):
                    job = f"pp{TB * c + t}"
                    act.activation(PLEV[:, t, 512 * c:512 * (c + 1)], ps(job)[:, :], ACT.Copy)
                    release(act.activation(ps(job)[:, :], ps(job)[:, :], ACT.Square,
                                           accum_out=PSQ[:, TB * c + t:TB * c + t + 1]), job)

            for i in range(3):
                for t in range(TB):
                    if i == 0:
                        act.wait_ge(S["x2_normal"], t + 1)
                    else:
                        act.wait_ge(S[f"rest_set_{t}"], i)
                    act.activation(XB[:, i, t, :], XN[:, t, :], ACT.Copy).then_inc(S["cast_set"], 1)
                if i == 0:
                    embeddings(0)
            act.wait_ge(S["logit_top"], 1)
            for t in range(TB):
                act.activation(GATES[:, t, :], LOGIT[:, t, 0:E], ACT.Exp, bias=NTOP[:, t:t + 1]).then_inc(S["exp_set"], 1)
            embeddings(1)
            act.wait_ge(S["pp_ms"], 1)
            act.activation(PRT, PSQ[:, 0:TB], ACT.Sqrt).then_inc(S["pp_root"], 1)

            def expert(m, n):
                act.wait_ge(m["g_set"], n + 1)
                act.activation(ACTS[:, 2, :], ACTS[:, 0, :], ACT.Sigmoid, scale=ALPHA).then_inc(m["sig_set"], 1)
                act.wait_ge(m["at_full"], n + 1)
                act.activation(ACTT, pairs(bank[ATB][:, :], WT), ACT.Copy).then_inc(m["at_set"], 1)
                act.wait_ge(m["y_full"], n + 1)
                act.activation(Y, bank[YB][:, :], ACT.Copy).then_inc(m["y_set"], 1)

            with act.Fori(0, E) as e:
                expert(M, e)
            act.wait_ge(S["flag_set"], 1)
            crowd = act.value_load(flag[0:1, 0:1], min_val=0, max_val=SEQ)
            with act.If(crowd > CAP):
                with act.Fori(0, E) as e:
                    with act.Fori(0, PASSES) as j:
                        expert(M, E + e * PASSES + j)
                act.wait_ge(S["over_done"], 1)

            for t in range(TB):
                act.wait_ge(S["x3_set"], t + 1)
                act.activation(X3_SQ[:, t, :], X2[:, t, :], ACT.Square, accum_out=SSQ[:, 4 + t:5 + t]).then_inc(S["x3_sq"], 1)
            act.wait_ge(S["x3_ms"], 1)
            act.activation(RSTD[:, 4:6], SSQ[:, 4:6], ACT.Sqrt).then_inc(S["x3_root"], 1)
            act.wait_ge(S["x3_ms"], 2)
            for i in range(4):
                t, c = divmod(i, 2)
                act.wait_ge(S["pg_full"], i + 1)
                act.activation(GSIG[:, t, 512 * c:512 * (c + 1)], bank[PG[i]][:, :], ACT.Sigmoid,
                               scale=RSTD[:, 4 + t:5 + t]).then_inc(S["pg_sig"], 1)

        @block.vector
        def _(dve):
            st = Steps(dve, S["dve_step"])
            T = lambda i: S5[:, i, :]

            def ts(*a):
                return st.link(dve.tensor_scalar(*a))

            def tt(*a):
                return st.link(dve.tensor_tensor(*a))

            def stt(*a):
                return st.link(dve.scalar_tensor_tensor(*a))

            def mean_plus_eps(ap, n):
                return dve.tensor_scalar(ap, ap, 1.0 / n, EPS, ALU.mult, ALU.add)

            dve.wait_ge(S["dt_in"], 16)
            dve.tensor_copy(PR[32:48, :].rearrange("p (q n) -> p q n", q=2),
                            spread(LDT[32:48, :], N)).then_inc(S["dt_rows"], 1)
            dve.wait_ge(S["x_sq"], TB)
            mean_plus_eps(SSQ[:, 0:TB], D).then_inc(S["x_ms"], 1)
            dve.wait_ge(S["x_root"], 1)
            st.link(dve.reciprocal(RSTD[:, 0:TB], RSTD[:, 0:TB]))
            for t in range(TB):
                dve.tensor_scalar(X[:, t, :], X[:, t, :], RSTD[:, t:t + 1], None, ALU.mult).then_inc(S["x_normal"], 1)
            wait_full(dve, "par")
            release(dve.tensor_copy(PAR, ps("par")[:, 0:NPAR]), "par")
            released(dve, "par")
            for i in range(4):
                t, half = divmod(i, 2)
                wait_full(dve, f"ht{i}")
                release(dve.tensor_tensor(HT[:, 4 * half:4 * half + 4, t * P:(t + 1) * P], pairs(ps(f"ht{i}")[:, :], 4),
                                          spread(PAR[:, P_GMIX + 4 * half:P_GMIX + 4 * half + 4], P), ALU.mult),
                        f"ht{i}")

            def expm1(y, v, z):
                ts(z, v, 1.0 / 2 ** SQUARINGS, None, ALU.mult)
                ts(y, z, 1.0 / TAYLOR, 1.0, ALU.mult, ALU.add)
                for k in range(TAYLOR - 1, 1, -1):
                    stt(y, y, 1.0 / k, z, ALU.mult, ALU.mult)
                    ts(y, y, 1.0, None, ALU.add)
                tt(y, y, z, ALU.mult)
                for _ in range(SQUARINGS):
                    stt(y, y, 2.0, y, ALU.add, ALU.mult)

            LR, LI = PAR[:, P_ARE:P_ARE + TILES], PAR[:, P_AIM:P_AIM + TILES]
            expm1(T(0), PAR[:, P_LDT:P_LDT + TILES], T(1))
            ts(T(0), T(0), 1.0, None, ALU.add)
            tt(T(2), LR, T(0), ALU.mult)
            tt(T(3), LI, T(0), ALU.mult)
            expm1(T(4), T(2), T(1))
            ts(RHO, T(4), 1.0, None, ALU.add)
            ts(T(5), T(3), 1.0 / TWO_PI, None, ALU.mult)
            ts(T(5), T(5), ROUNDER, None, ALU.add)
            ts(T(5), T(5), -ROUNDER, None, ALU.add)
            stt(T(10), T(5), -TWO_PI_HI, T(3), ALU.mult, ALU.add)
            stt(T(10), T(5), -TWO_PI_MID, T(10), ALU.mult, ALU.add)
            stt(T(10), T(5), -TWO_PI_LO, T(10), ALU.mult, ALU.add)
            dve.tensor_scalar(T(10), T(10), PI_F32, -PI_F32, ALU.min, ALU.max).then_inc(S["angle_set"], 1)
            dve.wait_ge(S["sine_set"], 2)
            stt(T(14), T(13), -2.0, T(13), ALU.mult, ALU.mult)
            ts(AKC, T(14), 1.0, None, ALU.add)
            st.link(dve.tensor_copy(AKS, T(12)))
            dve.tensor_tensor(T(6), T(4), AKC, ALU.mult).then_inc(S["turn_set"], 1)
            dve.wait_ge(S["turn_set"], 1)
            tt(T(6), T(6), T(14), ALU.add)
            tt(T(7), RHO, T(12), ALU.mult)
            tt(T(8), LR, LR, ALU.mult)
            tt(T(9), LI, LI, ALU.mult)
            tt(T(8), T(8), T(9), ALU.add)
            st.link(dve.reciprocal(T(8), T(8)))
            tt(T(16), T(6), LR, ALU.mult)
            tt(T(17), T(7), LI, ALU.mult)
            tt(T(16), T(16), T(17), ALU.add)
            tt(T(16), T(16), T(8), ALU.mult)
            tt(T(18), T(7), LR, ALU.mult)
            tt(T(19), T(6), LI, ALU.mult)
            tt(T(18), T(18), T(19), ALU.subtract)
            tt(T(18), T(18), T(8), ALU.mult)
            dve.wait_ge(S["bc_in"], 16 * 6)
            fr, fi = spread(T(16), 2 * GC), spread(T(18), 2 * GC)
            scratch = area(A_X, TILES, 2 * GC)
            for r, (f0, f1, op) in enumerate(((fr, fi, ALU.subtract), (fi, fr, ALU.add))):
                released(dve, "ht3")
                st.did(dve.tensor_tensor(B_BAR[:, r, :, :], B_RAW[:, 0, :, :], f0, ALU.mult))
                tt(scratch, B_RAW[:, 1, :, :], f1, ALU.mult)
                tt(B_BAR[:, r, :, :], B_BAR[:, r, :, :], scratch, op)
            dve.wait_ge(S["odd_set"], 1)
            odd = ODD.bitcast(I32)
            ts(odd, odd, 4, 1, ALU.logical_shift_right, ALU.bitwise_and)
            st.link(dve.tensor_copy(PARITY[:, 1:2], odd))
            ts(PARITY[:, 0:1], PARITY[:, 1:2], -1.0, 1.0, ALU.mult, ALU.add)
            for r in range(2):
                for q in range(2):
                    st.did(dve.tensor_scalar(C_MASK[:, r, :, q * N:(q + 1) * N], C_RAW[:, r, :, :],
                                             PARITY[:, q:q + 1], None, ALU.mult))
            st.settle()
            dve.memset(SUM[:, 0:1], 0.0).then_inc(S["bbar_set"], 1)

            dve.wait_ge(S["head_sq"], 4)
            dve.tensor_reduce(HSQ, SQ.rearrange("p i (h d) -> p (i h) d", h=H), AX, ALU.add).then_inc(S["head_ms"], 1)
            dve.wait_ge(S["head_ms"], 1)
            mean_plus_eps(HSQ, DH).then_inc(S["head_ms_all"], 1)
            dve.wait_ge(S["head_root"], 1)
            st.link(dve.reciprocal(HSQ, HSQ))
            for i in range(4):
                v = (Q, K)[i // 2][:, i % 2, :].rearrange("p (h d) -> p h d", h=H)
                released(dve, f"{'qk'[i // 2]}{i % 2}")
                dve.tensor_tensor(v, v, spread(HSQ[:, H * i:H * (i + 1)], DH), ALU.mult).then_inc(S["heads_set"], 1)
            turn_tables(dve, st, 0, DVE_TILES, A_X, range(5))
            for i in range(4):
                job = f"{'qk'[i // 2]}t{i % 2}"
                wait_full(dve, job)
                dst, col, scale = ((QT, P_GQ, DH ** -0.5), (KT, P_GK, 1.0))[i // 2]
                t = i % 2
                release(dve.tensor_scalar(dst[:, :, t * P:(t + 1) * P], pairs(ps(job)[:, :], PAIRS), PAR[:, col:col + 1],
                                          scale, ALU.mult, ALU.mult), job)

            TABLES_BESIDE = ((), (), (), (), (5, 6), (7,))
            for s in range(PAIRS + 2):
                for h in (2 * s, 2 * s + 1) if s < PAIRS else ():
                    wait_full(dve, f"z{h}")
                    if h >= 4:
                        dve.wait_ge(S["cum_full"], h - 3)
                    ts(SOFT[:, h % 4, :], ps(f"z{h}")[:, 0:384], 0.0, -2.0, ALU.max, ALU.mult)
                    dve.tensor_tensor(SOFT[:, h % 4, :], SOFT[:, h % 4, :], ps(f"z{h}")[:, 0:384],
                                      ALU.add).then_inc(S["abs_set"], 1)
                for h in (2 * s, 2 * s + 1) if s < PAIRS else ():
                    dve.wait_ge(S["soft_set"], h + 1)
                    dve.scalar_tensor_tensor(SOFT[:, h % 4, :], ps(f"z{h}")[:, 0:384], 0.0, SOFT[:, h % 4, :],
                                             ALU.max, ALU.add).then_inc(S["sp_set"], 1)
                if s >= 2:
                    job = f"o{s - 2}"
                    wait_full(dve, job)
                    release(dve.tensor_copy(OT[:, s - 2, :], ps(job)[:, 0:SEQ]), job)
                turn_tables(dve, st, 0, DVE_TILES, A_X, TABLES_BESIDE[s])

            st.settle()
            dve.memset(SUM[:, 0:1], 0.0).then_inc(S["tables_set"], 1)

            def y_out(b):
                wait_full(dve, f"y{b}")
                release(dve.scalar_tensor_tensor(GY[:, b, :], UT[:, b, :], PAR[:, P_DSKIP + b:P_DSKIP + b + 1],
                                                 ps(f"y{b}")[:, 0:SEQ], ALU.mult, ALU.add), f"y{b}")

            def mix_attention():
                for i in range(4):
                    wait_full(dve, f"a{i}")
                    released(dve, f"g{i}")
                    release(dve.tensor_tensor(GATE[:, 2 * i:2 * i + 2, :], GATE[:, 2 * i:2 * i + 2, :],
                                              pairs(ps(f"a{i}")[:, :]), ALU.mult), f"a{i}")

            dve.wait_ge(S["pool_tables_set"], 1)
            for i in range(TILES):
                b, j = divmod(i, 4)
                job = f"x{i}"
                m1, m2 = ROT[:, i % 2, 0, :], ROT[:, i % 2, 1, :]
                wait_full(dve, job)
                if i >= 2:
                    dve.wait_ge(S["back_set"], 2 * (i - 1))
                st.did(dve.tensor_tensor(pairs(m1), pairs(ps(job)[:, :]), COS[:, i:i + 1, :].broadcast_to([P, 2, SEQ]), ALU.mult))
                release(dve.tensor_tensor(pairs(m2), pairs(ps(job)[:, :]), SIN[:, i:i + 1, :].broadcast_to([P, 2, SEQ]),
                                          ALU.mult), job)
                released(dve, job)
                st.did(dve.tensor_tensor(m1[:, 0:SEQ], m1[:, 0:SEQ], m2[:, SEQ:], ALU.add))
                tt(m1[:, SEQ:], m1[:, SEQ:], m2[:, 0:SEQ], ALU.subtract)
                decay = RHO[:, i:i + 1].broadcast_to([P, SEQ])
                dve.tensor_tensor_scan(m2[:, 0:SEQ], decay, m1[:, 0:SEQ], 0.0, ALU.mult, ALU.add)
                dve.tensor_tensor_scan(m2[:, SEQ:], decay, m1[:, SEQ:], 0.0, ALU.mult, ALU.add).then_inc(S["rot_set"], 1)
                if j == 3 and b:
                    y_out(b - 1)
            y_out(3)
            dve.wait_ge(S["early_gates_set"], 1)
            mix_attention()

            released(dve, "a3")
            released(dve, "g7")
            for i in range(DT):
                job = f"glu{i}"
                z = SZ[:, i % 4, :]
                dve.wait_ge(S["sz_set"], i + 1)
                release(dve.scalar_tensor_tensor(z, ps(job)[:, 0:SEQ], PAR[:, P_BGLU + i:P_BGLU + i + 1], z,
                                                 ALU.add, ALU.mult), job)
                released(dve, job)
                tt(z, z, GATE[:, DT + i, :], ALU.mult)
                dve.tensor_tensor(GATE[:, i, :], GATE[:, i, :], z, ALU.add).then_inc(S["mixed_set"], 1)
            dve.wait_ge(S["x_again"], 16 * TB)
            for t in range(TB):
                for c in range(2):
                    job = f"out{2 * t + c}"
                    wait_full(dve, job)
                    part = X2[:, t, 512 * c:512 * (c + 1)]
                    release(dve.tensor_tensor(part, part, ps(job)[:, :], ALU.add), job)
                dve.wait_ge(S["x2_sq"], t + 1)
                mean_plus_eps(SSQ[:, 2 + t:3 + t], D).then_inc(S["x2_ms"], 1)
                dve.wait_ge(S["x2_root"], t + 1)
                st.link(dve.reciprocal(RSTD[:, 2 + t:3 + t], RSTD[:, 2 + t:3 + t]))
                dve.tensor_scalar(XN[:, t, :], X2[:, t, :], RSTD[:, 2 + t:3 + t], None, ALU.mult).then_inc(S["x2_normal"], 1)
                for half in range(2):
                    job = f"xt{2 * t + half}"
                    wait_full(dve, job)
                    release(dve.tensor_tensor(H2T[:, 4 * half:4 * half + 4, t * P:(t + 1) * P], pairs(ps(job)[:, :], 4),
                                              spread(PAR[:, P_GFFN + 4 * half:P_GFFN + 4 * half + 4], P), ALU.mult), job)

            def rest(i):
                dve.wait_ge(S["cast_set"], 2 * i + 2)
                dve.tensor_tensor(XN[:, 1, :], XN[:, 1, :], XB[:, i, 1, :], ALU.subtract).then_inc(S["rest_set_1"], 1)

            rest(0)

            dve.wait_ge(S["mixed_set"], DT)
            dve.wait_ge(S["slots_set"], 1)
            st.link(dve.tensor_copy(SLOT, SLOT_I))
            st.did(dve.memset(LOGIT[:, :, E:], NEVER))
            st.did(dve.memset(TOP8, NEVER))
            st.did(dve.memset(RANK[:, :, E:E + 1], -1.0))
            st.settle()
            wait_full(dve, "lg")
            release(dve.tensor_copy(LOGIT[:, :, 0:E], ps("lg")[:, 0:TB * E].rearrange("p (t e) -> p t e", t=TB)), "lg")
            released(dve, "lg")
            for t in range(TB):
                st.did(dve.max(TOP8[:, 8 * t:8 * t + 8], LOGIT[:, t, 0:E]))
            st.settle()
            for t in range(TB):
                st.did(dve.tensor_scalar(NTOP[:, t:t + 1], TOP8[:, 8 * t:8 * t + 1], -1.0, None, ALU.mult))
            st.settle()
            dve.memset(TOP8.rearrange("p (t k) -> p t k", t=TB)[:, :, 4:8], NEVER).then_inc(S["logit_top"], 1)
            dve.wait_ge(S["logit_top"], 1)
            for t in range(TB):
                st.did(dve.match_replace(LEFT[:, t, :], TOP8[:, 8 * t:8 * t + 8], LOGIT[:, t, :], TAKEN))
            st.settle()
            dve.tensor_tensor(CHOSEN, LEFT[:, :, 0:E], LOGIT[:, :, 0:E], ALU.not_equal).then_inc(S["chosen_set"], 1)
            rest(1)
            wait_full(dve, "rk")
            st.did(dve.scalar_tensor_tensor(RANK[:, :, 0:E], ps("rk")[:, 0:TB * E].rearrange("p (t e) -> p t e", t=TB), 1.0,
                                            CHOSEN, ALU.add, ALU.mult))
            release(dve.tensor_reduce(CNT[0:1, 0:1], ps("rk")[0:1, TB * E:TB * E + E], AX, ALU.max), "rk")
            released(dve, "rk")
            dve.tensor_copy(flag[0:1, 0:1], CNT[0:1, 0:1]).then_inc(S["flag_set"], 1)
            st.link(dve.tensor_scalar(RANK[:, :, 0:E], RANK[:, :, 0:E], -1.0, None, ALU.add))

            def at(e):
                return slice(e, e + 1) if isinstance(e, int) else bass.ds(e, 1)

            def select(m, e, slots):
                for t in range(TB):
                    last = dve.tensor_scalar(SELB[:, t, :], slots, RANK[:, t, at(e)], None, ALU.is_equal)
                last.then_inc(m["sel_set"], 1)

            def select_weighted(m, e, slots):
                for t in range(TB):
                    last = dve.tensor_scalar(pairs(WSEL[:, t, :]), slots.unsqueeze(1).broadcast_to([P, 2, CAP]),
                                             RANK[:, t, at(e)], GATES[:, t, at(e)], ALU.is_equal, ALU.mult)
                last.then_inc(m["wsel_set"], 1)

            def pick(m, e):
                dve.tensor_copy(PICK[0:E, :], ident[0:E, at(e)].broadcast_to([E, CAP])).then_inc(m["pick_set"], 1)

            def gathered(m, n):
                dve.wait_ge(m["gx_full"], n + 1)
                dve.tensor_tensor(XS, pairs(bank[GX][:, :], DT), spread(PAR[:, P_GFFN:P_GFFN + DT], CAP),
                                  ALU.mult).then_inc(m["xs_set"], 1)

            def activate(m, n):
                dve.wait_ge(m["up_g"], n + 1)
                dve.tensor_scalar(ACTS[:, 0, :], bank[UG][:, :], LIMIT, None, ALU.min).then_inc(m["g_set"], 1)
                dve.wait_ge(m["up_u"], n + 1)
                dve.tensor_scalar(ACTS[:, 1, :], bank[UU][:, :], LIMIT, -LIMIT, ALU.min, ALU.max).then_inc(m["dve_step"], 1)
                dve.wait_ge(m["dve_step"], n * 2 + 1)
                dve.scalar_tensor_tensor(ACTS[:, 1, :], ACTS[:, 1, :], 1.0, ACTS[:, 0, :], ALU.add,
                                         ALU.mult).then_inc(m["dve_step"], 1)
                dve.wait_ge(m["dve_step"], n * 2 + 2)
                dve.wait_ge(m["sig_set"], n + 1)
                dve.tensor_tensor(ACTS[:, 1, :], ACTS[:, 1, :], ACTS[:, 2, :], ALU.mult).then_inc(m["act_set"], 1)

            def weights_back(m, n):
                dve.wait_ge(m["wt_full"], n + 1)
                dve.tensor_copy(WSELT, bank[WTB][:, 0:SEQ].rearrange("p (t n) -> p t n", t=TB)).then_inc(m["wt_set"], 1)

            def add_up(m, n, last=False):
                for q in range(4):
                    t, c = divmod(q, 2)
                    dve.wait_ge(m["sc_full"], n * 4 + q + 1)
                    part = X2[:, t, 512 * c:512 * (c + 1)]
                    dve.tensor_tensor(part, part, bank[SCATTER[q]][:, :], ALU.add).then_inc(m["sc_add"], 1)
                    if last and c == 1:
                        dve.wait_ge(m["sc_add"], n * 4 + q + 1)
                        dve.memset(SUM[:, 0:1], 0.0).then_inc(S["x3_set"], 1)

            def expert(m, n, last=False):
                select(m, n + 1, SLOT[:, 0:CAP])
                select_weighted(m, n, SLOT[:, 0:CAP])
                activate(m, n)
                gathered(m, n + 1)
                weights_back(m, n)
                pick(m, n + 1)
                add_up(m, n, last)

            select(M, 0, SLOT[:, 0:CAP])
            pick(M, 0)
            dve.wait_ge(S["exp_set"], TB)
            dve.wait_ge(S["chosen_set"], 1)
            tt(GATES, GATES, CHOSEN, ALU.mult)
            st.link(dve.tensor_reduce(SUM[:, 0:TB], GATES, AX, ALU.add))
            st.link(dve.reciprocal(SUM[:, 0:TB], SUM[:, 0:TB]))
            dve.tensor_tensor(GATES, GATES, spread(SUM[:, 0:TB], E), ALU.mult).then_inc(S["gates_ready"], 1)
            gathered(M, 0)
            dve.wait_ge(S["gt_full"], 1)
            dve.tensor_copy(GT[0:E, :, :], bank[ATB][0:E, 0:SEQ].rearrange("p (t n) -> p t n", t=TB)).then_inc(S["gt_set"], 1)
            for c in range(2):
                for t in range(TB):
                    released(dve, f"pp{TB * c + t}")
            dve.wait_ge(S["gates_ready"], 1)
            tt(PSQ[:, 0:TB], PSQ[:, 0:TB], PSQ[:, TB:2 * TB], ALU.add)
            mean_plus_eps(PSQ[:, 0:TB], D).then_inc(S["pp_ms"], 1)
            dve.wait_ge(S["pp_root"], 1)
            st.link(dve.reciprocal(PRT, PRT))
            dve.wait_ge(S["post_in"], 16)
            for t in range(TB):
                st.did(dve.scalar_tensor_tensor(PLEV[:, t, :], PLEV[:, t, :], PRT[:, t:t + 1], GPOST, ALU.mult, ALU.mult))
            st.settle()
            for i in range(4):
                t, c = divmod(i, 2)
                dve.wait_ge(S["bd_full"], i + 1)
                part = X2[:, t, 512 * c:512 * (c + 1)]
                dve.tensor_tensor(part, part, bank[SCATTER[i]][:, :], ALU.add).then_inc(S["bd_add"], 1)
            with dve.Fori(0, E - 1) as e:
                expert(M, e)
            expert(M, E - 1, True)
            dve.wait_ge(S["flag_set"], 1)
            crowd = dve.value_load(flag[0:1, 0:1], min_val=0, max_val=SEQ)
            with dve.If(crowd > CAP):
                dve.wait_ge(M["pick_set"], E + 1)
                dve.wait_ge(M["sc_add"], 4 * E)
                with dve.Fori(0, E) as e:
                    with dve.Fori(0, PASSES) as j:
                        n = E + e * PASSES + j
                        slots = SLOT[:, bass.ds(j * CAP + CAP, CAP)]
                        select(M, e, slots)
                        select_weighted(M, e, slots)
                        pick(M, e)
                        gathered(M, n + 1)
                        activate(M, n)
                        weights_back(M, n)
                        add_up(M, n)

                dve.memset(SUM[:, 0:1], 0.0).then_inc(S["over_done"], 1)

            for i in range(4):
                t, half = divmod(i, 2)
                dve.wait_ge(S["xt3_full"], i + 1)
                dve.tensor_tensor(XT3[:, 4 * half:4 * half + 4, t * P:(t + 1) * P], pairs(bank[XT3B[i]][:, :], 4),
                                  spread(PAR[:, P_GPLE + 4 * half:P_GPLE + 4 * half + 4], P), ALU.mult).then_inc(S["xt3_set"], 1)
            dve.wait_ge(S["x3_sq"], TB)
            mean_plus_eps(SSQ[:, 4:6], D).then_inc(S["x3_ms"], 1)
            dve.wait_ge(S["x3_root"], 1)
            dve.reciprocal(RSTD[:, 4:6], RSTD[:, 4:6]).then_inc(S["x3_ms"], 1)
            for i in range(4):
                t, c = divmod(i, 2)
                cols = slice(512 * c, 512 * (c + 1))
                dve.wait_ge(S["pg_sig"], i + 1)
                tt(GSIG[:, t, cols], GSIG[:, t, cols], PLEV[:, t, cols], ALU.mult)
                dve.tensor_tensor(X2[:, t, cols], X2[:, t, cols], GSIG[:, t, cols], ALU.add).then_inc(S["fin_set"], 1)

        @block.tensor
        def _(pe):
            I = ident[:, :]

            def take(job):
                at, use = BANKS[job]
                if use:
                    pe.wait_ge(free[at], use)
                return bank[at]

            def done(ins, job):
                return ins.then_inc(full[BANKS[job][0]], 1)

            def arrive(key):
                at, use = TURN[key]
                pe.wait_ge(arrived[at], 16 * (use + 1))

            pe.wait_ge(S["ident_set"], 1)
            pe.wait_ge(S["params_in"], 16 * 11)
            pe.wait_ge(S["dt_rows"], 1)
            done(pe.transpose(take("par")[:, 0:NPAR], PR[0:NPAR, :], I[0:NPAR, 0:NPAR]), "par")
            for i in range(4):
                t, half = divmod(i, 2)
                b = take(f"ht{i}")
                pe.wait_ge(S["x_normal"], t + 1)
                for k in range(4):
                    last = pe.transpose(b[:, P * k:P * (k + 1)], X[:, t, P * (4 * half + k):P * (4 * half + k + 1)], I)
                done(last, f"ht{i}")

            def columns(job, key, a, parts, rhs, n=DT):
                b = take(job)
                for i, m in enumerate(parts):
                    for k in range(n):
                        last = pe.matmul(b[:, SEQ * i:SEQ * (i + 1)], weight(key, a)[:, k, P * m:P * (m + 1)], rhs[:, k, :],
                                         start=(k == 0), stop=(k == n - 1))
                return done(last, job)

            released(pe, "ht3")
            for n, name in enumerate("qkv"):
                arrive(("in", n))
                for t in range(TB):
                    b = take(f"{name}{t}")
                    for k in range(DT):
                        last = pe.matmul(b[:, :], HT[:, k, t * P:(t + 1) * P], weight(("in", n), DT)[:, k, :],
                                         start=(k == 0), stop=(k == DT - 1))
                    done(last, f"{name}{t}")

            def projected(job):
                i = int(job[1])
                n = 3 if job[0] == "u" else 4 + i // 2
                arrive(("in", n))
                columns(job, ("in", n), DT, (2 * (i % 2), 2 * (i % 2) + 1), HT)

            pe.wait_ge(S["bbar_set"], 1)
            for r in range(2):
                b = take(f"bt{r}")
                flat = B_BAR[:, r, :, :].rearrange("p t c -> p (t c)")
                for k in range(WT):
                    last = pe.transpose(b[:, P * k:P * (k + 1)], flat[:, P * k:P * (k + 1)], I)
                done(last, f"bt{r}")
            for r in range(2):
                b = take(f"ct{r}")
                for k in range(WT):
                    last = pe.transpose(b[:, P * k:P * (k + 1)], C_MASK[:, r, k, :], I)
                done(last, f"ct{r}")
            for i in range(4):
                job = f"{'qk'[i // 2]}t{i % 2}"
                b = take(job)
                pe.wait_ge(S["heads_set"], i + 1)
                for k in range(PAIRS):
                    last = pe.transpose(b[:, P * k:P * (k + 1)], (Q, K)[i // 2][:, i % 2, P * k:P * (k + 1)], I)
                done(last, job)

            def s5_in(blk):
                bs = [take(f"x{4 * blk + j}") for j in range(4)]
                for r in range(2):
                    for j in range(4):
                        rows = slice(32 * j, 32 * j + 32)
                        last = pe.matmul(bs[j][:, SEQ * r:SEQ * (r + 1)], BT[rows, r, blk, :], UT[rows, blk, :],
                                         start=True, stop=True)
                        if r == 1:
                            done(last, f"x{4 * blk + j}")

            def s5_out(blk):
                b = take(f"y{blk}")
                pe.wait_ge(S["back_set"], 8 * (blk + 1))
                for k, (c, s, r) in enumerate(((0, 0, 0), (1, 1, 1), (2, 1, 0), (2, 0, 1))):
                    for j in range(4):
                        last = pe.matmul(b[32 * j:32 * j + 32, 0:SEQ], CT[:, c, blk, 32 * j:32 * j + 32],
                                         BACK[:, j, s, SEQ * r:SEQ * (r + 1)], start=(k == 0), stop=(k == 3))
                done(last, f"y{blk}")

            released(pe, "kt1")
            for s in range(PAIRS + 2):
                if s < PAIRS:
                    zs = [take(f"z{2 * s + q}") for q in range(2)]
                    for k, (lo, n) in enumerate(((0, SEQ), (P, P))):
                        for q in range(2):
                            rows = slice(DH * q, DH * (q + 1))
                            pe.matmul(zs[q][:, SEQ * k:SEQ * k + n], KT[rows, s, P * k:P * (k + 1)], QT[rows, s, lo:lo + n],
                                      start=(k == 0), stop=False, skip_group_check=True)
                    for q in range(2):
                        for k in range(2):
                            last = pe.matmul(zs[q][:, SEQ * k:SEQ * k + P], ident_b[:, :], hide_b[:, :],
                                             start=False, stop=True, skip_group_check=True)
                        done(last, f"z{2 * s + q}")
                if 1 <= s <= PAIRS:
                    for h in (2 * s - 2, 2 * s - 1):
                        b, sp = ps(f"z{h}"), SOFT[:, h % 4, :]
                        pe.wait_ge(S["sp_set"], h + 1)
                        pe.matmul(b[:, 0:SEQ], neg_tri[:, :], sp[:, 0:SEQ], start=False, stop=True, skip_group_check=True)
                        pe.matmul(b[:, P:SEQ], neg_ones[:, :], sp[:, SEQ:], start=False, stop=True, skip_group_check=True)
                        pe.matmul(b[:, SEQ:SEQ + P], neg_tri[:, :], sp[:, SEQ:], start=False, stop=True,
                                  skip_group_check=True).then_inc(S["cum_full"], 1)
                if s >= 2:
                    b = take(f"o{s - 2}")
                    for k in range(2):
                        for q in range(2):
                            h = 2 * (s - 2) + q
                            released(pe, f"z{h}")
                            last = pe.matmul(b[DH * q:DH * (q + 1), P * k:SEQ], V[:, k, DH * h:DH * (h + 1)],
                                             PROB[:, q, SEQ * k:SEQ * (k + 1) - P * k],
                                             start=(k == 0), stop=(k == 1))
                    done(last, f"o{s - 2}")
                if s == PAIRS + 1:
                    released(pe, "ct1")
                    released(pe, "u1")
                    s5_in(0)
                projected(BESIDE_ATTENTION[s])

            def branch(i):
                columns(f"a{i}", ("attn", 0), WT, (2 * i, 2 * i + 1), OT, WT)

            for blk in range(WT):
                if blk < WT - 1:
                    s5_in(blk + 1)
                projected(f"g{4 + blk}")
                if blk == WT - 1:
                    released(pe, "o3")
                    arrive(("attn", 0))
                    for i in range(2):
                        branch(i)
                s5_out(blk)
            for i in range(2, 4):
                branch(i)
            pe.wait_ge(S["gelu_set"], WT)
            arrive(("glu", 0))
            arrive(("glu", 1))
            for i in range(DT):
                b = take(f"glu{i}")
                for h in range(2):
                    m = i + DT * h
                    for k in range(WT):
                        last = pe.matmul(b[:, SEQ * h:SEQ * (h + 1)], weight(("glu", k // 2), 2)[:, k % 2, P * m:P * (m + 1)],
                                         GY[:, k, :], start=(k == 0), stop=(k == WT - 1))
                done(last, f"glu{i}")
            def output(i):
                t, c = divmod(i, 2)
                b = take(f"out{i}")
                arrive(("out", c))
                for k in range(DT):
                    last = pe.matmul(b[:, :], GATE[:, k, t * P:(t + 1) * P], weight(("out", c), DT)[:, k, :],
                                     start=(k == 0), stop=(k == DT - 1))
                done(last, f"out{i}")

            def transposed(t):
                for half in range(2):
                    job = f"xt{2 * t + half}"
                    b = take(job)
                    pe.wait_ge(S["x2_normal"], t + 1)
                    for k in range(4):
                        last = pe.transpose(b[:, P * k:P * (k + 1)], XN[:, t, P * (4 * half + k):P * (4 * half + k + 1)], I)
                    done(last, job)

            def embeddings(i):
                c, t = divmod(i, 2)
                b = take(f"pp{i}")
                for k in range(PLE // P):
                    last = pe.matmul(b[:, :], PT_IN[:, k, P * t:P * (t + 1)], WPP[:, k, 512 * c:512 * (c + 1)],
                                     start=(k == 0), stop=(k == PLE // P - 1))
                done(last, f"pp{i}")

            pe.wait_ge(S["mixed_set"], DT)
            output(0)
            output(1)
            output(2)
            transposed(0)
            b = take("pt")
            pe.wait_ge(S["ple_in"], 32)
            for k in range(PLE // P):
                for t in range(TB):
                    last = pe.transpose(b[:, SEQ * k + P * t:SEQ * k + P * (t + 1)], PIN[:, t, P * k:P * (k + 1)], I)
            done(last, "pt")
            output(3)
            released(pe, "pt")
            embeddings(0)
            embeddings(1)
            transposed(1)
            b = take("lg")
            pe.wait_ge(S["router_in"], 32)
            for t in range(TB):
                released(pe, f"xt{2 * t + 1}")
                o = b[:, E * t:E * (t + 1)]
                pe.matmul(o, ONES[0:1, :], BROUT[0:1, :], start=True, stop=False)
                for k in range(DT):
                    last = pe.matmul(o, H2T[:, k, t * P:(t + 1) * P], WR[:, k, :], start=False, stop=(k == DT - 1))
            done(last, "lg")
            embeddings(2)
            b = take("rk")
            pe.wait_ge(S["chosen_set"], 1)
            pe.matmul(b[:, 0:E], TRI, CHOSEN[:, 0, :], start=True, stop=True)
            pe.matmul(b[:, E:2 * E], ONES, CHOSEN[:, 0, :], start=True, stop=False)
            pe.matmul(b[:, E:2 * E], TRI, CHOSEN[:, 1, :], start=False, stop=True)
            for t in range(TB):
                last = pe.matmul(b[0:1, 2 * E:3 * E], ONES[:, 0:1], CHOSEN[:, t, :], start=(t == 0), stop=(t == 1))
            done(last, "rk")
            embeddings(3)

            def gather(m, n):
                pe.wait_ge(m["sel_set"], n + 1)
                for d in range(DT):
                    for i in range(3 * TB):
                        part, t = divmod(i, TB)
                        last = pe.matmul(bank[GX][:, CAP * d:CAP * (d + 1)], XB[:, part, t, P * d:P * (d + 1)], SELB[:, t, :],
                                         start=(i == 0), stop=(i == 3 * TB - 1))
                last.then_inc(m["gx_full"], 1)

            def chunk(c):
                return place(EXP_PLACE[c]).rearrange("p (a n) -> p a n", a=2 if c < 4 else 4)

            def up(m, n, wait_chunk, leave_chunk):
                pe.wait_ge(m["xs_set"], n + 1)
                pe.wait_ge(m["pick_set"], n + 1)
                for w in range(2):
                    for h in range(2):
                        pe.matmul(bank[UG + w][HALF * h:HALF * (h + 1), :], PICK[0:E, :],
                                  BUP[0:E, 512 * (2 * w + h):512 * (2 * w + h + 1)], start=True, stop=False)
                for c in range(4):
                    wait_chunk(c)
                    for k in (2 * c, 2 * c + 1):
                        for w in range(2):
                            for h in range(2):
                                last = pe.matmul(bank[UG + w][HALF * h:HALF * (h + 1), :], XS[:, k, :],
                                                 chunk(c)[:, k % 2, 512 * (2 * w + h):512 * (2 * w + h + 1)],
                                                 start=False, stop=(k == DT - 1))
                            if k == DT - 1:
                                last.then_inc(m[("up_g", "up_u")[w]], 1)
                    leave_chunk(last, c)

            def down(m, n, wait_chunk, leave_chunk):
                pe.wait_ge(m["wsel_set"], n + 1)
                for t in range(TB):
                    last = pe.transpose(bank[WTB][:, P * t:P * (t + 1)], WSEL[:, t, :], I)
                last.then_inc(m["wt_full"], 1)
                pe.wait_ge(m["act_set"], n + 1)
                for j in range(4):
                    last = pe.transpose(bank[ATB][:, P * j:P * (j + 1)], ACTS[:, 1, P * j:P * (j + 1)], I)
                last.then_inc(m["at_full"], 1)
                pe.wait_ge(m["at_set"], n + 1)
                for h in range(2):
                    wait_chunk(4 + h)
                    for j in range(4):
                        for c in range(2):
                            last = pe.matmul(bank[YB][HALF * c:HALF * (c + 1), :], ACTT[:, j, HALF * h:HALF * (h + 1)],
                                             chunk(4 + h)[:, j, 512 * c:512 * (c + 1)],
                                             start=(h == 0 and j == 0), stop=(h == 1 and j == 3))
                    if h == 1:
                        last.then_inc(m["y_full"], 1)
                    leave_chunk(last, 4 + h)
                pe.wait_ge(m["wt_set"], n + 1)
                pe.wait_ge(m["y_set"], n + 1)
                for q in range(4):
                    t, c = divmod(q, 2)
                    rows = slice(HALF * c, HALF * (c + 1))
                    pe.matmul(bank[SCATTER[q]][:, :], WSELT[rows, t, :], Y[rows, :], start=True,
                              stop=True).then_inc(m["sc_full"], 1)

            def main_wait(n):
                return lambda c: pe.wait_ge(arrived[EXP_PLACE[c]], n * 16 + 16 * (EXP_USES[c] + 1))

            def main_leave(last, c):
                if c in READ:
                    last.then_inc(READ[c], 1)

            def vacant(*banks):
                for i in banks:
                    pe.wait_ge(free[i], sum(1 for at, _ in BANKS.values() if at == i))

            vacant(GX)
            pe.wait_ge(S["cast_set"], 6)
            gather(M, 0)
            pe.wait_ge(S["gates_ready"], 1)
            vacant(ATB)
            for t in range(TB):
                last = pe.transpose(bank[ATB][0:E, P * t:P * (t + 1)], GATES[:, t, :], I)
            last.then_inc(S["gt_full"], 1)
            pe.wait_ge(S["up_bias_in"], 16)
            vacant(UG, UU)
            up(M, 0, main_wait(0), main_leave)
            pe.wait_ge(S["gt_set"], 1)
            pe.wait_ge(S["down_bias_in"], 16)
            vacant(YB, *SCATTER)
            for i in range(4):
                t, c = divmod(i, 2)
                pe.matmul(bank[SCATTER[i]][:, :], GT[0:E, t, :], BDOWN[0:E, 512 * c:512 * (c + 1)],
                          start=True, stop=True).then_inc(S["bd_full"], 1)
            gather(M, 1)
            pe.wait_ge(S["bd_add"], 4)
            down(M, 0, main_wait(0), main_leave)
            with pe.Fori(1, E) as e:
                up(M, e, main_wait(e), main_leave)
                gather(M, e + 1)
                down(M, e, main_wait(e), main_leave)
            pe.wait_ge(S["flag_set"], 1)
            crowd = pe.value_load(flag[0:1, 0:1], min_val=0, max_val=SEQ)
            with pe.If(crowd > CAP):
                with pe.Fori(0, E) as e:
                    with pe.Fori(0, PASSES) as j:
                        n = E + e * PASSES + j
                        gather(M, n + 1)
                        up(M, n + 1, main_wait(n), main_leave)
                        down(M, n, main_wait(n), main_leave)
                pe.wait_ge(S["over_done"], 1)
            for t in range(TB):
                pe.wait_ge(S["x3_set"], t + 1)
                for half in range(2):
                    for k in range(4):
                        last = pe.transpose(bank[XT3B[2 * t + half]][:, P * k:P * (k + 1)],
                                            X2[:, t, P * (4 * half + k):P * (4 * half + k + 1)], I)
                    last.then_inc(S["xt3_full"], 1)
            pe.wait_ge(S["gate_in"], 16)
            for i in range(4):
                t, c = divmod(i, 2)
                pe.wait_ge(S["xt3_set"], 2 * t + 2)
                for k in range(DT):
                    last = pe.matmul(bank[PG[i]][:, :], XT3[:, k, P * t:P * (t + 1)], WPG[:, k, 512 * c:512 * (c + 1)],
                                     start=(k == 0), stop=(k == DT - 1))
                last.then_inc(S["pg_full"], 1)


_INS = ["x", "p", "g_mix", "w_in", "g_q", "g_k", "w_attn_branch", "a_re", "a_im", "log_dt", "b_re", "b_im", "c_re", "c_im",
        "d_skip", "w_glu", "b_glu", "w_out", "g_ffn", "w_router", "b_router", "w_up", "b_up", "w_down", "b_down",
        "g_ple_gate", "w_ple_gate", "w_ple_proj", "g_ple_post"]
_OUTS = [((1, 256, 1024), "float32")]


def kernel(**inputs):
    import numpy as _np
    import concourse.bacc as _bacc
    from concourse import mybir as _mybir
    from concourse.bass_utils import run_bass_kernel_spmd as _run

    nc = _bacc.Bacc("TRN2", target_bir_lowering=False, num_devices=1)
    arrays, args = {}, []
    for name in _INS:
        a = _np.ascontiguousarray(inputs[name])
        arrays[f"in_{name}_dram"] = a
        args.append(nc.dram_tensor(f"in_{name}_dram", a.shape, _mybir.dt.from_np(a.dtype), kind="ExternalInput").ap())
    for i, (shape, dtype) in enumerate(_OUTS):
        dt = _mybir.dt.from_np(_np.dtype(dtype))
        args.append(nc.dram_tensor(f"out_{i}_dram", shape, dt, kind="ExternalOutput").ap())
    hybrid_layer(nc, *args)
    r = _run(nc, [arrays], core_ids=[0])
    got = tuple(r.results[0][f"out_{i}_dram"] for i in range(len(_OUTS)))
    return got[0]
```

```python
from contextlib import ExitStack

import concourse.bass as bass
from concourse import mybir

P = 128
HALF = P // 2
BANK = 512
NBANKS = 8
F32 = mybir.dt.float32
BF16 = mybir.dt.bfloat16
I32 = mybir.dt.int32
ALU = mybir.AluOpType
ACT = mybir.ActivationFunctionType
AX = mybir.AxisListType.X

EPS = 1e-6
LIMIT = 7.0
ALPHA = 1.702
HIDDEN = -1e30
NEVER = -3e38
TAKEN = 3e38
TWO_PI = 6.283185307179586
TWO_PI_HI, TWO_PI_MID = 6.28125, 0.0019340515136718750
TWO_PI_LO = TWO_PI - TWO_PI_HI - TWO_PI_MID
ROUNDER = 12582912.0
PI_F32 = 3.1415925
SQUARINGS = 8
TAYLOR = 7
CAP = 64
BESIDE_ATTENTION = ("u0", "u1", "g0", "g1", "g2", "g3")
EARLY_GATES = 2


class Steps:

    def __init__(self, eng, sem):
        self.eng, self.sem, self.n, self.shift = eng, sem, 0, 0

    def did(self, ins):
        self.n += 1
        return ins.then_inc(self.sem, 1)

    def settle(self):
        self.eng.wait_ge(self.sem, self.n + self.shift)

    def link(self, ins):
        self.did(ins)
        self.settle()
        return ins


def order_of_banks():
    jobs = ["ht0", "ht1", "par", "ht2", "ht3", "q0", "q1", "k0", "k1", "v0", "v1"]
    jobs += ["qt0", "qt1", "kt0", "kt1", "bt0", "bt1", "ct0", "ct1"]
    for s in range(4 + 2):
        if s < 4:
            jobs += [f"z{2 * s}", f"z{2 * s + 1}"]
        if s >= 2:
            jobs += [f"o{s - 2}"]
        if s == 5:
            jobs += [f"x{i}" for i in range(4)]
        jobs += [BESIDE_ATTENTION[s]]
    for b in range(4):
        if b < 3:
            jobs += [f"x{4 * b + 4 + i}" for i in range(4)]
        jobs += [f"g{b + 4}", f"y{b}"] if b < 3 else [f"g{b + 4}", "a0", "a1", f"y{b}", "a2", "a3"]
    jobs += [f"glu{i}" for i in range(8)]
    jobs += ["out0", "out1", "out2", "xt0", "xt1", "pt", "out3", "lg", "pp0", "xt2", "xt3", "pp1", "pp2",
             "rk", "pp3"]
    return {name: (i % NBANKS, i // NBANKS) for i, name in enumerate(jobs)}


def hybrid_layer(nc, x, p, g_mix, w_in, g_q, g_k, w_attn, a_re, a_im, log_dt, b_re, b_im, c_re, c_im, d_skip,
                 w_glu, b_glu, w_out, g_ffn, w_router, b_router, w_up, b_up, w_down, b_down,
                 g_ple_gate, w_ple_gate, w_ple_proj, g_ple_post, out):
    _, SEQ, D = x.shape
    PLE = p.shape[3]
    G, N = a_re.shape[1:]
    GC = b_re.shape[3]
    W = G * GC
    E = w_router.shape[2]
    F = w_down.shape[2]
    DH = g_q.shape[1]
    H = w_attn.shape[1] // DH
    TB = SEQ // P
    DT = D // P
    WT = W // P
    PAIRS = H // 2
    TILES = G * N // P
    assert (TB, DT, WT, PAIRS, TILES, E, F, PLE) == (2, 8, 4, 4, 16, 32, D, 2 * P)
    BANKS = order_of_banks()

    with ExitStack() as ctx:
        def sem(name):
            return ctx.enter_context(nc.semaphore(name))

        def sb(name, cols, dt=F32):
            return ctx.enter_context(nc.sbuf_tensor(name, [P, cols], dt))

        PLACES, PLACE = 6, 4096
        ring = sb("ring", PLACES * PLACE)
        arena = sb("arena", 27136)
        ident = sb("ident", P)
        neg_tri = sb("neg_tri", P)
        neg_ones = sb("neg_ones", P)
        small = sb("small", 680)
        ident_b = sb("ident_b", P, BF16)
        hide_b = sb("hide_b", P, BF16)
        flag = sb("flag", 1, I32)
        bank = [ctx.enter_context(nc.psum_tensor(f"bank{i}", [P, BANK], F32)) for i in range(NBANKS)]

        def area(at, *dims):
            n = 1
            for d in dims:
                n *= d
            ap = arena[:, at:at + n]
            if len(dims) == 2:
                return ap.rearrange("p (a b) -> p a b", a=dims[0])
            if len(dims) == 3:
                return ap.rearrange("p (a b c) -> p a b c", a=dims[0], b=dims[1])
            return ap

        def spread(ap, n):
            return ap.unsqueeze(2).broadcast_to([ap.shape[0], ap.shape[1], n])

        A_X, A_HT, A_Q, A_K, A_QT, A_KT, A_V, A_UT, A_OT, A_GY, A_TC, A_GATE, A_BT, A_CT = (
            0, 2048, 4096, 5120, 6144, 7168, 8192, 9216, 10240, 11264, 12288, 20480, 24576, 25600)
        X = area(A_X, TB, D)
        HT = area(A_HT, DT, SEQ)
        Q = area(A_Q, TB, 512)
        K = area(A_K, TB, 512)
        QT = area(A_QT, PAIRS, SEQ)
        KT = area(A_KT, PAIRS, SEQ)
        V = area(A_V, TB, 512)
        UT = area(A_UT, WT, SEQ)
        OT = area(A_OT, PAIRS, SEQ)
        GY = area(A_GY, WT, SEQ)
        COS = area(A_TC, TILES, SEQ)
        SIN = area(A_TC + 4096, TILES, SEQ)
        GATE = area(A_GATE, 2 * DT, SEQ)
        BT = area(A_BT, 2, WT, P)
        CT = area(A_CT, 3, WT, P)
        SQ = area(A_UT, 4, 512)
        SOFT = area(A_Q, 4, 384)
        PROB = area(A_GY, 2, 384)
        ROT = area(A_X, 2, 2, 512)
        BACK = area(A_Q, 4, 2, 512)
        X_SQ = area(A_TC, TB, D)
        B_RAW = area(A_GATE, 2, TILES, 2 * GC)
        B_BAR = area(A_GATE + 1024, 2, TILES, 2 * GC)
        C_RAW = area(A_GATE + 2048, 2, WT, N)
        C_MASK = area(A_GATE + 2560, 2, WT, P)
        S5 = area(A_GATE + 3584, 32, TILES)
        PR = area(A_OT, P)
        LDT = area(A_OT + 128, 2)
        SZ = area(A_X, 4, SEQ)
        X2 = area(A_HT, TB, D)
        XN = area(A_Q, TB, D)
        H2T = area(A_QT, DT, SEQ)
        XB = arena[:, A_GATE:A_GATE + 3072].bitcast(BF16).rearrange("p (s t d) -> p s t d", s=3, t=TB)
        WPG = area(A_TC, DT, D)
        WPP = area(A_X, PLE // P, D)
        XS = area(A_V + 512, DT, CAP)
        ACTT = area(A_V + 1024, WT, P)
        Y = area(A_V + 1536, 512)
        WSEL = area(A_V + 3584, TB, P)
        WSELT = area(A_V + 3840, TB, P)
        EXTRA = arena[:, A_Q:A_Q + PLACE]
        BUP = area(A_V, 512)
        ACTS = area(A_V + 2048, 3, 512)
        PIN = area(A_V + 3584, TB, PLE)
        PLEV = area(A_X, TB, D)
        GPOST = area(A_BT, D)
        PT_IN = area(A_BT + 1024, PLE // P, SEQ)
        BDOWN = area(A_BT + 1536, 512)
        XT3 = area(A_Q, DT, SEQ)
        GSIG = area(A_V, TB, D)
        R0 = A_GATE + 3072
        SLOT = arena[:, R0:R0 + SEQ]
        SLOT_I = area(A_V + 2560, SEQ).bitcast(I32)
        LOGIT = area(R0 + 256, TB, E + 8)
        LEFT = area(R0 + 336, TB, E + 8)
        CHOSEN = area(R0 + 416, TB, E)
        GATES = area(R0 + 480, TB, E)
        RANK = area(R0 + 544, TB, E + 1)
        WR = area(R0 + 612, DT, E)
        GT = area(A_BT + 2048, TB, P)
        GATES4 = area(A_BT + 2304, TB, P)
        X3_SQ = area(A_GATE, TB, D)
        SELB = arena[:, R0 + 868:R0 + 868 + CAP].bitcast(BF16).rearrange("p (t c) -> p t c", t=TB)
        PICK = arena[:, R0 + 932:R0 + 932 + CAP]
        NPAR = 94
        PAR = small[:, 0:NPAR]
        P_ARE, P_AIM, P_LDT, P_GMIX, P_GFFN, P_GPLE, P_DSKIP, P_BGLU, P_GQ, P_GK = 0, 16, 32, 48, 56, 64, 72, 76, 92, 93
        RHO = small[:, 96:112]
        SSQ = small[:, 112:120]
        RSTD = small[:, 120:128]
        HSQ = small[:, 128:160]
        PARITY = small[:, 160:162]
        TOP8 = small[:, 162:178]
        NTOP = small[:, 178:180]
        SUM = small[:, 180:184]
        CNT = small[:, 184:186]
        BROUT = small[:, 186:218]
        AKC = small[:, 218:234]
        AKS = small[:, 234:250]
        AKT = small[:, 576:576 + 3 * TILES]
        ODD = small[:, 282:283]
        MARK_POOL, MARK = small[:, 283:284], small[:, 285:286]
        TABLE = small[:, 284:285]
        EYES = small[:, 624:624 + E + 1]
        EYES2 = small[:, 576:576 + E]
        PSQ = small[:, 288:292]
        PRT = small[:, 286:288]
        TRI = small[:, 320:448]
        ONES = small[:, 448:576]

        full = [sem(f"full{i}") for i in range(NBANKS)]
        free = [sem(f"free{i}") for i in range(NBANKS)]
        arrived = [sem(f"arrived{i}") for i in range(PLACES)]
        names = ("x_in_0 x_in_1 half_in extra_in params_in dt_in bc_in ident_set odd_set b_zero x_sq x_ms x_root x_normal dt_rows angle_set "
                 "sine_set turn_set bbar_set tables_set pool_tables_set head_sq head_ms head_ms_all head_root heads_set "
                 "abs_set soft_set sp_set cum_full early_gates_set rot_set back_set gelu_set sz_set mixed_set x_again "
                 "x2_sq x2_ms x2_root x2_normal router_in slots_set logit_top exp_set chosen_set flag_set gates_ready "
                 "down_bias_in cast_set rest_set_0 rest_set_1 up_bias_in gate_in post_in ple_in pp_ms pp_root "
                 "gt_full gt_set bd_full bd_add over_done x3_set x3_sq x3_ms x3_root xt3_full xt3_set pg_full "
                 "pg_sig fin_set stored dve_step act_step pool_step").split()
        S = {n: sem(n) for n in names}
        moe_names = ("sel_set wsel_set pick_set wt_full wt_set gx_full xs_set up_g up_u g_set sig_set act_set at_full "
                     "at_set y_full y_set sc_full sc_add dve_step").split()
        M = {n: sem("e_" + n) for n in moe_names}

        W_ORDER = [("in", i) for i in range(8)] + [("attn", 0)] + [("glu", 0), ("glu", 1)] + [("out", 0), ("out", 1)]
        TURN = {k: (i % PLACES, i // PLACES) for i, k in enumerate(W_ORDER)}
        FIRST = len(W_ORDER)
        PER_EXPERT = 6
        EXP_PLACE = [(FIRST + c) % PLACES for c in range(PER_EXPERT)]
        EXP_USES = [(FIRST + c) // PLACES for c in range(PER_EXPERT)]
        LAST_READ = {("in", 3): "u1", ("in", 0): "q1", ("in", 1): "k1", ("in", 2): "v1", ("attn", 0): "a3",
                     ("glu", 0): "glu7", ("glu", 1): "glu7", ("out", 0): "out2", ("out", 1): "out3"}
        LAST_READ.update({("in", 4 + i): f"g{2 * i + 1}" for i in range(4)})
        READ = {c: sem(f"read{c}") for c in (0, 1, 2, 4)}

        def place(i):
            return ring[:, i * PLACE:(i + 1) * PLACE]

        def weight(key, a):
            return place(TURN[key][0]).rearrange("p (a n) -> p a n", a=a)

        def expert_source(e, c):
            if isinstance(e, int):
                if c < 4:
                    return w_up[0, e, 2 * P * c:2 * P * (c + 1), :].rearrange("(k p) n -> p k n", p=P)
                return w_down[0, e, 4 * P * (c - 4):4 * P * (c - 3), :].rearrange("(k p) n -> p k n", p=P)
            if c < 4:
                return w_up[0, bass.ds(e, 1), 2 * P * c:2 * P * (c + 1), :].rearrange("o (k p) n -> p (o k) n", p=P)
            c -= 4
            return w_down[0, bass.ds(e, 1), 4 * P * c:4 * P * (c + 1), :].rearrange("o (k p) n -> p (o k) n", p=P)

        PASSES = TB * P // CAP - 1

        def wait_full(eng, job):
            eng.wait_ge(full[BANKS[job][0]], BANKS[job][1] + 1)

        def release(ins, job):
            return ins.then_inc(free[BANKS[job][0]], 1)

        def released(eng, job):
            eng.wait_ge(free[BANKS[job][0]], BANKS[job][1] + 1)

        def ps(job):
            return bank[BANKS[job][0]]

        def pairs(ap, a=2):
            return ap.rearrange("p (a n) -> p a n", a=a)

        LEVELS, DVE_TILES = SEQ.bit_length() - 1, 4

        def turn_tables(eng, st, lo, n, tmp_at, levels=range(LEVELS)):
            def tt(*a):
                return st.link(eng.tensor_tensor(*a))

            tiles = slice(lo, lo + n)
            c_a, s_a = AKC[:, tiles], AKS[:, tiles]
            c_sq, s_sq, c_s = (AKT[:, TILES * i + lo:TILES * i + lo + n] for i in range(3))
            for level in levels:
                k = 1 << level
                if level == 0:
                    st.did(eng.memset(COS[:, tiles, 0:1], 1.0))
                    st.link(eng.memset(SIN[:, tiles, 0:1], 0.0))
                c_k, s_k = spread(c_a, k), spread(s_a, k)
                tmp = area(tmp_at, n * k).rearrange("p (a b) -> p a b", a=n)
                c0, s0, c1, s1 = COS[:, tiles, 0:k], SIN[:, tiles, 0:k], COS[:, tiles, k:2 * k], SIN[:, tiles, k:2 * k]
                st.did(eng.tensor_tensor(tmp, s0, s_k, ALU.mult))
                tt(c1, c0, c_k, ALU.mult)
                st.did(eng.tensor_tensor(s1, s0, c_k, ALU.mult))
                tt(c1, c1, tmp, ALU.subtract)
                tt(tmp, c0, s_k, ALU.mult)
                tt(s1, s1, tmp, ALU.add)
                if level < LEVELS - 1:
                    st.did(eng.tensor_tensor(c_sq, c_a, c_a, ALU.mult))
                    st.did(eng.tensor_tensor(s_sq, s_a, s_a, ALU.mult))
                    tt(c_s, c_a, s_a, ALU.mult)
                    st.did(eng.tensor_tensor(c_a, c_sq, s_sq, ALU.subtract))
                    tt(s_a, c_s, c_s, ALU.add)

        GX, UG, UU, WTB, ATB, YB = 0, 1, 2, 3, 4, 5
        SCATTER = (6, 7, WTB, ATB)
        XT3B = (GX, UG, UU, YB)
        PARTS = [(0, slice(0, 512), 6), (0, slice(512, D), 7), (1, slice(0, 512), WTB), (1, slice(512, 768), ATB),
                 (1, slice(768, D), GX)]

        block = ctx.enter_context(nc.Block())

        def parameter_rows():
            rows = [(P_ARE, a_re[0].rearrange("(t q) n -> t (q n)", q=2), TILES),
                    (P_AIM, a_im[0].rearrange("(t q) n -> t (q n)", q=2), TILES),
                    (P_GMIX, g_mix[0].rearrange("(k p) -> k p", p=P), DT),
                    (P_GFFN, g_ffn[0].rearrange("(k p) -> k p", p=P), DT),
                    (P_GPLE, g_ple_gate[0].rearrange("(k p) -> k p", p=P), DT),
                    (P_DSKIP, d_skip[0].rearrange("(k p) -> k p", p=P), WT),
                    (P_BGLU, b_glu[0].rearrange("(k p) -> k p", p=P), 2 * DT)]
            both = [(PR[at:at + n, :], src) for at, src, n in rows]
            for at, g in ((P_GQ, g_q), (P_GK, g_k)):
                both += [(PR[at:at + 1, h * DH:(h + 1) * DH], g) for h in range(2)]
            return both

        @block.sync
        def _(sp):
            for t in range(TB):
                sp.dma_start(X[:, t, :], x[0, t * P:(t + 1) * P, :]).then_inc(S[f"x_in_{t}"], 16)
            rows = parameter_rows()
            sp.dma_start(LDT[32:48, :], log_dt[0].rearrange("(t q) -> t q", q=2)).then_inc(S["dt_in"], 16)
            for at, src in rows[:5]:
                sp.dma_start(at, src).then_inc(S["params_in"], 16)

            def source(key):
                name, i = key
                if name == "in":
                    return w_in[0, :, 512 * i:512 * (i + 1)].rearrange("(k p) n -> p k n", p=P)
                if name == "attn":
                    return w_attn[0].rearrange("(k p) n -> p k n", p=P)
                if name == "glu":
                    return w_glu[0, 2 * P * i:2 * P * (i + 1), :].rearrange("(k p) n -> p k n", p=P)
                return w_out[0, :, 512 * i:512 * (i + 1)].rearrange("(k p) n -> p k n", p=P)

            def load(at, src):
                sp.dma_start(place(at).rearrange("p (a n) -> p a n", a=src.shape[1]), src).then_inc(arrived[at], 16)

            held = {}
            for key in W_ORDER:
                at = TURN[key][0]
                if at in held:
                    wait_full(sp, held[at])
                src = source(key)
                if key == ("in", 0):
                    half = place(at).rearrange("p (a n) -> p a n", a=DT)
                    sp.dma_start(half[:, 0:DT // 2, :], src[:, 0:DT // 2, :]).then_inc(S["half_in"], 16)
                    for to, row in rows[5:]:
                        sp.dma_start(to, row).then_inc(S["params_in"], 16)
                    sp.dma_start(half[:, DT // 2:, :], src[:, DT // 2:, :]).then_inc(arrived[at], 16)
                else:
                    load(at, src)
                held[at] = LAST_READ[key]
                if key == ("in", 1):
                    sp.wait_ge(S["b_zero"], 1)
                    for r, src in enumerate((b_re, b_im)):
                        for q in range(2):
                            sp.dma_start(B_RAW[q * N:(q + 1) * N, r, :, q * GC:(q + 1) * GC],
                                         src[0].rearrange("(t q) n c -> q n t c", q=2)[q]).then_inc(S["bc_in"], 16)
                    for r, src in enumerate((c_re, c_im)):
                        sp.dma_start(C_RAW[:, r, :, :],
                                     src[0].rearrange("(b g) c n -> (g c) b n", b=WT)).then_inc(S["bc_in"], 16)
            for c in range(PER_EXPERT):
                wait_full(sp, held[EXP_PLACE[c]])
                load(EXP_PLACE[c], expert_source(0, c))

            wait_full(sp, "lg")
            sp.wait_ge(S["cast_set"], 3 * TB)
            sp.dma_start(EXTRA.rearrange("p (a n) -> p a n", a=2), expert_source(1, 0)).then_inc(S["extra_in"], 16)

            def load_piece(n, e, c):
                sp.wait_ge(READ[c] if c in READ else M["up_u" if c == 3 else "y_full"], n - 1 if c == 0 else n)
                load(EXP_PLACE[c], expert_source(e, c))

            for e, c in ((2, 0), (1, 1), (1, 2), (1, 3), (1, 4), (1, 5)):
                load_piece(e, e, c)
            with sp.Fori(2, E - 1) as e:
                for c in range(1, PER_EXPERT):
                    load_piece(e, e, c)
                load_piece(e + 1, e + 1, 0)
            for c in range(1, PER_EXPERT):
                load_piece(E - 1, E - 1, c)
            sp.wait_ge(S["flag_set"], 1)
            crowd = sp.value_load(flag[0:1, 0:1], min_val=0, max_val=SEQ)
            with sp.If(crowd > CAP):
                with sp.Fori(0, E) as e:
                    with sp.Fori(0, PASSES) as j:
                        n = E + e * PASSES + j
                        for c in range(PER_EXPERT):
                            load_piece(n, e, c)
            for i, (t, cols, _) in enumerate(PARTS):
                sp.wait_ge(S["fin_set"], i + 1)
                sp.dma_start(out[0, t * P:(t + 1) * P, cols], X2[:, t, cols]).then_inc(S["stored"], 16)
            sp.wait_ge(S["stored"], 16 * len(PARTS))

        @block.gpsimd
        def _(pool):
            st = Steps(pool, S["pool_step"])
            for m, v in ((ident[:, :], 0.0), (neg_ones[:, :], -1.0), (neg_tri[:, :], -1.0), (TRI, 1.0), (ONES, 1.0),
                         (hide_b[:, :], 0.0), (ident_b[:, :], 0.0)):
                st.did(pool.memset(m, v))
            st.settle()
            for m in (ident, ident_b):
                st.did(pool.affine_select(out=m[:, :], in_=m[:, :], compare_op=ALU.not_equal, fill=1.0, base=0,
                                          pattern=[[-1, P]], channel_multiplier=1))
            st.did(pool.affine_select(out=neg_tri[:, :], in_=neg_tri[:, :], compare_op=ALU.is_ge, fill=0.0, base=0,
                                      pattern=[[-1, P]], channel_multiplier=1))
            st.did(pool.affine_select(out=TRI, in_=TRI, compare_op=ALU.is_gt, fill=0.0, base=0,
                                      pattern=[[1, P]], channel_multiplier=-1))
            st.did(pool.affine_select(out=hide_b[:, :], in_=hide_b[:, :], compare_op=ALU.is_gt, fill=HIDDEN, base=0,
                                      pattern=[[1, P]], channel_multiplier=-1))
            st.settle()
            pool.sem_inc(S["ident_set"], 1)
            pool.iota(ODD.bitcast(I32), [[0, 1]], base=0, channel_multiplier=1).then_inc(S["odd_set"], 1)
            pool.memset(arena[:, A_GATE:A_GATE + 2 * TILES * 2 * GC], 0.0).then_inc(S["b_zero"], 1)

            pool.wait_ge(S["turn_set"], 1)
            turn_tables(pool, st, DVE_TILES, TILES - DVE_TILES, A_X + DVE_TILES * HALF * 2)
            pool.memset(MARK_POOL, 0.0).then_inc(S["pool_tables_set"], 1)

            released(pool, "o3")
            for i in range(TILES):
                b, j = divmod(i, 4)
                pool.wait_ge(S["rot_set"], i + 1)
                if b and j == 0:
                    wait_full(pool, f"y{b - 1}")
                for s, table in enumerate((COS, SIN)):
                    pool.tensor_tensor(pairs(BACK[:, j, s, :]), pairs(ROT[:, i % 2, 1, :]),
                                       table[:, i:i + 1, :].broadcast_to([P, 2, SEQ]), ALU.mult).then_inc(S["back_set"], 1)
            wait_full(pool, "g7")
            for t in range(TB):
                pool.dma_start(X2[:, t, :], x[0, t * P:(t + 1) * P, :]).then_inc(S["x_again"], 16)
            released(pool, "y3")
            for g in range(4):
                rows = slice(E * g, E * (g + 1))
                pool.dma_start(BDOWN[rows, :], b_down[0, :, 512 * (g % 2):512 * (g % 2 + 1)]).then_inc(S["down_bias_in"], 16)
                pool.dma_start(BUP[rows, :], b_up[0, :, 512 * g:512 * (g + 1)]).then_inc(S["up_bias_in"], 16)
            pool.dma_start(GPOST, g_ple_post[0:1, :].broadcast_to([P, D])).then_inc(S["post_in"], 16)
            pool.dma_start(WPG, w_ple_gate[0].rearrange("(k p) n -> p k n", p=P)).then_inc(S["gate_in"], 16)
            pool.wait_ge(S["mixed_set"], DT)
            pool.iota(SLOT_I, [[1, SEQ]], base=0, channel_multiplier=0).then_inc(S["slots_set"], 1)
            for i in range(2):
                pool.wait_ge(S["cast_set"], 2 * i + 2)
                pool.tensor_tensor(XN[:, 0, :], XN[:, 0, :], XB[:, i, 0, :], ALU.subtract).then_inc(S["rest_set_0"], 1)

        @block.scalar
        def _(act):
            st = Steps(act, S["act_step"])
            act.wait_ge(S["ident_set"], 1)
            act.activation(RSTD[:, 0:TB], ident[:, 0:TB], ACT.Sqrt)
            for t in range(TB):
                act.wait_ge(S[f"x_in_{t}"], 16)
                act.activation(X_SQ[:, t, :], X[:, t, :], ACT.Square, accum_out=SSQ[:, t:t + 1]).then_inc(S["x_sq"], 1)
            for t in range(TB):
                act.wait_ge(S["x_ms"], t + 1)
                act.activation(RSTD[:, t:t + 1], SSQ[:, t:t + 1], ACT.Sqrt).then_inc(S["x_root"], 1)
            for i, job in enumerate(("q0", "q1", "k0", "k1")):
                wait_full(act, job)
                act.activation(SQ[:, i, :], ps(job)[:, :], ACT.Square).then_inc(S["head_sq"], 1)
                release(act.activation((Q, K)[i // 2][:, i % 2, :], ps(job)[:, :], ACT.Copy), job)
                if i == 1:
                    act.wait_ge(S["angle_set"], 1)
                    act.activation(S5[:, 12, :], S5[:, 10, :], ACT.Sin).then_inc(S["sine_set"], 1)
                    act.activation(S5[:, 13, :], S5[:, 10, :], ACT.Sin, scale=0.5).then_inc(S["sine_set"], 1)
            act.wait_ge(S["head_ms_all"], 1)
            act.activation(HSQ, HSQ, ACT.Sqrt).then_inc(S["head_root"], 1)
            for t in range(TB):
                wait_full(act, f"v{t}")
                release(act.activation(V[:, t, :], ps(f"v{t}")[:, :], ACT.Copy), f"v{t}")
            for r in range(2):
                wait_full(act, f"bt{r}")
                release(act.activation(BT[:, r, :, :], pairs(ps(f"bt{r}")[:, :], WT), ACT.Copy),
                        f"bt{r}")
            wait_full(act, "ct0")
            act.activation(CT[:, 0, :, :], pairs(ps("ct0")[:, :], WT), ACT.Copy)
            release(act.activation(CT[:, 1, :, :], pairs(ps("ct0")[:, :], WT), ACT.Copy, scale=-1.0),
                    "ct0")
            wait_full(act, "ct1")
            release(act.activation(CT[:, 2, :, :], pairs(ps("ct1")[:, :], WT), ACT.Copy, scale=-1.0),
                    "ct1")

            def gate(i):
                wait_full(act, f"g{i}")
                release(act.activation(GATE[:, 2 * i:2 * i + 2, :], pairs(ps(f"g{i}")[:, :]), ACT.Sigmoid), f"g{i}")

            for s in range(PAIRS + 2):
                for h in (2 * s, 2 * s + 1) if s < PAIRS else ():
                    act.wait_ge(S["abs_set"], h + 1)
                    st.link(act.activation(SOFT[:, h % 4, :], SOFT[:, h % 4, :], ACT.Exp))
                    act.activation(SOFT[:, h % 4, :], SOFT[:, h % 4, :], ACT.Ln, bias=1.0).then_inc(S["soft_set"], 1)
                for h in (2 * s - 2, 2 * s - 1) if 1 <= s <= PAIRS else ():
                    act.wait_ge(S["cum_full"], h + 1)
                    if h >= 2:
                        wait_full(act, f"o{h // 2 - 1}")
                    release(act.activation(PROB[:, h % 2, :], ps(f"z{h}")[:, 0:384], ACT.Exp),
                            f"z{h}")
                beside = BESIDE_ATTENTION[s]
                wait_full(act, beside)
                i = int(beside[1])
                if beside[0] == "u":
                    release(act.activation(UT[:, 2 * i:2 * i + 2, :], pairs(ps(beside)[:, :]), ACT.Copy), beside)
                elif i < EARLY_GATES:
                    release(act.activation(GATE[:, 2 * i:2 * i + 2, :], pairs(ps(beside)[:, :]), ACT.Copy), beside)
                else:
                    gate(i)
            for i in range(EARLY_GATES):
                released(act, f"g{i}")
            early = GATE[:, 0:2 * EARLY_GATES, :]
            act.activation(early, early, ACT.Sigmoid).then_inc(S["early_gates_set"], 1)
            for i in range(4, DT):
                if i == DT - 1:
                    act.wait_ge(S["tables_set"], 1)
                gate(i)
            for b in range(WT):
                released(act, f"y{b}")
                act.activation(GY[:, b, :], GY[:, b, :], ACT.Gelu_apprx_tanh).then_inc(S["gelu_set"], 1)
            for i in range(DT):
                wait_full(act, f"glu{i}")
                if i >= 4:
                    act.wait_ge(S["mixed_set"], i - 3)
                act.activation(SZ[:, i % 4, :], ps(f"glu{i}")[:, SEQ:2 * SEQ], ACT.Sigmoid,
                               bias=PAR[:, P_BGLU + DT + i:P_BGLU + DT + i + 1]).then_inc(S["sz_set"], 1)

            act.wait_ge(S["mixed_set"], DT)
            act.dma_start(WR, w_router[0].rearrange("(k p) n -> p k n", p=P)).then_inc(S["router_in"], 16)
            act.dma_start(BROUT[0:1, :], b_router).then_inc(S["router_in"], 16)
            act.dma_start(WPP, w_ple_proj[0].rearrange("(k p) n -> p k n", p=P)).then_inc(S["ple_in"], 16)
            act.dma_start(PIN, p[0, 0].rearrange("(t p) n -> p t n", p=P)).then_inc(S["ple_in"], 16)
            for t in range(TB):
                for c in range(2):
                    released(act, f"out{2 * t + c}")
                act.activation(XN[:, t, :], X2[:, t, :], ACT.Square, accum_out=SSQ[:, 2 + t:3 + t]).then_inc(S["x2_sq"], 1)
                act.wait_ge(S["x2_ms"], t + 1)
                act.activation(RSTD[:, 2 + t:3 + t], SSQ[:, 2 + t:3 + t], ACT.Sqrt).then_inc(S["x2_root"], 1)
                if t == 0:
                    wait_full(act, "pt")
                    release(act.activation(PT_IN, pairs(ps("pt")[:, :], PLE // P), ACT.Copy), "pt")

            def embeddings(c):
                for t in range(TB):
                    wait_full(act, f"pp{TB * c + t}")
                for t in range(TB):
                    job = f"pp{TB * c + t}"
                    act.activation(PLEV[:, t, 512 * c:512 * (c + 1)], ps(job)[:, :], ACT.Copy)
                    release(act.activation(ps(job)[:, :], ps(job)[:, :], ACT.Square,
                                           accum_out=PSQ[:, TB * c + t:TB * c + t + 1]), job)

            for i in range(3):
                for t in range(TB):
                    if i == 0:
                        act.wait_ge(S["x2_normal"], t + 1)
                    else:
                        act.wait_ge(S[f"rest_set_{t}"], i)
                    act.activation(XB[:, i, t, :], XN[:, t, :], ACT.Copy).then_inc(S["cast_set"], 1)
                if i == 1:
                    embeddings(0)
            act.wait_ge(S["logit_top"], 1)
            for t in range(TB):
                act.activation(GATES[:, t, :], LOGIT[:, t, 0:E], ACT.Exp, bias=NTOP[:, t:t + 1]).then_inc(S["exp_set"], 1)
            embeddings(1)
            act.wait_ge(S["pp_ms"], 1)
            act.activation(PRT, PSQ[:, 0:TB], ACT.Sqrt).then_inc(S["pp_root"], 1)

            def expert(m, n):
                act.wait_ge(m["g_set"], n + 1)
                act.activation(ACTS[:, 2, :], ACTS[:, 0, :], ACT.Sigmoid, scale=ALPHA).then_inc(m["sig_set"], 1)
                act.wait_ge(m["at_full"], n + 1)
                act.activation(ACTT, pairs(bank[ATB][:, :], WT), ACT.Copy).then_inc(m["at_set"], 1)
                act.wait_ge(m["y_full"], n + 1)
                act.activation(Y, bank[YB][:, :], ACT.Copy).then_inc(m["y_set"], 1)

            act.activation(TABLE, PSQ[:, 0:1], ACT.Sigmoid)
            act.wait_ge(S["gt_full"], 1)
            act.activation(GT, bank[ATB][:, 0:SEQ].rearrange("p (t n) -> p t n", t=TB),
                           ACT.Copy).then_inc(S["gt_set"], 1)
            with act.Fori(0, E) as e:
                expert(M, e)
            act.wait_ge(S["flag_set"], 1)
            crowd = act.value_load(flag[0:1, 0:1], min_val=0, max_val=SEQ)
            with act.If(crowd > CAP):
                with act.Fori(0, E) as e:
                    with act.Fori(0, PASSES) as j:
                        expert(M, E + e * PASSES + j)
                act.wait_ge(S["over_done"], 1)

            for t in range(TB):
                act.wait_ge(S["x3_set"], t + 1)
                act.activation(X3_SQ[:, t, :], X2[:, t, :], ACT.Square, accum_out=SSQ[:, 4 + t:5 + t]).then_inc(S["x3_sq"], 1)
            act.wait_ge(S["x3_ms"], 1)
            act.activation(RSTD[:, 4:6], SSQ[:, 4:6], ACT.Sqrt).then_inc(S["x3_root"], 1)
            act.wait_ge(S["x3_ms"], 2)
            for i, (t, cols, at) in enumerate(PARTS):
                act.wait_ge(S["pg_full"], i + 1)
                act.activation(GSIG[:, t, cols], bank[at][:, 0:cols.stop - cols.start], ACT.Sigmoid,
                               scale=RSTD[:, 4 + t:5 + t]).then_inc(S["pg_sig"], 1)

        @block.vector
        def _(dve):
            st = Steps(dve, S["dve_step"])
            T = lambda i: S5[:, i, :]

            def ts(*a):
                return st.link(dve.tensor_scalar(*a))

            def tt(*a):
                return st.link(dve.tensor_tensor(*a))

            def stt(*a):
                return st.link(dve.scalar_tensor_tensor(*a))

            def mean_plus_eps(ap, n):
                return dve.tensor_scalar(ap, ap, 1.0 / n, EPS, ALU.mult, ALU.add)

            dve.wait_ge(S["dt_in"], 16)
            dve.tensor_copy(PR[32:48, :].rearrange("p (q n) -> p q n", q=2),
                            spread(LDT[32:48, :], N)).then_inc(S["dt_rows"], 1)
            for t in range(TB):
                dve.wait_ge(S["x_sq"], t + 1)
                mean_plus_eps(SSQ[:, t:t + 1], D).then_inc(S["x_ms"], 1)
                dve.wait_ge(S["x_root"], t + 1)
                st.link(dve.reciprocal(RSTD[:, t:t + 1], RSTD[:, t:t + 1]))
                dve.tensor_scalar(X[:, t, :], X[:, t, :], RSTD[:, t:t + 1], None, ALU.mult).then_inc(S["x_normal"], 1)
            wait_full(dve, "par")
            release(dve.tensor_copy(PAR, ps("par")[:, 0:NPAR]), "par")
            released(dve, "par")
            for i in range(4):
                t, half = divmod(i, 2)
                wait_full(dve, f"ht{i}")
                release(dve.tensor_tensor(HT[:, 4 * half:4 * half + 4, t * P:(t + 1) * P], pairs(ps(f"ht{i}")[:, :], 4),
                                          spread(PAR[:, P_GMIX + 4 * half:P_GMIX + 4 * half + 4], P), ALU.mult),
                        f"ht{i}")

            def expm1(y, v, z):
                ts(z, v, 1.0 / 2 ** SQUARINGS, None, ALU.mult)
                ts(y, z, 1.0 / TAYLOR, 1.0, ALU.mult, ALU.add)
                for k in range(TAYLOR - 1, 1, -1):
                    stt(y, y, 1.0 / k, z, ALU.mult, ALU.mult)
                    ts(y, y, 1.0, None, ALU.add)
                tt(y, y, z, ALU.mult)
                for _ in range(SQUARINGS):
                    stt(y, y, 2.0, y, ALU.add, ALU.mult)

            LR, LI = PAR[:, P_ARE:P_ARE + TILES], PAR[:, P_AIM:P_AIM + TILES]
            expm1(T(0), PAR[:, P_LDT:P_LDT + TILES], T(1))
            ts(T(0), T(0), 1.0, None, ALU.add)
            tt(T(2), LR, T(0), ALU.mult)
            tt(T(3), LI, T(0), ALU.mult)
            expm1(T(4), T(2), T(1))
            ts(RHO, T(4), 1.0, None, ALU.add)
            ts(T(5), T(3), 1.0 / TWO_PI, None, ALU.mult)
            ts(T(5), T(5), ROUNDER, None, ALU.add)
            ts(T(5), T(5), -ROUNDER, None, ALU.add)
            stt(T(10), T(5), -TWO_PI_HI, T(3), ALU.mult, ALU.add)
            stt(T(10), T(5), -TWO_PI_MID, T(10), ALU.mult, ALU.add)
            stt(T(10), T(5), -TWO_PI_LO, T(10), ALU.mult, ALU.add)
            dve.tensor_scalar(T(10), T(10), PI_F32, -PI_F32, ALU.min, ALU.max).then_inc(S["angle_set"], 1)
            dve.wait_ge(S["sine_set"], 2)
            stt(T(14), T(13), -2.0, T(13), ALU.mult, ALU.mult)
            ts(AKC, T(14), 1.0, None, ALU.add)
            st.link(dve.tensor_copy(AKS, T(12)))
            dve.tensor_tensor(T(6), T(4), AKC, ALU.mult).then_inc(S["turn_set"], 1)
            dve.wait_ge(S["turn_set"], 1)
            tt(T(6), T(6), T(14), ALU.add)
            tt(T(7), RHO, T(12), ALU.mult)
            tt(T(8), LR, LR, ALU.mult)
            tt(T(9), LI, LI, ALU.mult)
            tt(T(8), T(8), T(9), ALU.add)
            st.link(dve.reciprocal(T(8), T(8)))
            tt(T(16), T(6), LR, ALU.mult)
            tt(T(17), T(7), LI, ALU.mult)
            tt(T(16), T(16), T(17), ALU.add)
            tt(T(16), T(16), T(8), ALU.mult)
            tt(T(18), T(7), LR, ALU.mult)
            tt(T(19), T(6), LI, ALU.mult)
            tt(T(18), T(18), T(19), ALU.subtract)
            tt(T(18), T(18), T(8), ALU.mult)
            dve.wait_ge(S["bc_in"], 16 * 6)
            fr, fi = spread(T(16), 2 * GC), spread(T(18), 2 * GC)
            scratch = area(A_X, TILES, 2 * GC)
            for r, (f0, f1, op) in enumerate(((fr, fi, ALU.subtract), (fi, fr, ALU.add))):
                released(dve, "ht3")
                st.did(dve.tensor_tensor(B_BAR[:, r, :, :], B_RAW[:, 0, :, :], f0, ALU.mult))
                tt(scratch, B_RAW[:, 1, :, :], f1, ALU.mult)
                tt(B_BAR[:, r, :, :], B_BAR[:, r, :, :], scratch, op)
            dve.wait_ge(S["odd_set"], 1)
            odd = ODD.bitcast(I32)
            ts(odd, odd, 4, 1, ALU.logical_shift_right, ALU.bitwise_and)
            st.link(dve.tensor_copy(PARITY[:, 1:2], odd))
            ts(PARITY[:, 0:1], PARITY[:, 1:2], -1.0, 1.0, ALU.mult, ALU.add)
            for r in range(2):
                for q in range(2):
                    st.did(dve.tensor_scalar(C_MASK[:, r, :, q * N:(q + 1) * N], C_RAW[:, r, :, :],
                                             PARITY[:, q:q + 1], None, ALU.mult))
            st.settle()
            dve.memset(MARK, 0.0).then_inc(S["bbar_set"], 1)

            dve.wait_ge(S["head_sq"], 4)
            dve.tensor_reduce(HSQ, SQ.rearrange("p i (h d) -> p (i h) d", h=H), AX, ALU.add).then_inc(S["head_ms"], 1)
            dve.wait_ge(S["head_ms"], 1)
            mean_plus_eps(HSQ, DH).then_inc(S["head_ms_all"], 1)
            dve.wait_ge(S["head_root"], 1)
            st.link(dve.reciprocal(HSQ, HSQ))
            for i in range(4):
                v = (Q, K)[i // 2][:, i % 2, :].rearrange("p (h d) -> p h d", h=H)
                released(dve, f"{'qk'[i // 2]}{i % 2}")
                dve.tensor_tensor(v, v, spread(HSQ[:, H * i:H * (i + 1)], DH), ALU.mult).then_inc(S["heads_set"], 1)
            turn_tables(dve, st, 0, DVE_TILES, A_X, range(4))
            for i in range(4):
                job = f"{'qk'[i // 2]}t{i % 2}"
                wait_full(dve, job)
                dst, col, scale = ((QT, P_GQ, DH ** -0.5), (KT, P_GK, 1.0))[i // 2]
                t = i % 2
                release(dve.tensor_scalar(dst[:, :, t * P:(t + 1) * P], pairs(ps(job)[:, :], PAIRS), PAR[:, col:col + 1],
                                          scale, ALU.mult, ALU.mult), job)

            TABLES_BESIDE = ((), (), (), (), (4, 5, 6), (7,))
            for s in range(PAIRS + 2):
                for h in (2 * s, 2 * s + 1) if s < PAIRS else ():
                    wait_full(dve, f"z{h}")
                    if h >= 4:
                        dve.wait_ge(S["cum_full"], h - 3)
                    ts(SOFT[:, h % 4, :], ps(f"z{h}")[:, 0:384], 0.0, -2.0, ALU.max, ALU.mult)
                    dve.tensor_tensor(SOFT[:, h % 4, :], SOFT[:, h % 4, :], ps(f"z{h}")[:, 0:384],
                                      ALU.add).then_inc(S["abs_set"], 1)
                for h in (2 * s, 2 * s + 1) if s < PAIRS else ():
                    dve.wait_ge(S["soft_set"], h + 1)
                    dve.scalar_tensor_tensor(SOFT[:, h % 4, :], ps(f"z{h}")[:, 0:384], 0.0, SOFT[:, h % 4, :],
                                             ALU.max, ALU.add).then_inc(S["sp_set"], 1)
                if s >= 2:
                    job = f"o{s - 2}"
                    wait_full(dve, job)
                    release(dve.tensor_copy(OT[:, s - 2, :], ps(job)[:, 0:SEQ]), job)
                turn_tables(dve, st, 0, DVE_TILES, A_X, TABLES_BESIDE[s])

            st.settle()
            dve.memset(MARK, 0.0).then_inc(S["tables_set"], 1)

            def y_out(b):
                wait_full(dve, f"y{b}")
                release(dve.scalar_tensor_tensor(GY[:, b, :], UT[:, b, :], PAR[:, P_DSKIP + b:P_DSKIP + b + 1],
                                                 ps(f"y{b}")[:, 0:SEQ], ALU.mult, ALU.add), f"y{b}")

            def mix_attention():
                for i in range(4):
                    wait_full(dve, f"a{i}")
                    released(dve, f"g{i}")
                    release(dve.tensor_tensor(GATE[:, 2 * i:2 * i + 2, :], GATE[:, 2 * i:2 * i + 2, :],
                                              pairs(ps(f"a{i}")[:, :]), ALU.mult), f"a{i}")

            dve.wait_ge(S["pool_tables_set"], 1)
            for i in range(TILES):
                b, j = divmod(i, 4)
                job = f"x{i}"
                m1, m2 = ROT[:, i % 2, 0, :], ROT[:, i % 2, 1, :]
                wait_full(dve, job)
                if i >= 2:
                    dve.wait_ge(S["back_set"], 2 * (i - 1))
                st.did(dve.tensor_tensor(pairs(m1), pairs(ps(job)[:, :]), COS[:, i:i + 1, :].broadcast_to([P, 2, SEQ]), ALU.mult))
                release(dve.tensor_tensor(pairs(m2), pairs(ps(job)[:, :]), SIN[:, i:i + 1, :].broadcast_to([P, 2, SEQ]),
                                          ALU.mult), job)
                released(dve, job)
                st.did(dve.tensor_tensor(m1[:, 0:SEQ], m1[:, 0:SEQ], m2[:, SEQ:], ALU.add))
                tt(m1[:, SEQ:], m1[:, SEQ:], m2[:, 0:SEQ], ALU.subtract)
                decay = RHO[:, i:i + 1].broadcast_to([P, SEQ])
                dve.tensor_tensor_scan(m2[:, 0:SEQ], decay, m1[:, 0:SEQ], 0.0, ALU.mult, ALU.add)
                dve.tensor_tensor_scan(m2[:, SEQ:], decay, m1[:, SEQ:], 0.0, ALU.mult, ALU.add).then_inc(S["rot_set"], 1)
                if j == 3 and b:
                    y_out(b - 1)
            y_out(3)
            dve.wait_ge(S["early_gates_set"], 1)
            mix_attention()

            released(dve, "a3")
            released(dve, "g7")
            for i in range(DT):
                job = f"glu{i}"
                z = SZ[:, i % 4, :]
                dve.wait_ge(S["sz_set"], i + 1)
                release(dve.scalar_tensor_tensor(z, ps(job)[:, 0:SEQ], PAR[:, P_BGLU + i:P_BGLU + i + 1], z,
                                                 ALU.add, ALU.mult), job)
                released(dve, job)
                tt(z, z, GATE[:, DT + i, :], ALU.mult)
                dve.tensor_tensor(GATE[:, i, :], GATE[:, i, :], z, ALU.add).then_inc(S["mixed_set"], 1)
            dve.wait_ge(S["x_again"], 16 * TB)
            for t in range(TB):
                for c in range(2):
                    job = f"out{2 * t + c}"
                    wait_full(dve, job)
                    part = X2[:, t, 512 * c:512 * (c + 1)]
                    release(dve.tensor_tensor(part, part, ps(job)[:, :], ALU.add), job)
                dve.wait_ge(S["x2_sq"], t + 1)
                mean_plus_eps(SSQ[:, 2 + t:3 + t], D).then_inc(S["x2_ms"], 1)
                dve.wait_ge(S["x2_root"], t + 1)
                st.link(dve.reciprocal(RSTD[:, 2 + t:3 + t], RSTD[:, 2 + t:3 + t]))
                dve.tensor_scalar(XN[:, t, :], X2[:, t, :], RSTD[:, 2 + t:3 + t], None, ALU.mult).then_inc(S["x2_normal"], 1)
                for half in range(2):
                    job = f"xt{2 * t + half}"
                    wait_full(dve, job)
                    release(dve.tensor_tensor(H2T[:, 4 * half:4 * half + 4, t * P:(t + 1) * P], pairs(ps(job)[:, :], 4),
                                              spread(PAR[:, P_GFFN + 4 * half:P_GFFN + 4 * half + 4], P), ALU.mult), job)

            def rest(i):
                dve.wait_ge(S["cast_set"], 2 * i + 2)
                dve.tensor_tensor(XN[:, 1, :], XN[:, 1, :], XB[:, i, 1, :], ALU.subtract).then_inc(S["rest_set_1"], 1)

            rest(0)

            def at(e):
                return slice(e, e + 1) if isinstance(e, int) else bass.ds(e, 1)

            def select(m, e, slots):
                for t in range(TB):
                    last = dve.tensor_scalar(SELB[:, t, :], slots, RANK[:, t, at(e)], None, ALU.is_equal)
                last.then_inc(m["sel_set"], 1)

            def select_weighted(m, e, slots):
                for t in range(TB):
                    last = dve.tensor_scalar(pairs(WSEL[:, t, :]), slots.unsqueeze(1).broadcast_to([P, 2, CAP]),
                                             RANK[:, t, at(e)], GATES[:, t, at(e)], ALU.is_equal, ALU.mult)
                last.then_inc(m["wsel_set"], 1)

            def pick(m, e):
                dve.tensor_copy(PICK, EYES[:, at(e)].broadcast_to([P, CAP])).then_inc(m["pick_set"], 1)

            dve.wait_ge(S["mixed_set"], DT)
            st.did(dve.memset(EYES[:, E:], 0.0))
            st.did(dve.tensor_tensor(EYES[:, 0:E], ident[:, 0:E], ident[:, E:2 * E], ALU.add))
            tt(EYES2, ident[:, 2 * E:3 * E], ident[:, 3 * E:], ALU.add)
            tt(EYES[:, 0:E], EYES[:, 0:E], EYES2, ALU.add)
            dve.wait_ge(S["slots_set"], 1)
            st.link(dve.tensor_copy(SLOT, SLOT_I))
            st.did(dve.memset(LOGIT[:, :, E:], NEVER))
            st.did(dve.memset(TOP8, NEVER))
            st.did(dve.memset(RANK[:, :, E:E + 1], -1.0))
            st.settle()
            wait_full(dve, "lg")
            release(dve.tensor_copy(LOGIT[:, :, 0:E], ps("lg")[:, 0:TB * E].rearrange("p (t e) -> p t e", t=TB)), "lg")
            released(dve, "lg")
            for t in range(TB):
                st.did(dve.max(TOP8[:, 8 * t:8 * t + 8], LOGIT[:, t, 0:E]))
            st.settle()
            for t in range(TB):
                st.did(dve.tensor_scalar(NTOP[:, t:t + 1], TOP8[:, 8 * t:8 * t + 1], -1.0, None, ALU.mult))
            st.settle()
            dve.memset(TOP8.rearrange("p (t k) -> p t k", t=TB)[:, :, 4:8], NEVER).then_inc(S["logit_top"], 1)
            dve.wait_ge(S["logit_top"], 1)
            for t in range(TB):
                st.did(dve.match_replace(LEFT[:, t, :], TOP8[:, 8 * t:8 * t + 8], LOGIT[:, t, :], TAKEN))
            st.settle()
            dve.tensor_tensor(CHOSEN, LEFT[:, :, 0:E], LOGIT[:, :, 0:E], ALU.not_equal).then_inc(S["chosen_set"], 1)
            rest(1)
            pick(M, 0)
            wait_full(dve, "rk")
            st.did(dve.scalar_tensor_tensor(RANK[:, :, 0:E], ps("rk")[:, 0:TB * E].rearrange("p (t e) -> p t e", t=TB), 1.0,
                                            CHOSEN, ALU.add, ALU.mult))
            release(dve.tensor_reduce(CNT[0:1, 0:1], ps("rk")[0:1, TB * E:TB * E + E], AX, ALU.max), "rk")
            released(dve, "rk")
            dve.tensor_copy(flag[0:1, 0:1], CNT[0:1, 0:1]).then_inc(S["flag_set"], 1)
            st.link(dve.tensor_scalar(RANK[:, :, 0:E], RANK[:, :, 0:E], -1.0, None, ALU.add))

            def gathered(m, n):
                dve.wait_ge(m["gx_full"], n + 1)
                dve.tensor_tensor(XS, pairs(bank[GX][:, :], DT), spread(PAR[:, P_GFFN:P_GFFN + DT], CAP),
                                  ALU.mult).then_inc(m["xs_set"], 1)

            def activate(m, n):
                dve.wait_ge(m["up_g"], n + 1)
                dve.tensor_scalar(ACTS[:, 0, :], bank[UG][:, :], LIMIT, None, ALU.min).then_inc(m["g_set"], 1)
                dve.wait_ge(m["up_u"], n + 1)
                dve.tensor_scalar(ACTS[:, 1, :], bank[UU][:, :], LIMIT, -LIMIT, ALU.min, ALU.max).then_inc(m["dve_step"], 1)
                dve.wait_ge(m["dve_step"], n * 2 + 1)
                dve.scalar_tensor_tensor(ACTS[:, 1, :], ACTS[:, 1, :], 1.0, ACTS[:, 0, :], ALU.add,
                                         ALU.mult).then_inc(m["dve_step"], 1)
                dve.wait_ge(m["dve_step"], n * 2 + 2)
                dve.wait_ge(m["sig_set"], n + 1)
                dve.tensor_tensor(ACTS[:, 1, :], ACTS[:, 1, :], ACTS[:, 2, :], ALU.mult).then_inc(m["act_set"], 1)

            def weights_back(m, n):
                dve.wait_ge(m["wt_full"], n + 1)
                dve.tensor_copy(WSELT, bank[WTB][:, 0:SEQ].rearrange("p (t n) -> p t n", t=TB)).then_inc(m["wt_set"], 1)

            def add_up(m, n, last=False):
                for q in range(4):
                    t, c = divmod(q, 2)
                    dve.wait_ge(m["sc_full"], n * 4 + q + 1)
                    part = X2[:, t, 512 * c:512 * (c + 1)]
                    dve.tensor_tensor(part, part, bank[SCATTER[q]][:, :], ALU.add).then_inc(m["sc_add"], 1)
                    if last and c == 1:
                        dve.wait_ge(m["sc_add"], n * 4 + q + 1)
                        dve.memset(MARK, 0.0).then_inc(S["x3_set"], 1)

            def add_biases():
                for i in (3, 2, 0, 1):
                    t, c = divmod(i, 2)
                    dve.wait_ge(S["bd_full"], i + 1)
                    part = X2[:, t, 512 * c:512 * (c + 1)]
                    dve.tensor_tensor(part, part, bank[SCATTER[i]][:, :], ALU.add).then_inc(S["bd_add"], 1)

            def expert(m, n, last=False):
                select(m, n + 1, SLOT[:, 0:CAP])
                select_weighted(m, n, SLOT[:, 0:CAP])
                activate(m, n)
                if isinstance(n, int) and n == 0:
                    add_biases()
                gathered(m, n + 1)
                weights_back(m, n)
                pick(m, n + 1)
                add_up(m, n, last)

            select(M, 0, SLOT[:, 0:CAP])
            gathered(M, 0)
            dve.wait_ge(S["exp_set"], TB)
            dve.wait_ge(S["chosen_set"], 1)
            tt(GATES, GATES, CHOSEN, ALU.mult)
            st.link(dve.tensor_reduce(SUM[:, 0:TB], GATES, AX, ALU.add))
            st.link(dve.reciprocal(SUM[:, 0:TB], SUM[:, 0:TB]))
            tt(GATES, GATES, spread(SUM[:, 0:TB], E), ALU.mult)
            dve.tensor_copy(GATES4.rearrange("p t (g e) -> p t g e", g=4),
                            GATES.unsqueeze(2).broadcast_to([P, TB, 4, E])).then_inc(S["gates_ready"], 1)
            for c in range(2):
                for t in range(TB):
                    released(dve, f"pp{TB * c + t}")
            dve.wait_ge(S["gates_ready"], 1)
            tt(PSQ[:, 0:TB], PSQ[:, 0:TB], PSQ[:, TB:2 * TB], ALU.add)
            mean_plus_eps(PSQ[:, 0:TB], D).then_inc(S["pp_ms"], 1)
            dve.wait_ge(S["pp_root"], 1)
            st.link(dve.reciprocal(PRT, PRT))
            dve.wait_ge(S["post_in"], 16)
            for t in range(TB):
                st.did(dve.scalar_tensor_tensor(PLEV[:, t, :], PLEV[:, t, :], PRT[:, t:t + 1], GPOST, ALU.mult, ALU.mult))
            st.settle()
            expert(M, 0)
            with dve.Fori(1, E - 1) as e:
                expert(M, e)
            expert(M, E - 1, True)
            dve.wait_ge(S["flag_set"], 1)
            crowd = dve.value_load(flag[0:1, 0:1], min_val=0, max_val=SEQ)
            with dve.If(crowd > CAP):
                dve.wait_ge(M["pick_set"], E + 1)
                dve.wait_ge(M["sc_add"], 4 * E)
                with dve.Fori(0, E) as e:
                    with dve.Fori(0, PASSES) as j:
                        n = E + e * PASSES + j
                        slots = SLOT[:, bass.ds(j * CAP + CAP, CAP)]
                        select(M, e, slots)
                        select_weighted(M, e, slots)
                        pick(M, e)
                        gathered(M, n + 1)
                        activate(M, n)
                        weights_back(M, n)
                        add_up(M, n)

                dve.memset(MARK, 0.0).then_inc(S["over_done"], 1)

            for i in range(4):
                t, half = divmod(i, 2)
                dve.wait_ge(S["xt3_full"], i + 1)
                dve.tensor_tensor(XT3[:, 4 * half:4 * half + 4, t * P:(t + 1) * P], pairs(bank[XT3B[i]][:, :], 4),
                                  spread(PAR[:, P_GPLE + 4 * half:P_GPLE + 4 * half + 4], P), ALU.mult).then_inc(S["xt3_set"], 1)
            dve.wait_ge(S["x3_sq"], TB)
            mean_plus_eps(SSQ[:, 4:6], D).then_inc(S["x3_ms"], 1)
            dve.wait_ge(S["x3_root"], 1)
            dve.reciprocal(RSTD[:, 4:6], RSTD[:, 4:6]).then_inc(S["x3_ms"], 1)
            for i, (t, cols, _) in enumerate(PARTS):
                dve.wait_ge(S["pg_sig"], i + 1)
                tt(GSIG[:, t, cols], GSIG[:, t, cols], PLEV[:, t, cols], ALU.mult)
                dve.tensor_tensor(X2[:, t, cols], X2[:, t, cols], GSIG[:, t, cols], ALU.add).then_inc(S["fin_set"], 1)

        @block.tensor
        def _(pe):
            I = ident[:, :]

            def take(job):
                at, use = BANKS[job]
                if use:
                    pe.wait_ge(free[at], use)
                return bank[at]

            def done(ins, job):
                return ins.then_inc(full[BANKS[job][0]], 1)

            def arrive(key):
                at, use = TURN[key]
                pe.wait_ge(arrived[at], 16 * (use + 1))

            pe.wait_ge(S["ident_set"], 1)
            for i in range(4):
                t, half = divmod(i, 2)
                if i == 2:
                    pe.wait_ge(S["params_in"], 16 * 11)
                    pe.wait_ge(S["dt_rows"], 1)
                    done(pe.transpose(take("par")[:, 0:NPAR], PR[0:NPAR, :], I[0:NPAR, 0:NPAR]), "par")
                b = take(f"ht{i}")
                pe.wait_ge(S["x_normal"], t + 1)
                for k in range(4):
                    last = pe.transpose(b[:, P * k:P * (k + 1)], X[:, t, P * (4 * half + k):P * (4 * half + k + 1)], I)
                done(last, f"ht{i}")

            def columns(job, key, a, parts, rhs, n=DT):
                b = take(job)
                for i, m in enumerate(parts):
                    for k in range(n):
                        last = pe.matmul(b[:, SEQ * i:SEQ * (i + 1)], weight(key, a)[:, k, P * m:P * (m + 1)], rhs[:, k, :],
                                         start=(k == 0), stop=(k == n - 1))
                return done(last, job)

            pe.wait_ge(S["half_in"], 16)
            for n, name in enumerate("qkv"):
                for t in range(TB):
                    b = take(f"{name}{t}")
                    if n == 0:
                        released(pe, f"ht{2 * t + 1}")
                    for k in range(DT):
                        if t == 0 and k == (DT // 2 if n == 0 else 0):
                            arrive(("in", n))
                        last = pe.matmul(b[:, :], HT[:, k, t * P:(t + 1) * P], weight(("in", n), DT)[:, k, :],
                                         start=(k == 0), stop=(k == DT - 1))
                    done(last, f"{name}{t}")

            def projected(job):
                i = int(job[1])
                n = 3 if job[0] == "u" else 4 + i // 2
                arrive(("in", n))
                columns(job, ("in", n), DT, (2 * (i % 2), 2 * (i % 2) + 1), HT)

            for i in range(4):
                job = f"{'qk'[i // 2]}t{i % 2}"
                b = take(job)
                pe.wait_ge(S["heads_set"], i + 1)
                for k in range(PAIRS):
                    last = pe.transpose(b[:, P * k:P * (k + 1)], (Q, K)[i // 2][:, i % 2, P * k:P * (k + 1)], I)
                done(last, job)

            pe.wait_ge(S["bbar_set"], 1)
            for r in range(2):
                b = take(f"bt{r}")
                flat = B_BAR[:, r, :, :].rearrange("p t c -> p (t c)")
                for k in range(WT):
                    last = pe.transpose(b[:, P * k:P * (k + 1)], flat[:, P * k:P * (k + 1)], I)
                done(last, f"bt{r}")
            for r in range(2):
                b = take(f"ct{r}")
                for k in range(WT):
                    last = pe.transpose(b[:, P * k:P * (k + 1)], C_MASK[:, r, k, :], I)
                done(last, f"ct{r}")
            def s5_in(blk):
                bs = [take(f"x{4 * blk + j}") for j in range(4)]
                for r in range(2):
                    for j in range(4):
                        rows = slice(32 * j, 32 * j + 32)
                        last = pe.matmul(bs[j][:, SEQ * r:SEQ * (r + 1)], BT[rows, r, blk, :], UT[rows, blk, :],
                                         start=True, stop=True)
                        if r == 1:
                            done(last, f"x{4 * blk + j}")

            def s5_out(blk):
                b = take(f"y{blk}")
                pe.wait_ge(S["back_set"], 8 * (blk + 1))
                for k, (c, s, r) in enumerate(((0, 0, 0), (1, 1, 1), (2, 1, 0), (2, 0, 1))):
                    for j in range(4):
                        last = pe.matmul(b[32 * j:32 * j + 32, 0:SEQ], CT[:, c, blk, 32 * j:32 * j + 32],
                                         BACK[:, j, s, SEQ * r:SEQ * (r + 1)], start=(k == 0), stop=(k == 3))
                done(last, f"y{blk}")

            released(pe, "kt1")
            for s in range(PAIRS + 2):
                if s < PAIRS:
                    zs = [take(f"z{2 * s + q}") for q in range(2)]
                    for k, (lo, n) in enumerate(((0, SEQ), (P, P))):
                        for q in range(2):
                            rows = slice(DH * q, DH * (q + 1))
                            pe.matmul(zs[q][:, SEQ * k:SEQ * k + n], KT[rows, s, P * k:P * (k + 1)], QT[rows, s, lo:lo + n],
                                      start=(k == 0), stop=False, skip_group_check=True)
                    for q in range(2):
                        for k in range(2):
                            last = pe.matmul(zs[q][:, SEQ * k:SEQ * k + P], ident_b[:, :], hide_b[:, :],
                                             start=False, stop=True, skip_group_check=True)
                        done(last, f"z{2 * s + q}")
                if 1 <= s <= PAIRS:
                    for h in (2 * s - 2, 2 * s - 1):
                        b, sp = ps(f"z{h}"), SOFT[:, h % 4, :]
                        pe.wait_ge(S["sp_set"], h + 1)
                        pe.matmul(b[:, 0:SEQ], neg_tri[:, :], sp[:, 0:SEQ], start=False, stop=True, skip_group_check=True)
                        pe.matmul(b[:, P:SEQ], neg_ones[:, :], sp[:, SEQ:], start=False, stop=True, skip_group_check=True)
                        pe.matmul(b[:, SEQ:SEQ + P], neg_tri[:, :], sp[:, SEQ:], start=False, stop=True,
                                  skip_group_check=True).then_inc(S["cum_full"], 1)
                if s >= 2:
                    b = take(f"o{s - 2}")
                    for k in range(2):
                        for q in range(2):
                            h = 2 * (s - 2) + q
                            released(pe, f"z{h}")
                            last = pe.matmul(b[DH * q:DH * (q + 1), P * k:SEQ], V[:, k, DH * h:DH * (h + 1)],
                                             PROB[:, q, SEQ * k:SEQ * (k + 1) - P * k],
                                             start=(k == 0), stop=(k == 1))
                    done(last, f"o{s - 2}")
                if s == PAIRS + 1:
                    released(pe, "ct1")
                    released(pe, "u1")
                    s5_in(0)
                projected(BESIDE_ATTENTION[s])

            def branch(i):
                columns(f"a{i}", ("attn", 0), WT, (2 * i, 2 * i + 1), OT, WT)

            for blk in range(WT):
                if blk < WT - 1:
                    s5_in(blk + 1)
                projected(f"g{4 + blk}")
                if blk == WT - 1:
                    released(pe, "o3")
                    arrive(("attn", 0))
                    for i in range(2):
                        branch(i)
                s5_out(blk)
            for i in range(2, 4):
                branch(i)
            arrive(("glu", 0))
            arrive(("glu", 1))
            for i in range(DT):
                b = take(f"glu{i}")
                for h in range(2):
                    m = i + DT * h
                    for k in range(WT):
                        if i == 0 and h == 0:
                            pe.wait_ge(S["gelu_set"], k + 1)
                        last = pe.matmul(b[:, SEQ * h:SEQ * (h + 1)], weight(("glu", k // 2), 2)[:, k % 2, P * m:P * (m + 1)],
                                         GY[:, k, :], start=(k == 0), stop=(k == WT - 1))
                done(last, f"glu{i}")
            def output(i):
                t, c = divmod(i, 2)
                b = take(f"out{i}")
                arrive(("out", c))
                for k in range(DT):
                    if i == 0:
                        pe.wait_ge(S["mixed_set"], k + 1)
                    last = pe.matmul(b[:, :], GATE[:, k, t * P:(t + 1) * P], weight(("out", c), DT)[:, k, :],
                                     start=(k == 0), stop=(k == DT - 1))
                done(last, f"out{i}")

            def transposed(t):
                for half in range(2):
                    job = f"xt{2 * t + half}"
                    b = take(job)
                    pe.wait_ge(S["x2_normal"], t + 1)
                    for k in range(4):
                        last = pe.transpose(b[:, P * k:P * (k + 1)], XN[:, t, P * (4 * half + k):P * (4 * half + k + 1)], I)
                    done(last, job)

            def embeddings(i):
                c, t = divmod(i, 2)
                b = take(f"pp{i}")
                for k in range(PLE // P):
                    last = pe.matmul(b[:, :], PT_IN[:, k, P * t:P * (t + 1)], WPP[:, k, 512 * c:512 * (c + 1)],
                                     start=(k == 0), stop=(k == PLE // P - 1))
                done(last, f"pp{i}")

            output(0)
            output(1)
            output(2)
            transposed(0)
            b = take("pt")
            pe.wait_ge(S["ple_in"], 32)
            for k in range(PLE // P):
                for t in range(TB):
                    last = pe.transpose(b[:, SEQ * k + P * t:SEQ * k + P * (t + 1)], PIN[:, t, P * k:P * (k + 1)], I)
            done(last, "pt")
            output(3)
            released(pe, "pt")
            b_lg = take("lg")
            pe.wait_ge(S["router_in"], 32)

            def logits(t):
                o = b_lg[:, E * t:E * (t + 1)]
                pe.matmul(o, ONES[0:1, :], BROUT[0:1, :], start=True, stop=False)
                for k in range(DT):
                    if k % 4 == 0:
                        released(pe, f"xt{2 * t + k // 4}")
                    last = pe.matmul(o, H2T[:, k, t * P:(t + 1) * P], WR[:, k, :], start=False, stop=(k == DT - 1))
                return last

            logits(0)
            released(pe, "pt")
            embeddings(0)
            transposed(1)
            embeddings(1)
            done(logits(1), "lg")
            embeddings(2)
            b = take("rk")
            pe.wait_ge(S["chosen_set"], 1)
            pe.matmul(b[:, 0:E], TRI, CHOSEN[:, 0, :], start=True, stop=True)
            pe.matmul(b[:, E:2 * E], ONES, CHOSEN[:, 0, :], start=True, stop=False)
            pe.matmul(b[:, E:2 * E], TRI, CHOSEN[:, 1, :], start=False, stop=True)
            for t in range(TB):
                last = pe.matmul(b[0:1, 2 * E:3 * E], ONES[:, 0:1], CHOSEN[:, t, :], start=(t == 0), stop=(t == 1))
            done(last, "rk")

            def gather(m, n):
                pe.wait_ge(m["sel_set"], n + 1)
                for d in range(DT):
                    for i in range(3 * TB):
                        part, t = divmod(i, TB)
                        last = pe.matmul(bank[GX][:, CAP * d:CAP * (d + 1)], XB[:, part, t, P * d:P * (d + 1)], SELB[:, t, :],
                                         start=(i == 0), stop=(i == 3 * TB - 1))
                last.then_inc(m["gx_full"], 1)

            def chunk(c):
                return place(EXP_PLACE[c]).rearrange("p (a n) -> p a n", a=2 if c < 4 else 4)

            def up_bias(m, n):
                pe.wait_ge(m["pick_set"], n + 1)
                for w in range(2):
                    for h in range(2):
                        rows = slice(E * (2 * w + h), E * (2 * w + h + 1))
                        pe.matmul(bank[UG + w][HALF * h:HALF * (h + 1), :], PICK[rows, :], BUP[rows, :], start=True, stop=False)

            def up(m, n, wait_chunk, leave_chunk, first=None, beside=None):
                pe.wait_ge(m["xs_set"], n + 1)
                for c in range(4):
                    piece = chunk(c)
                    if c == 0 and first is not None:
                        piece = first.rearrange("p (a n) -> p a n", a=2)
                        pe.wait_ge(S["extra_in"], 16)
                    else:
                        wait_chunk(c)
                    for k in (2 * c, 2 * c + 1):
                        for w in range(2):
                            for h in range(2):
                                last = pe.matmul(bank[UG + w][HALF * h:HALF * (h + 1), :], XS[:, k, :],
                                                 piece[:, k % 2, 512 * (2 * w + h):512 * (2 * w + h + 1)],
                                                 start=False, stop=(k == DT - 1))
                            if k == DT - 1:
                                last.then_inc(m[("up_g", "up_u")[w]], 1)
                    if c or first is None:
                        leave_chunk(last, c)
                    if c == 0 and beside is not None:
                        beside()

            def down(m, n, wait_chunk, leave_chunk, bias_of_next=True):
                pe.wait_ge(m["act_set"], n + 1)
                for j in range(4):
                    last = pe.transpose(bank[ATB][:, P * j:P * (j + 1)], ACTS[:, 1, P * j:P * (j + 1)], I)
                last.then_inc(m["at_full"], 1)
                pe.wait_ge(m["wsel_set"], n + 1)
                for t in range(TB):
                    last = pe.transpose(bank[WTB][:, P * t:P * (t + 1)], WSEL[:, t, :], I)
                last.then_inc(m["wt_full"], 1)
                pe.wait_ge(m["at_set"], n + 1)
                for h in range(2):
                    wait_chunk(4 + h)
                    for j in range(4):
                        for c in range(2):
                            last = pe.matmul(bank[YB][HALF * c:HALF * (c + 1), :], ACTT[:, j, HALF * h:HALF * (h + 1)],
                                             chunk(4 + h)[:, j, 512 * c:512 * (c + 1)],
                                             start=(h == 0 and j == 0), stop=(h == 1 and j == 3))
                    if h == 1:
                        last.then_inc(m["y_full"], 1)
                    leave_chunk(last, 4 + h)
                if bias_of_next:
                    up_bias(m, n + 1)
                pe.wait_ge(m["wt_set"], n + 1)
                pe.wait_ge(m["y_set"], n + 1)
                for q in range(4):
                    t, c = divmod(q, 2)
                    rows = slice(HALF * c, HALF * (c + 1))
                    pe.matmul(bank[SCATTER[q]][:, :], WSELT[rows, t, :], Y[rows, :], start=True,
                              stop=True).then_inc(m["sc_full"], 1)

            def main_wait(n):
                def wait(c):
                    less = 0 if c or isinstance(n, int) and n == 0 else 1
                    pe.wait_ge(arrived[EXP_PLACE[c]], n * 16 + 16 * (EXP_USES[c] + 1 - less))
                return wait

            def main_leave(last, c):
                if c in READ:
                    last.then_inc(READ[c], 1)

            def vacant(*banks):
                for i in banks:
                    pe.wait_ge(free[i], sum(1 for at, _ in BANKS.values() if at == i))

            pe.wait_ge(S["up_bias_in"], 16 * 4)
            vacant(UG, UU)
            up_bias(M, 0)
            vacant(GX)
            pe.wait_ge(S["cast_set"], 6)
            gather(M, 0)
            up(M, 0, main_wait(0), main_leave, beside=lambda: embeddings(3))
            pe.wait_ge(S["gates_ready"], 1)
            vacant(ATB)
            for t in range(TB):
                last = pe.transpose(bank[ATB][:, P * t:P * (t + 1)], GATES4[:, t, :], I)
            last.then_inc(S["gt_full"], 1)
            pe.wait_ge(S["gt_set"], 1)
            vacant(YB, *SCATTER)
            pe.wait_ge(S["down_bias_in"], 16 * 4)
            for i in range(4):
                t, c = divmod(i, 2)
                rows = slice(E * i, E * (i + 1))
                pe.matmul(bank[SCATTER[i]][:, :], GT[rows, t, :], BDOWN[rows, :],
                          start=True, stop=True).then_inc(S["bd_full"], 1)
            gather(M, 1)
            pe.wait_ge(S["bd_add"], 2)
            down(M, 0, main_wait(0), main_leave)
            up(M, 1, main_wait(1), main_leave, EXTRA)
            gather(M, 2)
            down(M, 1, main_wait(1), main_leave)
            with pe.Fori(2, E - 1) as e:
                up(M, e, main_wait(e), main_leave)
                gather(M, e + 1)
                down(M, e, main_wait(e), main_leave)
            up(M, E - 1, main_wait(E - 1), main_leave)
            gather(M, E)
            down(M, E - 1, main_wait(E - 1), main_leave, bias_of_next=False)
            pe.wait_ge(S["flag_set"], 1)
            crowd = pe.value_load(flag[0:1, 0:1], min_val=0, max_val=SEQ)
            with pe.If(crowd > CAP):
                with pe.Fori(0, E) as e:
                    with pe.Fori(0, PASSES) as j:
                        n = E + e * PASSES + j
                        gather(M, n + 1)
                        up_bias(M, n + 1)
                        up(M, n + 1, main_wait(n), main_leave)
                        down(M, n, main_wait(n), main_leave, bias_of_next=False)
                pe.wait_ge(S["over_done"], 1)
            for t in range(TB):
                pe.wait_ge(S["x3_set"], t + 1)
                for half in range(2):
                    for k in range(4):
                        last = pe.transpose(bank[XT3B[2 * t + half]][:, P * k:P * (k + 1)],
                                            X2[:, t, P * (4 * half + k):P * (4 * half + k + 1)], I)
                    last.then_inc(S["xt3_full"], 1)
            pe.wait_ge(S["gate_in"], 16)
            for t, cols, at in PARTS:
                for k in range(DT):
                    if cols.start == 0 and k in (0, DT // 2):
                        pe.wait_ge(S["xt3_set"], 2 * t + 1 + k // (DT // 2))
                    last = pe.matmul(bank[at][:, 0:cols.stop - cols.start], XT3[:, k, P * t:P * (t + 1)], WPG[:, k, cols],
                                     start=(k == 0), stop=(k == DT - 1))
                last.then_inc(S["pg_full"], 1)


_INS = ["x", "p", "g_mix", "w_in", "g_q", "g_k", "w_attn_branch", "a_re", "a_im", "log_dt", "b_re", "b_im", "c_re", "c_im",
        "d_skip", "w_glu", "b_glu", "w_out", "g_ffn", "w_router", "b_router", "w_up", "b_up", "w_down", "b_down",
        "g_ple_gate", "w_ple_gate", "w_ple_proj", "g_ple_post"]
_OUTS = [((1, 256, 1024), "float32")]


def kernel(**inputs):
    import numpy as _np
    import concourse.bacc as _bacc
    from concourse import mybir as _mybir
    from concourse.bass_utils import run_bass_kernel_spmd as _run

    nc = _bacc.Bacc("TRN2", target_bir_lowering=False, num_devices=1)
    arrays, args = {}, []
    for name in _INS:
        a = _np.ascontiguousarray(inputs[name])
        arrays[f"in_{name}_dram"] = a
        args.append(nc.dram_tensor(f"in_{name}_dram", a.shape, _mybir.dt.from_np(a.dtype), kind="ExternalInput").ap())
    for i, (shape, dtype) in enumerate(_OUTS):
        dt = _mybir.dt.from_np(_np.dtype(dtype))
        args.append(nc.dram_tensor(f"out_{i}_dram", shape, dt, kind="ExternalOutput").ap())
    hybrid_layer(nc, *args)
    r = _run(nc, [arrays], core_ids=[0])
    got = tuple(r.results[0][f"out_{i}_dram"] for i in range(len(_OUTS)))
    return got[0]
```
